# Optimizing a Trainium2 kernel written in Bass

```python
import math
import jax, jax.numpy as jnp
from jax import lax
import numpy as np

D_MODEL = 2048
BATCH = 1
SEQ = 256
DEPTH = 1
DEC_BATCH = 8
DEC_SEQ = 8
PAST_LEN = 2048
PAGE_SIZE = 128

N_HEADS = 16
HEAD_DIM = 64
N_KV = 4
GROUP = N_HEADS // N_KV
CMP_LEN = 32
CMP_STRIDE = 16
SEL_BLOCK = 64
SEL_TOP = 16
WINDOW = 512
Q_CHUNK = 64
WIN_QBLK = 128
SSM_WIDTH = D_MODEL // 2
SSM_GROUP = 16
SSM_NGROUPS = SSM_WIDTH // SSM_GROUP
SSM_STATE = 64
D_FF = ((-(-8 * D_MODEL // 3)) + 255) // 256 * 256

Q_COLS = N_HEADS * HEAD_DIM
KV_COLS = N_KV * HEAD_DIM
IN_COLS = Q_COLS + 6 * KV_COLS + 3 * N_HEADS + SSM_WIDTH + 2 * D_MODEL
EPS = 1e-6
NEG = -1e30
FORCE_SCORE = 1e4

kernel_name = 'nsa_s5_gated_hybrid_step'

def _rmsnorm(x, g):
    xf = x.astype(jnp.float32)
    y = xf * lax.rsqrt(jnp.mean(xf * xf, axis=-1, keepdims=True) + EPS)
    return (y * g.astype(jnp.float32)).astype(x.dtype)

def _alibi_slopes():
    return jnp.exp2(-8.0 * jnp.arange(1, N_HEADS + 1, dtype=jnp.float32) / N_HEADS).reshape(N_KV, GROUP)

def _in_proj(x, g_mix, w_in):
    B, T = x.shape[:2]
    z = _rmsnorm(x, g_mix) @ w_in
    cuts = np.cumsum([Q_COLS, 6 * KV_COLS, 3 * N_HEADS, SSM_WIDTH]).tolist()
    q, kv, gt, u, mg = jnp.split(z, cuts, axis=-1)
    return (q.reshape(B, T, N_HEADS, HEAD_DIM),
            kv.reshape(B, T, 6, N_KV, HEAD_DIM),
            jax.nn.sigmoid(gt.reshape(B, T, 3, N_HEADS)),
            u,
            mg.reshape(B, T, 2, D_MODEL))

def _compress(x, pe, pool, phi):
    B, Tp = x.shape[:2]
    r = CMP_LEN // CMP_STRIDE
    nsub = Tp // CMP_STRIDE
    nc = nsub - r + 1
    sub = x.reshape(B, nsub, CMP_STRIDE, N_KV, HEAD_DIM)
    parts = jnp.einsum('bnsgd,ms->bmngd', sub, pool.reshape(r, CMP_STRIDE))
    pooled = parts[:, 0, :nc]
    for m in range(1, r):
        pooled = pooled + parts[:, m, m:m + nc]
    pooled = pooled + jnp.einsum('l,ld->d', pool, pe)
    return jax.nn.gelu(pooled) @ phi

def _cmp_sel_attend(q, q_pos, kv4, pe, pool, phi, slopes):
    B, Tq = q.shape[:2]
    Tk = kv4.shape[1]
    Tp = -(-Tk // SEL_BLOCK) * SEL_BLOCK
    kv4 = jnp.pad(kv4, ((0, 0), (0, Tp - Tk), (0, 0), (0, 0), (0, 0)))
    k_cmp = _compress(kv4[:, :, 0], pe[0], pool[0], phi[0])
    v_cmp = _compress(kv4[:, :, 1], pe[1], pool[1], phi[1])
    nc = k_cmp.shape[1]
    cmp_end = jnp.arange(nc, dtype=jnp.int32) * CMP_STRIDE + (CMP_LEN - 1)
    ns = Tp // SEL_BLOCK
    sel_start = jnp.arange(ns, dtype=jnp.int32) * SEL_BLOCK
    overlap = ((cmp_end[:, None] - (CMP_LEN - 1) < sel_start[None, :] + SEL_BLOCK)
               & (cmp_end[:, None] >= sel_start[None, :])).astype(jnp.float32)
    k_blk = kv4[:, :, 2].reshape(B, ns, SEL_BLOCK, N_KV, HEAD_DIM).transpose(0, 3, 1, 2, 4)
    v_blk = kv4[:, :, 3].reshape(B, ns, SEL_BLOCK, N_KV, HEAD_DIM).transpose(0, 3, 1, 2, 4)
    n_top = min(SEL_TOP, ns)
    scale = HEAD_DIM ** -0.5
    bi = jnp.arange(B)[:, None, None, None]
    gi = jnp.arange(N_KV)[None, :, None, None]
    blk_ids = jnp.arange(ns, dtype=jnp.int32)
    qc_len = math.gcd(Tq, Q_CHUNK)
    nch = Tq // qc_len

    def chunk(args):
        qc, pc = args
        qg = qc.reshape(B, qc_len, N_KV, GROUP, HEAD_DIM)
        s = jnp.einsum('bqgnd,bcgd->bgnqc', qg, k_cmp, preferred_element_type=jnp.float32) * scale
        dist = (pc[:, None] - cmp_end[None, :]).astype(jnp.float32)
        valid = cmp_end[None, :] <= pc[:, None]
        s = s - slopes[:, :, None, None] * dist
        p = jax.nn.softmax(jnp.where(valid, s, NEG), axis=-1) * valid
        o_c = jnp.einsum('bgnqc,bcgd->bqgnd', p.astype(v_cmp.dtype), v_cmp)
        imp = jnp.einsum('bgnqc,cs->bgqs', p, overlap)
        cur = pc // SEL_BLOCK
        forced = (blk_ids[None, :] == 0) | (blk_ids[None, :] == cur[:, None]) | (blk_ids[None, :] == cur[:, None] - 1)
        imp = jnp.where(forced, FORCE_SCORE, imp)
        imp = jnp.where(blk_ids[None, :] <= cur[:, None], imp, -1.0)
        _, idx = lax.top_k(imp, n_top)
        kg = k_blk[bi, gi, idx]
        vg = v_blk[bi, gi, idx]
        kpos = idx[..., None] * SEL_BLOCK + jnp.arange(SEL_BLOCK, dtype=jnp.int32)
        dsel = pc[None, None, :, None, None] - kpos
        s2 = jnp.einsum('bqgnd,bgqksd->bgnqks', qg, kg, preferred_element_type=jnp.float32) * scale
        s2 = s2 - slopes[None, :, :, None, None, None] * dsel[:, :, None].astype(jnp.float32)
        s2 = jnp.where(dsel[:, :, None] >= 0, s2, NEG)
        sh = s2.shape
        p2 = jax.nn.softmax(s2.reshape(*sh[:-2], -1), axis=-1).reshape(sh)
        o_s = jnp.einsum('bgnqks,bgqksd->bqgnd', p2.astype(vg.dtype), vg)
        return (o_c.reshape(B, qc_len, N_HEADS, HEAD_DIM), o_s.reshape(B, qc_len, N_HEADS, HEAD_DIM))

    qs = q.reshape(B, nch, qc_len, N_HEADS, HEAD_DIM).transpose(1, 0, 2, 3, 4)
    ps = q_pos.reshape(nch, qc_len)
    o_c, o_s = lax.map(chunk, (qs, ps))
    o_c = o_c.transpose(1, 0, 2, 3, 4).reshape(B, Tq, N_HEADS, HEAD_DIM)
    o_s = o_s.transpose(1, 0, 2, 3, 4).reshape(B, Tq, N_HEADS, HEAD_DIM)
    return o_c, o_s

def _window_attend(q, q_pos, kw, vw, k_pos, slopes):
    B, Tq = q.shape[:2]
    qg = q.reshape(B, Tq, N_KV, GROUP, HEAD_DIM)
    s = jnp.einsum('bqgnd,bkgd->bgnqk', qg, kw, preferred_element_type=jnp.float32) * (HEAD_DIM ** -0.5)
    dist = q_pos[:, None] - k_pos[None, :]
    valid = (dist >= 0) & (dist < WINDOW) & (k_pos[None, :] >= 0)
    s = s - slopes[:, :, None, None] * dist.astype(jnp.float32)
    p = jax.nn.softmax(jnp.where(valid, s, NEG), axis=-1)
    o = jnp.einsum('bgnqk,bkgd->bqgnd', p.astype(vw.dtype), vw)
    return o.reshape(B, Tq, N_HEADS, HEAD_DIM)

def _window_prompt(q, kvw, slopes):
    B, T = q.shape[:2]
    kpad = jnp.pad(kvw, ((0, 0), (WINDOW, 0), (0, 0), (0, 0), (0, 0)))
    span = WINDOW + WIN_QBLK

    def blk(i):
        q0 = i * WIN_QBLK
        qb = lax.dynamic_slice_in_dim(q, q0, WIN_QBLK, axis=1)
        kb = lax.dynamic_slice_in_dim(kpad, q0, span, axis=1)
        qpos = q0 + jnp.arange(WIN_QBLK, dtype=jnp.int32)
        kpos = q0 - WINDOW + jnp.arange(span, dtype=jnp.int32)
        return _window_attend(qb, qpos, kb[:, :, 0], kb[:, :, 1], kpos, slopes)

    o = lax.map(blk, jnp.arange(T // WIN_QBLK, dtype=jnp.int32))
    return o.transpose(1, 0, 2, 3, 4).reshape(B, T, N_HEADS, HEAD_DIM)

def _cplx_affine_combine(e1, e2):
    a1r, a1i, b1r, b1i = e1
    a2r, a2i, b2r, b2i = e2
    return (a2r * a1r - a2i * a1i, a2r * a1i + a2i * a1r,
            a2r * b1r - a2i * b1i + b2r, a2r * b1i + a2i * b1r + b2i)

def _ssm_scan(u, h0_re, h0_im, lam_re, lam_im, log_dt, b_re, b_im, c_re, c_im, d_skip):
    f32 = jnp.float32
    B, T = u.shape[:2]
    uf = u.astype(f32).reshape(B, T, SSM_NGROUPS, SSM_GROUP)
    dt = jnp.exp(log_dt.astype(f32))[:, None]
    lr = lam_re.astype(f32)
    li = lam_im.astype(f32)
    mag = jnp.exp(lr * dt)
    ar = mag * jnp.cos(li * dt)
    ai = mag * jnp.sin(li * dt)
    den = lr * lr + li * li
    fr = ((ar - 1.0) * lr + ai * li) / den
    fi = (ai * lr - (ar - 1.0) * li) / den
    br = b_re.astype(f32)
    bim = b_im.astype(f32)
    bbr = fr[..., None] * br - fi[..., None] * bim
    bbi = fr[..., None] * bim + fi[..., None] * br
    xr = jnp.einsum('btgc,gpc->btgp', uf, bbr)
    xi = jnp.einsum('btgc,gpc->btgp', uf, bbi)
    xr = jnp.concatenate([h0_re.astype(f32)[:, None], xr], axis=1)
    xi = jnp.concatenate([h0_im.astype(f32)[:, None], xi], axis=1)
    a_r = jnp.broadcast_to(ar, xr.shape)
    a_i = jnp.broadcast_to(ai, xr.shape)
    _, _, hr, hi = lax.associative_scan(_cplx_affine_combine, (a_r, a_i, xr, xi), axis=1)
    hr = hr[:, 1:]
    hi = hi[:, 1:]
    y = (jnp.einsum('btgp,gcp->btgc', hr, c_re.astype(f32))
         - jnp.einsum('btgp,gcp->btgc', hi, c_im.astype(f32))
         + d_skip.astype(f32).reshape(SSM_NGROUPS, SSM_GROUP) * uf)
    return y.reshape(B, T, SSM_WIDTH).astype(u.dtype), hr[:, -1], hi[:, -1]

def _merge_ffn(x, o_heads, y_ssm, mg, w_attn_out, w_glu, w_out, g_ffn, w_gate, w_up, w_down):
    B, T = x.shape[:2]
    ya = o_heads.reshape(B, T, Q_COLS) @ w_attn_out
    yg = jax.nn.gelu(y_ssm) @ w_glu
    yb = yg[..., :D_MODEL] * jax.nn.sigmoid(yg[..., D_MODEL:])
    m = jax.nn.sigmoid(mg[:, :, 0]) * ya + jax.nn.sigmoid(mg[:, :, 1]) * yb
    x = x + m @ w_out
    h = _rmsnorm(x, g_ffn)
    return x + (jax.nn.silu(h @ w_gate) * (h @ w_up)) @ w_down

def _layer_prompt(x, lw, slopes):
    (g_mix, w_in, pe, pool, phi, w_attn_out, lam_re, lam_im, log_dt, b_re, b_im, c_re, c_im,
     d_skip, w_glu, w_out, g_ffn, w_gate, w_up, w_down) = lw
    B, T = x.shape[:2]
    q, kv, gates, u, mg = _in_proj(x, g_mix, w_in)
    pos = jnp.arange(T, dtype=jnp.int32)
    o_c, o_s = _cmp_sel_attend(q, pos, kv[:, :, :4], pe, pool, phi, slopes)
    o_w = _window_prompt(q, kv[:, :, 4:], slopes)
    o = gates[:, :, 0, :, None] * o_c + gates[:, :, 1, :, None] * o_s + gates[:, :, 2, :, None] * o_w
    h0 = jnp.zeros((B, SSM_NGROUPS, SSM_STATE), jnp.float32)
    y_ssm, h_re, h_im = _ssm_scan(u, h0, h0, lam_re, lam_im, log_dt, b_re, b_im, c_re, c_im, d_skip)
    y = _merge_ffn(x, o, y_ssm, mg, w_attn_out, w_glu, w_out, g_ffn, w_gate, w_up, w_down)
    n_win = min(WINDOW, T)
    return y, kv[:, :, :4], kv[:, T - n_win:, 4:], h_re, h_im

def _layer_sample(x, kv_past, win_buf, h_re, h_im, lw, slopes):
    (g_mix, w_in, pe, pool, phi, w_attn_out, lam_re, lam_im, log_dt, b_re, b_im, c_re, c_im,
     d_skip, w_glu, w_out, g_ffn, w_gate, w_up, w_down) = lw
    B, T = x.shape[:2]
    past_len = kv_past.shape[1]
    q, kv, gates, u, mg = _in_proj(x, g_mix, w_in)
    pos = past_len + jnp.arange(T, dtype=jnp.int32)
    kv4 = jnp.concatenate([kv_past, kv[:, :, :4].astype(kv_past.dtype)], axis=1)
    o_c, o_s = _cmp_sel_attend(q, pos, kv4, pe, pool, phi, slopes)
    n_buf = win_buf.shape[1]
    kvw = jnp.concatenate([win_buf, kv[:, :, 4:].astype(win_buf.dtype)], axis=1)
    kpos = past_len - n_buf + jnp.arange(n_buf + T, dtype=jnp.int32)
    o_w = _window_attend(q, pos, kvw[:, :, 0], kvw[:, :, 1], kpos, slopes)
    o = gates[:, :, 0, :, None] * o_c + gates[:, :, 1, :, None] * o_s + gates[:, :, 2, :, None] * o_w
    y_ssm, hr, hi = _ssm_scan(u, h_re, h_im, lam_re, lam_im, log_dt, b_re, b_im, c_re, c_im, d_skip)
    y = _merge_ffn(x, o, y_ssm, mg, w_attn_out, w_glu, w_out, g_ffn, w_gate, w_up, w_down)
    n_keep = min(WINDOW, n_buf + T)
    return y, kv[:, :, :4], kvw[:, n_buf + T - n_keep:], hr, hi

def setup_inputs(seed: int = 0) -> dict:
    key = jax.random.key(seed)
    ks = iter(jax.random.split(key, 32))
    f32 = jnp.float32

    def nrm(shape, s=1.0):
        return jax.random.normal(next(ks), shape, f32) * s

    L = DEPTH
    n_pages = PAST_LEN // PAGE_SIZE
    n_pool = (DEC_BATCH * n_pages * 5) // 4
    n_win = min(WINDOW, PAST_LEN)
    x_prompt = nrm((BATCH, SEQ, D_MODEL))
    x_sample = nrm((DEC_BATCH, DEC_SEQ, D_MODEL))
    cache_kv = nrm((L, n_pool, PAGE_SIZE, 4, N_KV, HEAD_DIM))
    state_win = nrm((L, DEC_BATCH, n_win, 2, N_KV, HEAD_DIM))
    state_ssm_re = nrm((L, DEC_BATCH, SSM_NGROUPS, SSM_STATE), 0.1)
    state_ssm_im = nrm((L, DEC_BATCH, SSM_NGROUPS, SSM_STATE), 0.1)
    perm = jax.random.permutation(next(ks), n_pool)
    page_table = perm[:DEC_BATCH * n_pages].reshape(DEC_BATCH, n_pages).astype(jnp.int32)
    g_mix = 1.0 + nrm((L, D_MODEL), 0.01)
    w_in = nrm((L, D_MODEL, IN_COLS), D_MODEL ** -0.5)
    w_cmp_pe = nrm((L, 2, CMP_LEN, HEAD_DIM), 0.1)
    w_cmp_pool = (1.0 + nrm((L, 2, CMP_LEN), 0.1)) * CMP_LEN ** -0.5
    w_cmp_phi = nrm((L, 2, HEAD_DIM, HEAD_DIM), HEAD_DIM ** -0.5)
    w_attn_out = nrm((L, Q_COLS, D_MODEL), Q_COLS ** -0.5)
    ssm_lam_re = -0.5 + nrm((L, SSM_NGROUPS, SSM_STATE), 0.01)
    ssm_lam_im = jnp.pi * jnp.arange(SSM_STATE, dtype=f32) + nrm((L, SSM_NGROUPS, SSM_STATE), 0.01)
    ssm_log_dt = jax.random.uniform(next(ks), (L, SSM_NGROUPS), f32, math.log(1e-3), math.log(1e-1))
    ssm_b_re = nrm((L, SSM_NGROUPS, SSM_STATE, SSM_GROUP), (2.0 * SSM_GROUP) ** -0.5)
    ssm_b_im = nrm((L, SSM_NGROUPS, SSM_STATE, SSM_GROUP), (2.0 * SSM_GROUP) ** -0.5)
    ssm_c_re = nrm((L, SSM_NGROUPS, SSM_GROUP, SSM_STATE), (2.0 * SSM_STATE) ** -0.5)
    ssm_c_im = nrm((L, SSM_NGROUPS, SSM_GROUP, SSM_STATE), (2.0 * SSM_STATE) ** -0.5)
    ssm_d = nrm((L, SSM_WIDTH))
    w_glu = nrm((L, SSM_WIDTH, 2 * D_MODEL), SSM_WIDTH ** -0.5)
    w_out = nrm((L, D_MODEL, D_MODEL), D_MODEL ** -0.5)
    g_ffn = 1.0 + nrm((L, D_MODEL), 0.01)
    w_gate = nrm((L, D_MODEL, D_FF), D_MODEL ** -0.5)
    w_up = nrm((L, D_MODEL, D_FF), D_MODEL ** -0.5)
    w_down = nrm((L, D_FF, D_MODEL), D_FF ** -0.5)
    g_final = 1.0 + nrm((D_MODEL,), 0.01)
    return {'x_prompt': x_prompt, 'x_sample': x_sample, 'cache_kv': cache_kv, 'state_win': state_win,
            'state_ssm_re': state_ssm_re, 'state_ssm_im': state_ssm_im, 'page_table': page_table,
            'g_mix': g_mix, 'w_in': w_in, 'w_cmp_pe': w_cmp_pe, 'w_cmp_pool': w_cmp_pool, 'w_cmp_phi': w_cmp_phi,
            'w_attn_out': w_attn_out, 'ssm_lam_re': ssm_lam_re, 'ssm_lam_im': ssm_lam_im, 'ssm_log_dt': ssm_log_dt,
            'ssm_b_re': ssm_b_re, 'ssm_b_im': ssm_b_im, 'ssm_c_re': ssm_c_re, 'ssm_c_im': ssm_c_im, 'ssm_d': ssm_d,
            'w_glu': w_glu, 'w_out': w_out, 'g_ffn': g_ffn, 'w_gate': w_gate, 'w_up': w_up, 'w_down': w_down,
            'g_final': g_final}

def reference(x_prompt, x_sample, cache_kv, state_win, state_ssm_re, state_ssm_im, page_table,
              g_mix, w_in, w_cmp_pe, w_cmp_pool, w_cmp_phi, w_attn_out, ssm_lam_re, ssm_lam_im, ssm_log_dt,
              ssm_b_re, ssm_b_im, ssm_c_re, ssm_c_im, ssm_d, w_glu, w_out, g_ffn, w_gate, w_up, w_down, g_final):
    slopes = _alibi_slopes()
    n_seq, n_pages = page_table.shape
    page = cache_kv.shape[2]
    xp, xs = x_prompt, x_sample
    kvp_l, winp_l, hrp_l, hip_l = [], [], [], []
    kvs_l, wins_l, hrs_l, his_l = [], [], [], []
    for l in range(DEPTH):
        lw = (g_mix[l], w_in[l], w_cmp_pe[l], w_cmp_pool[l], w_cmp_phi[l], w_attn_out[l],
              ssm_lam_re[l], ssm_lam_im[l], ssm_log_dt[l], ssm_b_re[l], ssm_b_im[l], ssm_c_re[l], ssm_c_im[l],
              ssm_d[l], w_glu[l], w_out[l], g_ffn[l], w_gate[l], w_up[l], w_down[l])
        xp, kvp, winp, hrp, hip = _layer_prompt(xp, lw, slopes)
        kv_past = cache_kv[l][page_table].reshape(n_seq, n_pages * page, 4, N_KV, HEAD_DIM)
        xs, kvs, wins, hrs, his = _layer_sample(xs, kv_past, state_win[l], state_ssm_re[l], state_ssm_im[l], lw, slopes)
        kvp_l.append(kvp); winp_l.append(winp); hrp_l.append(hrp); hip_l.append(hip)
        kvs_l.append(kvs); wins_l.append(wins); hrs_l.append(hrs); his_l.append(his)
    y_prompt = _rmsnorm(xp, g_final)
    y_sample = _rmsnorm(xs, g_final)
    kv_rows_prompt = jnp.stack(kvp_l)
    win_prompt = jnp.stack(winp_l)
    ssm_re_prompt = jnp.stack(hrp_l)
    ssm_im_prompt = jnp.stack(hip_l)
    kv_rows_sample = jnp.stack(kvs_l)
    win_sample = jnp.stack(wins_l)
    ssm_re_sample = jnp.stack(hrs_l)
    ssm_im_sample = jnp.stack(his_l)
    return (y_prompt, y_sample, kv_rows_prompt, win_prompt, ssm_re_prompt, ssm_im_prompt,
            kv_rows_sample, win_sample, ssm_re_sample, ssm_im_sample)


_drawn_inputs = setup_inputs


def setup_inputs(seed=0):
    import zlib

    import numpy as np

    out = dict(_drawn_inputs(seed))
    spreads = {}
    factors = {'g_mix': 5.603,
     'w_cmp_pe': 2.995,
     'w_cmp_pool': 3.126,
     'ssm_lam_re': 4.542,
     'ssm_c_re': 4.106,
     'ssm_c_im': 4.162,
     'g_ffn': 8.0,
     'g_final': 5.656}
    for name, (base, spread) in spreads.items():
        noise = np.random.default_rng([zlib.crc32(name.encode()), seed]).standard_normal(out[name].shape)
        drawn = base * np.exp(spread * noise) if base else spread * noise
        out[name] = __import__('jax').numpy.asarray(drawn.astype(out[name].dtype))
    for name, factor in factors.items():
        out[name] = (out[name] * factor).astype(out[name].dtype)
    return out
```

```python
from contextlib import ExitStack, contextmanager

import numpy as np
import concourse.bass as bass
from concourse import mybir

F32 = mybir.dt.float32
I32 = mybir.dt.int32
ALU = mybir.AluOpType
ACT = mybir.ActivationFunctionType
AX_X = mybir.AxisListType.X

P = 128
DM = 2048
SEQ = 256
NB, NQ = 8, 8
NT = SEQ + NB * NQ
KT = DM // P
NH, HD, NKV, GRP = 16, 64, 4, 4
PAST, PAGE = 2048, 128
NPG = PAST // PAGE
WIN = 512
NG, NS, CH = 64, 64, 16
SSMW = NG * CH
DFF = 5632
FT = DFF // P
L = 8
NCH = NT // L
NPC = SEQ // L
GH = NG // 2
HGH = GH // 2
EPS = 1e-6
BIG = 1e30
FORCED = 1e4
NC_P = 15
NC_S = 127
NBLK = 33
SC = 0.125
C_Q, C_KV, C_GT, C_U, C_MG = 0, 1024, 2560, 2608, 3632
TWO_PI_HI = 6.28125
TWO_PI_LO = float(np.float32(2 * np.pi - 6.28125))
MAGIC = 12582912.0


def slope(h):
    return float(2.0 ** (-8.0 * (h + 1) / NH))


def small_constants():
    r = np.arange(P)
    parts = {}
    parts["ident"] = np.eye(P)
    parts["same"] = ((r[:, None] // 32 == r[None, :] // 32) & (r[:, None] % 8 == r[None, :] % 8))
    k = np.arange(SEQ)
    d = 128 + r[:, None] - k[None, :]
    parts["half"] = r[:, None] // 64 == np.arange(2)[None, :]
    parts["distp"] = np.where(d >= 0, d, BIG)
    end = np.arange(NC_P) * 16 + 31
    bias, valid = [], []
    for qt in range(2):
        q = qt * 128 + r
        dist = q[:, None] - end[None, :]
        ok = dist >= 0
        valid.append(ok)
        for h in range(NH):
            bias.append(np.where(ok, -np.float32(slope(h)) * dist, -BIG))
    parts["biascp"] = np.concatenate(bias, 1)
    parts["validcp"] = np.concatenate(valid, 1)
    c = np.arange(P) * 16
    s = np.arange(NBLK) * 64
    parts["overlap"] = (c[:, None] < s[None, :] + 64) & (c[:, None] + 31 >= s[None, :])
    m = np.zeros((P, 3, P))
    for br in range(3):
        for h in range(NH):
            m[br * NH + h, br, h * 8:h * 8 + 8] = 1
    parts["gatesel"] = m.reshape(P, -1)
    parts["qmask"] = r[:, None] % 8 == np.arange(8)[None, :]
    parts["submask"] = r[:, None] // 16 == np.arange(8)[None, :]
    parts["chandiag"] = r[:, None] % 16 == np.arange(16)[None, :]
    h, q = r // 8, r % 8
    sl = np.array([slope(x) for x in h], np.float32)[:, None]
    parts["biascs"] = -sl * (2048 + q[:, None] - (np.arange(NC_S) * 16 + 31)[None, :]).astype(np.float32)
    at, cols = {}, 0
    for name, a in parts.items():
        at[name] = (cols, cols + a.shape[1])
        cols += a.shape[1]
    return np.concatenate([np.asarray(a, np.float32) for a in parts.values()], 1), at


def key_biases():
    r = np.arange(P)
    q = r % 8
    sl = np.array([slope(x) for x in r // 8], np.float32)[:, None]
    d = 2048 + q[:, None] - np.arange(PAST + NQ)[None, :]
    sel = np.where(d >= 0, -sl * d.astype(np.float32), -BIG)
    d = 512 + q[:, None] - np.arange(WIN + NQ)[None, :]
    win = np.where((d >= 0) & (d < WIN), -sl * d.astype(np.float32), -BIG)
    return np.concatenate([sel, win], 1).astype(np.float32)


_, CAT = small_constants()
CW = max(b for _, b in CAT.values())


def build(nc, ins, outs):
    (x_prompt, x_sample, cache_kv, state_win, h0_re, h0_im, page_table, g_mix, w_in, w_pe, w_pool, w_phi,
     w_ao, lam_re, lam_im, log_dt, b_re, b_im, c_re, c_im, ssm_d, w_glu, w_out, g_ffn, w_gate, w_up,
     w_down, g_final, consts, kbias) = ins
    (y_prompt, y_sample, kvr_prompt, win_prompt, sre_prompt, sim_prompt, kvr_sample, win_sample,
     sre_sample, sim_sample) = outs
    with ExitStack() as ctx:
        def sb(name, shape, dt=F32):
            return ctx.enter_context(nc.sbuf_tensor(name, shape, dt))

        sems = {}

        lasting = ("slot_landed", "step_used", "bank_f", "square_", "mean_ready", "root_ready", "rstd_ready",
                   "stored", "y_stored", "x_spilled")
        def S(name):
            if name not in sems:
                sems[name] = nc.alloc_semaphore(name)
            return sems[name]

        @contextmanager
        def program():
            with nc.Block() as block:
                yield block
            own = [n for n in sems if not n.startswith(lasting)]
            nc.clear_and_free_semaphores([sems.pop(n) for n in own])
            nc.all_engine_barrier()

        PS = [ctx.enter_context(nc.psum_tensor(f"bank{i}", [P, 512], F32)) for i in range(8)]
        ctx.enter_context(nc.allow_non_contiguous_dma(reason="small parameter tables"))

        ring = [sb(f"ring{s}", [P, 4096]) for s in range(2)]
        cst = sb("cst", [P, CW])
        ones = sb("ones", [P, P])
        xT = sb("xT", [P, KT, NT])
        hT = sb("hT", [P, KT, NT])
        oT = sb("oT", [P, 8, NT])
        ysT = sb("ysT", [P, 8, NT])
        gcol = sb("gcol", [P, 48])
        gN = sb("gN", [P, 2, 48])
        gS = sb("gS", [P, 3, NB])
        poolw = sb("poolw", [P, 2, 2, 8])
        pec = sb("pec", [P, 2])
        phi = sb("phi", [P, 2, P])
        qs = sb("qs", [P, 8, NB * NQ])
        ks = sb("ks", [P, 4, NB * NQ])
        rstd = sb("rstd", [P, NT])
        sq = sb("sq", [P, 2, NT])
        ARW = 25600
        arena = sb("arena", [P, ARW])

        def C(name, rows=P):
            a, b = CAT[name]
            return cst[0:rows, a:b]

        def scratch(top=0, region=None, size=ARW):
            region = arena[:, :] if region is None else region
            at = [top]

            def take(width):
                a = at[0]
                at[0] += width
                assert at[0] <= size, at[0]
                return region[:, a:a + width]
            take.at = at
            return take

        ident = C("ident")
        u_dram = nc.dram_tensor("u_scratch", [NT, SSMW], F32).ap()
        x_dram = nc.dram_tensor("x_scratch", [P, KT, NT], F32).ap()
        y_dram = nc.dram_tensor("y_scratch", [NT, SSMW], F32).ap()

        count = {}

        class Job:
            def __init__(self, n, kt, loads, groups):
                self.n, self.kt, self.loads, self.groups = n, kt, loads, groups
                self.base = dict(count)
                self.per = {}
                self.done = {}
                self.landed = []
                self.used = []
                self.emptied = []
                for st, gs in enumerate(groups):
                    s = st % 2
                    self.used.append(self.add(f"step_used{s}"))
                    self.landed.append(self.add(f"slot_landed{s}", 16 * len(loads(0, st))))
                    for g, (bank, _, _, first, last) in enumerate(gs):
                        self.emptied.append(self.add(f"bank_free{bank}") if first else None)
                        if last:
                            end = g == len(gs) - 1
                            name = f"step_used{s}" if end else f"bank_full{bank}"
                            self.done[bank] = (name, self.used[-1] if end else self.add(name))
                for name, k in self.per.items():
                    count[name] = count.get(name, 0) + n * k

            def add(self, name, k=1):
                self.per[name] = self.per.get(name, 0) + k
                return self.per[name]

            def value(self, name, i, k):
                return i * self.per[name] + self.base.get(name, 0) + k

        def stream(sp, job):
            with sp.Fori(0, job.n) as i:
                for st in range(len(job.groups)):
                    name = f"step_used{st % 2}"
                    sp.wait_ge(S(name), job.value(name, i, job.used[st]))
                    for dst, src in job.loads(i, st):
                        sp.dma_start(dst, src).then_inc(S(f"slot_landed{st % 2}"), 16)

        def products(pe, job, rhs):
            with pe.Fori(0, job.n) as i:
                g = 0
                for st, gs in enumerate(job.groups):
                    name = f"slot_landed{st % 2}"
                    pe.wait_ge(S(name), job.value(name, i, job.landed[st]))
                    for at, (bank, lhs, k0, first, last) in enumerate(gs):
                        if first:
                            pe.wait_ge(S(f"bank_free{bank}"), job.value(f"bank_free{bank}", i, job.emptied[g]))
                        g += 1
                        for k in range(job.kt):
                            mm = pe.matmul(PS[bank][:, 0:NT], lhs(ring[st % 2], k), rhs[:, k0 + k, :],
                                           start=bool(first and k == 0), stop=bool(last and k == job.kt - 1))
                        if at == len(gs) - 1:
                            mm.then_inc(S(f"step_used{st % 2}"), 1)
                        elif last:
                            mm.then_inc(S(f"bank_full{bank}"), 1)

        def full(eng, job, bank, i):
            name, k = job.done[bank]
            eng.wait_ge(S(name), job.value(name, i, k) + (1 if name.startswith("step_used") else 0))

        def plain(w, kt, cols, col0=0):
            def loads(i, st):
                return [(ring[st % 2][:, 0:kt * cols].rearrange("p (k c) -> p k c", k=kt),
                         w.rearrange("(k p) c -> p k c", p=P)[:, :, bass.ds(i * (2 * cols) + (st * cols + col0), cols)])]
            return loads

        def lhs_at(cols, j):
            return lambda slot, k: slot[:, k * cols + j * P:k * cols + (j + 1) * P]

        two_steps = [[(2 * st + j, lhs_at(256, j), 0, True, True) for j in range(2)] for st in range(2)]

        def q_loads(i, st):
            view = w_in.rearrange("(k p) c -> p k c", p=P)
            slot = ring[st % 2][:, 0:KT * 256].rearrange("p (k n h c) -> p k n h c", k=KT, n=2, h=2)
            return [(slot[:, :, n, half, :], view[:, :, bass.ds(i * 512 + (half * 256 + st * P + n * HD), HD)])
                    for half in range(2) for n in range(2)]

        def gu_loads(i, st):
            return [
                (ring[st][:, 0:KT * 256].rearrange("p (k c) -> p k c", k=KT),
                 (w_gate, w_up)[st].rearrange("(k p) c -> p k c", p=P)[:, :, bass.ds(i * 256, 256)])]

        def glu_loads(i, st):
            return [(ring[st][:, 0:8 * 256].rearrange("p (k c) -> p k c", k=8),
                     w_glu.rearrange("(k p) c -> p k c", p=P)[:, :, bass.ds(i * 256 + st * DM, 256)])]

        def down_loads(i, st):
            return [(ring[st % 2][:, 0:11 * 256].rearrange("p (k c) -> p k c", k=11),
                     w_down.rearrange("(k p) c -> p k c", p=P)[:, st * 11:st * 11 + 11, bass.ds(i * 256, 256)])]

        job_q = Job(2, KT, q_loads, two_steps)
        job_kv = Job(3, KT, plain(w_in, KT, 256, C_KV), two_steps)
        job_u = Job(2, KT, plain(w_in, KT, 256, C_U), two_steps)
        job_mg = Job(8, KT, plain(w_in, KT, 256, C_MG), two_steps)
        job_ao = Job(4, 8, plain(w_ao, 8, 256), two_steps)
        job_glu = Job(8, 8, glu_loads, two_steps)
        job_out = Job(4, KT, plain(w_out, KT, 256), two_steps)
        job_ffn = Job(FT // 2, KT, gu_loads, two_steps)
        job_down = Job(8, 11, down_loads,
                       [[(j, lhs_at(256, j), st * 11, st == 0, st == 3) for j in range(2)] for st in range(4)])

        norms = [0]

        class Norm:
            def __init__(self):
                self.n = norms[0]
                norms[0] += 1

        def norm_squares(act, nm, src):
            for k in range(KT):
                if nm.n * KT + k >= 2:
                    act.wait_ge(S("square_used"), nm.n * KT + k - 1)
                nc.scalar.activation(sq[:, k % 2, :], src[:, k, :], ACT.Square).then_inc(S("square_ready"), 1)

        def norm_sum(pe, nm):
            if nm.n:
                pe.wait_ge(S("mean_ready"), nm.n)
            for k in range(KT):
                pe.wait_ge(S("square_ready"), nm.n * KT + k + 1)
                mm = pe.matmul(PS[7][:, 0:NT], ones[:, :], sq[:, k % 2, :], start=k == 0, stop=k == KT - 1)
                mm.then_inc(S("square_used"), 1)

        def norm_scale(dve, nm, src, dst, gc, done):
            dve.wait_ge(S("square_used"), (nm.n + 1) * KT)
            nc.vector.tensor_scalar(rstd[:, :], PS[7][:, 0:NT], 1.0 / DM, EPS, ALU.mult, ALU.add).then_inc(S("mean_ready"), 1)
            dve.wait_ge(S("root_ready"), nm.n + 1)
            nc.vector.reciprocal(rstd[:, :], rstd[:, :]).then_inc(S("rstd_ready"), 1)
            dve.wait_ge(S("rstd_ready"), nm.n + 1)
            for k in range(KT):
                nc.vector.scalar_tensor_tensor(out=dst[:, k, :], in0=src[:, k, :], scalar=gcol[:, gc * KT + k:gc * KT + k + 1],
                                               in1=rstd[:, :], op0=ALU.mult, op1=ALU.mult).then_inc(S(done), 1)

        def norm_root(act, nm):
            act.wait_ge(S("mean_ready"), nm.n + 1)
            nc.scalar.activation(rstd[:, :], rstd[:, :], ACT.Sqrt).then_inc(S("root_ready"), 1)

        norm1, norm2, norm3 = Norm(), Norm(), Norm()

        take = scratch()
        kvT = take(12 * NT).rearrange("p (t n) -> p t n", t=12)
        qT = take(8 * NT).rearrange("p (t n) -> p t n", t=8)
        keep = take.at[0]
        uT = take(8 * NT).rearrange("p (t n) -> p t n", t=8)
        xrow = take(3 * DM).rearrange("p (t n) -> p t n", t=3)
        wg48 = take(KT * 48).rearrange("p (k c) -> p k c", k=KT)
        gT = take(NT)
        grow = take(P)
        TOK = [P, P, NT - 2 * P]

        with program() as block:
            @block.sync
            def _(sp):
                sp.dma_start(xrow[:, 0, :], x_prompt[0, 0:P, :]).then_inc(S("x_landed"), 16)
                sp.dma_start(xrow[:, 1, :], x_prompt[0, P:SEQ, :]).then_inc(S("x_landed"), 16)
                sp.dma_start(xrow[0:TOK[2], 2, :], x_sample.rearrange("b t d -> (b t) d")).then_inc(S("x_landed"), 16)
                for job in (job_q, job_kv, job_u):
                    stream(sp, job)

            @block.gpsimd
            def _(pool):
                nc.gpsimd.memset(ones[:, :], 1.0).then_inc(S("ones_ready"), 1)

            @block.tensor
            def _(pe):
                pe.wait_ge(S("consts_landed"), 16)
                pe.wait_ge(S("grow_landed"), 48)
                nc.tensor.transpose(PS[6][:, 0:48], grow[0:48, :], ident[0:48, 0:48]).then_inc(S("gcol_full"), 1)
                pe.wait_ge(S("x_landed"), 48)
                n = 0
                for t in range(3):
                    for c in range(KT // 4):
                        if n >= 2:
                            pe.wait_ge(S("xt_copied"), n - 1)
                        for j in range(4):
                            k = 4 * c + j
                            tr = nc.tensor.transpose(PS[4 + n % 2][:, j * P:j * P + TOK[t]],
                                                     xrow[0:TOK[t], t, k * P:(k + 1) * P], ident[0:TOK[t], 0:TOK[t]])
                        tr.then_inc(S("xt_full"), 1)
                        n += 1
                pe.wait_ge(S("ones_ready"), 1)
                norm_sum(pe, norm1)
                pe.sem_inc(S("step_used0"), 1)
                pe.sem_inc(S("step_used1"), 1)
                pe.wait_ge(S("h_ready"), KT)
                for job in (job_q, job_kv, job_u):
                    products(pe, job, hT)
                pe.wait_ge(S("wg_landed"), 16)
                pe.wait_ge(S("gcol_copied"), 1)
                for k in range(KT):
                    mm = pe.matmul(PS[6][0:48, 0:NT], wg48[:, k, :], hT[:, k, :], start=k == 0, stop=k == KT - 1)
                mm.then_inc(S("gate_full"), 1)
                pe.wait_ge(S("gate_ready"), 1)
                for t in range(2):
                    tr = nc.tensor.transpose(PS[4][:, t * 48:(t + 1) * 48], gT[0:48, t * P:(t + 1) * P], ident[0:48, 0:48])
                tr.then_inc(S("gn_full"), 1)
                for br in range(3):
                    sel = C("gatesel", 48)[:, br * P:(br + 1) * P]
                    mm = pe.matmul(PS[5][:, br * 64:(br + 1) * 64], sel, gT[0:48, SEQ:NT], start=True, stop=True)
                mm.then_inc(S("gs_full"), 1)

            @block.scalar
            def _(act):
                act.dma_start(cst[:, :], consts).then_inc(S("consts_landed"), 16)
                for n, g in enumerate((g_mix, g_ffn, g_final)):
                    src = g if n == 2 else g[0]
                    act.dma_start(grow[n * KT:(n + 1) * KT, :], src.rearrange("(k p) -> k p", p=P)).then_inc(S("grow_landed"), 16)
                act.dma_start(wg48, w_in.rearrange("(k p) c -> p k c", p=P)[:, :, C_GT:C_GT + 48]).then_inc(S("wg_landed"), 16)
                for b in range(4):
                    act.sem_inc(S(f"bank_free{b}"), 1)
                act.wait_ge(S("xt_copied"), 12)
                norm_squares(act, norm1, xT)
                norm_root(act, norm1)
                for job, dst, scale in ((job_q, qT, SC), (job_kv, kvT, 1.0), (job_u, uT, 1.0)):
                    with act.Fori(0, job.n) as i:
                        for b in range(4):
                            full(act, job, b, i)
                            nc.scalar.activation(dst[:, bass.ds(i * 4 + b, 1), :].rearrange("p a n -> p (a n)"), PS[b][:, 0:NT],
                                                 ACT.Copy, scale=scale).then_inc(S(f"bank_free{b}"), 1)
                act.wait_ge(S("gate_full"), 1)
                nc.scalar.activation(gT[0:48, :], PS[6][0:48, 0:NT], ACT.Sigmoid).then_inc(S("gate_ready"), 1)

            @block.vector
            def _(dve):
                dve.wait_ge(S("gcol_full"), 1)
                nc.vector.tensor_copy(gcol[:, :], PS[6][:, 0:48]).then_inc(S("gcol_copied"), 1)
                n = 0
                for t in range(3):
                    for c in range(KT // 4):
                        dve.wait_ge(S("xt_full"), n + 1)
                        nc.vector.tensor_copy(xT[:, 4 * c:4 * c + 4, t * P:t * P + TOK[t]],
                                              PS[4 + n % 2][:, :].rearrange("p (j n) -> p j n", j=4)[:, :, 0:TOK[t]])\
                            .then_inc(S("xt_copied"), 1)
                        n += 1
                norm_scale(dve, norm1, xT, hT, 0, "h_ready")
                dve.wait_ge(S("gn_full"), 1)
                nc.vector.tensor_copy(gN[:, :, :], PS[4][:, 0:96].rearrange("p (t c) -> p t c", t=2)).then_inc(S("gn_ready"), 1)
                dve.wait_ge(S("gs_full"), 1)
                for br in range(3):
                    nc.vector.tensor_tensor(sq[:, 0, br * 64:(br + 1) * 64].rearrange("p (b q) -> p b q", q=NQ),
                                            PS[5][:, br * 64:(br + 1) * 64].rearrange("p (b q) -> p b q", q=NQ),
                                            C("qmask").unsqueeze(1).broadcast_to([P, NB, NQ]), ALU.mult)\
                        .then_inc(S("gs_masked"), 1)
                dve.wait_ge(S("gs_masked"), 3)
                nc.vector.tensor_reduce(gS[:, :, :], sq[:, 0, 0:192].rearrange("p (r b q) -> p r b q", r=3, q=NQ), AX_X, ALU.add)\
                    .then_inc(S("gs_ready"), 1)

        take = scratch(keep + 8 * NT)
        kvn = take(3 * 1536).rearrange("p (t n) -> p t n", t=3)
        un = take(3 * SSMW).rearrange("p (t n) -> p t n", t=3)
        turns = [(kvT, t, c, kvn) for t in range(3) for c in range(3)] + [(uT, t, c, un) for t in range(3) for c in range(2)]
        with program() as block:
            @block.tensor
            def _(pe):
                for n, (src, t, c, _) in enumerate(turns):
                    if n >= 4:
                        pe.wait_ge(S(("turned_dve", "turned_act")[n % 2]), n // 2 - 1)
                    for j in range(4):
                        tr = nc.tensor.transpose(PS[4 + n % 4][0:TOK[t], j * P:(j + 1) * P],
                                                 src[:, 4 * c + j, t * P:t * P + TOK[t]], ident)
                    tr.then_inc(S("turn_full"), 1)

            def copy_turns(eng, parity, copy, done):
                for n, (_, t, c, dst) in enumerate(turns):
                    if n % 2 == parity:
                        eng.wait_ge(S("turn_full"), n + 1)
                        copy(dst[0:TOK[t], t, c * 512:(c + 1) * 512], PS[4 + n % 4][0:TOK[t], :]).then_inc(S(done), 1)

            @block.vector
            def _(dve):
                copy_turns(dve, 0, nc.vector.tensor_copy, "turned_dve")

            @block.scalar
            def _(act):
                copy_turns(act, 1, nc.scalar.copy, "turned_act")

            @block.sync
            def _(sp):
                sp.wait_ge(S("turned_dve"), 5)
                sp.wait_ge(S("turned_act"), 4)
                for t in range(2):
                    sp.dma_start(kvr_prompt[0, 0, t * P:(t + 1) * P].rearrange("t a g d -> t (a g d)"),
                                 kvn[:, t, 0:1024]).then_inc(S("stored"), 16)
                    sp.dma_start(win_prompt[0, 0, t * P:(t + 1) * P].rearrange("t a g d -> t (a g d)"),
                                 kvn[:, t, 1024:1536]).then_inc(S("stored"), 16)
                sp.dma_start(kvr_sample[0].rearrange("b t a g d -> (b t) (a g d)"), kvn[0:64, 2, 0:1024]).then_inc(S("stored"), 16)
                for b in range(NB):
                    sp.dma_start(win_sample[0, b, WIN - NQ:WIN].rearrange("t a g d -> t (a g d)"),
                                 kvn[b * NQ:(b + 1) * NQ, 2, 1024:1536]).then_inc(S("stored"), 16)
                    sp.dma_start(win_sample[0, b, 0:WIN - NQ].rearrange("t a g d -> t (a g d)"),
                                 state_win[0, b, NQ:WIN].rearrange("t a g d -> t (a g d)")).then_inc(S("stored"), 16)
                sp.wait_ge(S("turned_dve"), 8)
                sp.wait_ge(S("turned_act"), 7)
                for t in range(3):
                    sp.dma_start(u_dram[t * P:t * P + TOK[t]], un[0:TOK[t], t, :]).then_inc(S("u_stored"), 16)
                sp.wait_ge(S("u_stored"), 48)
                sp.wait_ge(S("stored"), 21 * 16)

        PG, NPART = 8, GH // 8
        take = scratch(keep)
        urows = take(L * PG * 32).rearrange("p (s c) -> p s c", s=L)
        Q = take(2 * PG * 9 * CH).rearrange("p (r g k c) -> p r g k c", r=2, g=PG, k=9)
        tq = take(2 * PG * 9 * CH)
        Tt = take(2 * PG * P).rearrange("p (h g n) -> p h g n", h=2, g=PG)
        Ga = take(PG * P).rearrange("p (g n) -> p g n", g=PG)
        UTa = take(PG * 80).rearrange("p (g n) -> p g n", g=PG)
        ea = take(NCH * 2 * PG).rearrange("p (c r g) -> p c r g", c=NCH, r=2)
        Ha = take(NCH * 2 * PG).rearrange("p (c r g) -> p c r g", c=NCH, r=2)
        Bb = take(2 * GH * CH).rearrange("p (r g c) -> p r g c", r=2, g=GH)
        Ct = take(2 * GH * CH).rearrange("p (r g c) -> p r g c", r=2, g=GH)
        PK = take(2 * 9 * GH).rearrange("p (r k g) -> p r k g", r=2, k=9)
        NPI = take(9 * GH).rearrange("p (k g) -> p k g", k=9)
        NPR = take(9 * GH).rearrange("p (k g) -> p k g", k=9)
        RK = take(2 * GH * L).rearrange("p (r g s) -> p r g s", r=2, g=GH)
        H0 = take(2 * NB * GH).rearrange("p (r b g) -> p r b g", r=2, b=NB)
        FinS = take(2 * NB * GH).rearrange("p (r b g) -> p r b g", r=2, b=NB)
        FinP = take(2 * GH).rearrange("p (r g) -> p r g", r=2)
        dcol = take(GH)
        dI = take(PG * CH).rearrange("p (g c) -> p g c", g=PG)
        ust = [take(256).rearrange("p (h s c) -> p h s c", h=2, s=L) for _ in range(2)]
        take_ys = scratch(0, ysT[:, :, :].rearrange("p k n -> p (k n)"), 8 * NT)
        stg_fin = take_ys(2 * 3 * P).rearrange("p (r t n) -> p r t n", r=2, t=3)
        EB = [take_ys(256).rearrange("p (r s c) -> p r s c", r=2, s=L) for _ in range(2)]
        tA = [take_ys(256).rearrange("p (r s c) -> p r s c", r=2, s=L) for _ in range(2)]
        tB = [take_ys(256).rearrange("p (r s c) -> p r s c", r=2, s=L) for _ in range(2)]
        stg = [take(336) for _ in range(2)]
        Bst = [take(64).rearrange("p (r h c) -> p r h c", r=2, h=2) for _ in range(2)]
        Hst = [take(160).rearrange("p (h r n) -> p h r n", h=2, r=2) for _ in range(2)]
        UTst = [take(80) for _ in range(2)]
        sc = take(3 * 2 * PG).rearrange("p (t r g) -> p t r g", t=3, r=2)
        par = ysT[:, :, :].rearrange("p k n -> p (k n)")
        Cn = par[:, 0:2048].rearrange("p (r t d s) -> p r t d s", r=2, t=8, d=2)
        h0n = oT[:, :, :].rearrange("p k n -> p (k n)")[:, 0:512].rearrange("p (r t n) -> p r t n", r=2, t=2)
        lamn = oT[:, :, :].rearrange("p k n -> p (k n)")[:, 512:896].rearrange("p (a n) -> p a n", a=3)
        ldn = oT[:, :, :].rearrange("p k n -> p (k n)")[:, 896:898]
        Bn = oT[:, :, :].rearrange("p k n -> p (k n)")[:, 1024:2048].rearrange("p (r g c) -> p r g c", r=2, g=GH)
        tp = oT[:, :, :].rearrange("p k n -> p (k n)")[:, 2048:2560].rearrange("p (t g) -> p t g", t=16)
        tb = tq[:, 0:1024].rearrange("p (t g c) -> p t g c", t=2, g=GH)

        with program() as block:
            @block.sync
            def _(sp):
                for r, c in enumerate((c_re, c_im)):
                    for d in range(2):
                        sp.dma_start(Cn[:, r, :, d, :], c[0].rearrange("(t g) c p -> (g c) t p", g=8)).then_inc(S("cn_landed"), 16)
                for r, h in enumerate((h0_re, h0_im)):
                    sp.dma_start(h0n[:, r, :, :], h[0].rearrange("b g p -> (b g p)").rearrange("(t a n) -> a t n", a=P, n=P))\
                        .then_inc(S("h0_landed"), 16)
                for part in range(NPART):
                    if part:
                        sp.wait_ge(S("y_stored"), 16 * part)
                    sp.dma_start(urows[0:NCH, :, :], u_dram.rearrange("(a s) c -> a s c", s=L)[:, :, part * PG * 32:(part + 1) * PG * 32])\
                        .then_inc(S("u_landed"), 16)
                    sp.wait_ge(S("g_diag"), part + 1)
                    sp.wait_ge(S("t_zero"), 1)
                    if part:
                        sp.wait_ge(S("y_copied"), PG * part + 2)
                    for s in range(L):
                        for h in range(2):
                            sp.dma_start(Tt[s * CH:(s + 1) * CH, h, :, s * CH:P], Ga[h * CH:(h + 1) * CH, :, 0:P - s * CH])\
                                .then_inc(S("t_landed"), 16)
                    sp.wait_ge(S("y_copied"), PG * (part + 1) + 2)
                    sp.dma_start(y_dram.rearrange("(a s) c -> a s c", s=L)[:, :, part * PG * 32:(part + 1) * PG * 32],
                                 urows[0:NCH, :, :]).then_inc(S("y_stored"), 16)
                for r, (op, os) in enumerate(((sre_prompt, sre_sample), (sim_prompt, sim_sample))):
                    sp.wait_ge(S("fin_copied"), r + 1)
                    for t in range(2):
                        sp.dma_start(os[0].rearrange("b g p -> (b g p)").rearrange("(t a n) -> t a n", a=P, n=P)[t],
                                     stg_fin[:, r, t, :]).then_inc(S("stored"), 16)
                    sp.dma_start(op[0, 0].rearrange("(g h) p -> g (h p)", h=2), stg_fin[0:GH, r, 2, :]).then_inc(S("stored"), 16)
                sp.wait_ge(S("stored"), (21 + 6) * 16)

            @block.gpsimd
            def _(pool):
                nc.gpsimd.memset(Tt, 0.0).then_inc(S("t_zero"), 1)
                pool.wait_ge(S("bbar_ready"), 1)
                for part in range(NPART):
                    pool.wait_ge(S("u_landed"), 16 * (part + 1))
                    with pool.Fori(0, PG // 2) as i:
                        for u in range(2):
                            n = part * PG + u
                            pool.wait_ge(S("turned"), i * 2 + n + 1)
                            pool.wait_ge(S("eg_full"), i * 2 + n + 1)
                            src = urows[0:NCH, :, bass.ds(i * 64 + u * 32, 32)].rearrange("p s (h c) -> p h s c", h=2)
                            nc.gpsimd.tensor_copy(ust[u][0:NCH], src)
                            nc.gpsimd.tensor_tensor(Bst[u], Bb[:, :, bass.ds(i * 2 + n, 1), :].broadcast_to([P, 2, 2, CH]),
                                                    C("half").unsqueeze(1).unsqueeze(3).broadcast_to([P, 2, 2, CH]), ALU.mult)\
                                .then_inc(S("u_staged"), 1)
                    pool.wait_ge(S("h_done"), part + 1)
                    with pool.Fori(0, PG // 2) as i:
                        for u in range(2):
                            n = part * PG + u
                            pool.wait_ge(S("y_full"), i * 2 + n + 1)
                            nc.gpsimd.tensor_copy(UTst[u], UTa[:, bass.ds(i * 2 + u, 1), :].rearrange("p a n -> p (a n)"))
                            nc.gpsimd.tensor_tensor(Hst[u], Ha[:, :, :, bass.ds(i * 2 + u, 1)].rearrange("p c r a -> p a r c").broadcast_to([P, 2, 2, NCH]),
                                                    C("half").unsqueeze(2).unsqueeze(3).broadcast_to([P, 2, 2, NCH]), ALU.mult)\
                                .then_inc(S("h_staged"), 1)

            @block.tensor
            def _(pe):
                for name, k in (("turned", 2), ("eg_full", 2), ("y_full", 2)):
                    pe.sem_inc(S(name), k)
                pe.wait_ge(S("ldt_rows"), 1)
                for a in range(3):
                    tr = nc.tensor.transpose(PS[0][:, a * GH:(a + 1) * GH], lamn[0:GH, a, :], ident[0:GH, 0:GH])
                tr.then_inc(S("lam_full"), 1)
                pe.wait_ge(S("cn_landed"), 64)
                for r in range(2):
                    for t in range(8):
                        tr = nc.tensor.transpose(PS[4 + 2 * r + t // 4][:, (t % 4) * P:(t % 4 + 1) * P],
                                                 Cn[:, r, t, :, :].rearrange("p d s -> p (d s)"), ident)
                tr.then_inc(S("ct_full"), 1)
                pe.wait_ge(S("h0_landed"), 32)
                for r in range(2):
                    for t in range(2):
                        tr = nc.tensor.transpose(PS[1][:, (2 * r + t) * P:(2 * r + t + 1) * P], h0n[:, r, t, :], ident)
                tr.then_inc(S("h0_full"), 1)
                pe.wait_ge(S("ct_ready"), 1)
                for part in range(NPART):
                    pe.wait_ge(S("q_ready"), part + 1)
                    with pe.Fori(0, PG // 2) as i:
                        for u in range(2):
                            n = part * PG + u
                            pe.wait_ge(S("u_staged"), i * 2 + n + 1)
                            pe.wait_ge(S("eb_ready"), i * 2 + n + 1)
                            for r in range(2):
                                nc.tensor.transpose(PS[4 + u][:, r * P:(r + 1) * P], EB[u][:, r].rearrange("p s c -> p (s c)"), ident)
                            for h in range(2):
                                tr = nc.tensor.transpose(PS[4 + u][:, 256 + h * NCH:256 + (h + 1) * NCH],
                                                         ust[u][0:NCH, h].rearrange("p s c -> p (s c)"), ident[0:NCH, 0:NCH])
                            tr.then_inc(S("turned"), 1)
                        for u in range(2):
                            n = part * PG + u
                            pe.wait_ge(S("eg_staged"), i * 2 + n + 1)
                            pe.wait_ge(S("e_copied"), i * 2 + n + 1)
                            pe.wait_ge(S("g_copied"), i * 2 + n + 1)
                            for h in range(2):
                                for r in range(2):
                                    pe.matmul(PS[6][h * 64:(h + 1) * 64, r * NCH:(r + 1) * NCH],
                                              stg[u][:, r * P + h * 64:r * P + (h + 1) * 64],
                                              stg[u][:, 256 + h * NCH:256 + (h + 1) * NCH], start=True, stop=True)
                            for r in range(2):
                                mm = pe.matmul(PS[7][0:32, 0:P], Bst[u][:, r].rearrange("p h c -> p (h c)"),
                                               Q[:, r, bass.ds(i * 2 + u, 1), 0:L, :].rearrange("p a k c -> p (a k c)"),
                                               start=r == 0, stop=r == 1)
                            mm.then_inc(S("eg_full"), 1)
                    pe.wait_ge(S("t_landed"), 256 * (part + 1))
                    with pe.Fori(0, PG // 2) as i:
                        for u in range(2):
                            n = part * PG + u
                            pe.wait_ge(S("h_staged"), i * 2 + n + 1)
                            pe.wait_ge(S("y_copied"), i * 2 + n + 1)
                            for h in range(2):
                                out = PS[4 + u][0:NCH, h * P:(h + 1) * P]
                                pe.matmul(out, UTst[u][:, h * NCH:(h + 1) * NCH],
                                          Tt[:, h, bass.ds(i * 2 + u, 1), :].rearrange("p a n -> p (a n)"), start=True, stop=False)
                                for r in range(2):
                                    mm = pe.matmul(out, Hst[u][:, h, r, :],
                                                   Q[:, r, bass.ds(i * 2 + u, 1), 1:L + 1, :].rearrange("p a k c -> p (a k c)"),
                                                   start=False, stop=r == 1)
                            mm.then_inc(S("y_full"), 1)
                pe.wait_ge(S("fin_ready"), 1)
                for r in range(2):
                    if r:
                        pe.wait_ge(S("fin_copied"), r)
                    for t in range(2):
                        nc.tensor.transpose(PS[6][:, t * P:(t + 1) * P], FinS[:, r, 4 * t:4 * t + 4, :].rearrange("p b g -> p (b g)"), ident)
                    nc.tensor.transpose(PS[6][0:GH, 256:384], FinP[:, r, :], ident).then_inc(S("fin_full"), 1)

            @block.scalar
            def _(act):
                act.sem_inc(S("g_copied"), 1)
                act.sem_inc(S("y_copied"), 2)
                for a, lam in enumerate((lam_re, lam_im)):
                    act.dma_start(lamn[0:GH, a, :], lam[0].rearrange("(g h) p -> g (h p)", h=2)).then_inc(S("lam_landed"), 16)
                act.dma_start(ldn[0:GH, :], log_dt[0].rearrange("(g h) -> g h", h=2)).then_inc(S("lam_landed"), 16)
                for r, b in enumerate((b_re, b_im)):
                    for h in range(2):
                        act.dma_start(Bn[h * 64:(h + 1) * 64, r, :, :], b[0].rearrange("(g h) p c -> h p g c", h=2)[h])\
                            .then_inc(S("bn_landed"), 16)
                act.dma_start(dcol[0:32, :], ssm_d[0].rearrange("(g a) -> a g", a=32)).then_inc(S("d_landed"), 16)
                act.wait_ge(S("lam_ready"), 1)
                nc.scalar.activation(tp[:, 3, :], tp[:, 2, :], ACT.Exp).then_inc(S("dt_ready"), 1)
                act.wait_ge(S("arg_ready"), 1)
                nc.scalar.activation(tp[:, 6, :], tp[:, 4, :], ACT.Exp).then_inc(S("mag_ready"), 1)
                act.wait_ge(S("arg_ready"), 2)
                nc.scalar.activation(tp[:, 9, :], tp[:, 7, :], ACT.Sin)
                nc.scalar.activation(tp[:, 10, :], tp[:, 8, :], ACT.Sin).then_inc(S("sin_ready"), 1)
                for part in range(NPART):
                    with act.Fori(0, PG // 2) as i:
                        for u in range(2):
                            n = part * PG + u
                            act.wait_ge(S("turned"), i * 2 + n + 3)
                            act.wait_ge(S("eg_full"), i * 2 + n + 1)
                            nc.scalar.copy(UTa[:, bass.ds(i * 2 + u, 1), :].rearrange("p a n -> p (a n)"), PS[4 + u][:, 256:336])
                            nc.scalar.copy(stg[u], PS[4 + u][:, 0:336]).then_inc(S("eg_staged"), 1)
                        for u in range(2):
                            n = part * PG + u
                            act.wait_ge(S("eg_full"), i * 2 + n + 3)
                            nc.scalar.copy(Ga[0:32, bass.ds(i * 2 + u, 1), :].rearrange("p a n -> p (a n)"), PS[7][0:32, 0:P])\
                                .then_inc(S("g_copied"), 1)
                    with act.Fori(0, PG // 2) as i:
                        for u in range(2):
                            n = part * PG + u
                            act.wait_ge(S("y_full"), i * 2 + n + 3)
                            nc.scalar.copy(urows[0:NCH, :, bass.ds(i * 64 + u * 32, 32)].rearrange("p s (h c) -> p h s c", h=2),
                                           PS[4 + u][0:NCH, 0:256].rearrange("p (h s c) -> p h s c", h=2, s=L)).then_inc(S("y_copied"), 1)

            @block.vector
            def _(dve):
                V = nc.vector
                order = [0]

                def link(ins):
                    order[0] += 1
                    ins.then_inc(S("s5_order"), 1)
                    dve.wait_ge(S("s5_order"), order[0])

                dve.sem_inc(S("e_copied"), 1)
                dve.wait_ge(S("lam_landed"), 48)
                V.tensor_copy(lamn[0:GH, 2, :].rearrange("p (h s) -> p h s", h=2),
                              ldn[0:GH, :].unsqueeze(2).broadcast_to([GH, 2, 64])).then_inc(S("ldt_rows"), 1)
                dve.wait_ge(S("lam_full"), 1)
                V.tensor_copy(tp[:, 0:3, :], PS[0][:, 0:96].rearrange("p (a g) -> p a g", a=3)).then_inc(S("lam_ready"), 1)
                dve.wait_ge(S("lam_ready"), 1)
                dve.wait_ge(S("dt_ready"), 1)
                V.tensor_tensor(tp[:, 4, :], tp[:, 0, :], tp[:, 3, :], ALU.mult).then_inc(S("arg_ready"), 1)
                link(V.tensor_tensor(tp[:, 5, :], tp[:, 1, :], tp[:, 3, :], ALU.mult))
                link(V.tensor_scalar(tp[:, 7, :], tp[:, 5, :], float(1 / (2 * np.pi)), MAGIC, ALU.mult, ALU.add))
                link(V.tensor_scalar(tp[:, 7, :], tp[:, 7, :], MAGIC, None, ALU.subtract))
                link(V.scalar_tensor_tensor(out=tp[:, 8, :], in0=tp[:, 7, :], scalar=-TWO_PI_HI, in1=tp[:, 5, :], op0=ALU.mult, op1=ALU.add))
                link(V.scalar_tensor_tensor(out=tp[:, 11, :], in0=tp[:, 7, :], scalar=-TWO_PI_LO, in1=tp[:, 8, :], op0=ALU.mult, op1=ALU.add))
                link(V.tensor_scalar(tp[:, 7, :], tp[:, 11, :], 3.1415925, -3.1415925, ALU.min, ALU.max))
                link(V.tensor_scalar(tp[:, 12, :], tp[:, 7, :], -1.0, None, ALU.mult))
                link(V.tensor_tensor(tp[:, 13, :], tp[:, 12, :], tp[:, 7, :], ALU.max))
                V.tensor_scalar(tp[:, 8, :], tp[:, 13, :], -1.0, float(np.pi / 2), ALU.mult, ALU.add).then_inc(S("arg_ready"), 1)
                dve.wait_ge(S("sin_ready"), 1)
                dve.wait_ge(S("mag_ready"), 1)
                V.tensor_tensor(PK[:, 0, 1, :], tp[:, 6, :], tp[:, 10, :], ALU.mult)
                link(V.tensor_tensor(PK[:, 1, 1, :], tp[:, 6, :], tp[:, 9, :], ALU.mult))
                V.memset(PK[:, 0, 0, :], 1.0)
                V.memset(PK[:, 1, 0, :], 0.0)
                V.tensor_scalar(tp[:, 7, :], PK[:, 0, 1, :], -1.0, None, ALU.add)
                V.tensor_tensor(tp[:, 8, :], tp[:, 0, :], tp[:, 0, :], ALU.mult)
                link(V.tensor_tensor(tp[:, 9, :], tp[:, 1, :], tp[:, 1, :], ALU.mult))
                link(V.tensor_tensor(tp[:, 8, :], tp[:, 8, :], tp[:, 9, :], ALU.add))
                V.reciprocal(tp[:, 9, :], tp[:, 8, :])
                V.tensor_tensor(tp[:, 10, :], tp[:, 7, :], tp[:, 0, :], ALU.mult)
                V.tensor_tensor(tp[:, 11, :], PK[:, 1, 1, :], tp[:, 1, :], ALU.mult)
                V.tensor_tensor(tp[:, 12, :], PK[:, 1, 1, :], tp[:, 0, :], ALU.mult)
                link(V.tensor_tensor(tp[:, 13, :], tp[:, 7, :], tp[:, 1, :], ALU.mult))
                V.tensor_tensor(tp[:, 10, :], tp[:, 10, :], tp[:, 11, :], ALU.add)
                link(V.tensor_tensor(tp[:, 12, :], tp[:, 12, :], tp[:, 13, :], ALU.subtract))
                V.tensor_tensor(tp[:, 14, :], tp[:, 10, :], tp[:, 9, :], ALU.mult)
                link(V.tensor_tensor(tp[:, 15, :], tp[:, 12, :], tp[:, 9, :], ALU.mult))
                for k in range(1, L):
                    V.tensor_tensor(tp[:, 7, :], PK[:, 0, k, :], PK[:, 0, 1, :], ALU.mult)
                    V.tensor_tensor(tp[:, 8, :], PK[:, 1, k, :], PK[:, 1, 1, :], ALU.mult)
                    V.tensor_tensor(tp[:, 10, :], PK[:, 0, k, :], PK[:, 1, 1, :], ALU.mult)
                    link(V.tensor_tensor(tp[:, 11, :], PK[:, 1, k, :], PK[:, 0, 1, :], ALU.mult))
                    V.tensor_tensor(PK[:, 0, k + 1, :], tp[:, 7, :], tp[:, 8, :], ALU.subtract)
                    link(V.tensor_tensor(PK[:, 1, k + 1, :], tp[:, 10, :], tp[:, 11, :], ALU.add))
                V.tensor_scalar(NPI, PK[:, 1], -1.0, None, ALU.mult)
                link(V.tensor_scalar(NPR, PK[:, 0], -1.0, None, ALU.mult))
                for s in range(L):
                    V.tensor_copy(RK[:, :, :, s], PK[:, :, L - 1 - s, :])
                dve.wait_ge(S("bn_landed"), 64)
                fr, fi = (tp[:, 14 + r, :].unsqueeze(2).broadcast_to([P, GH, CH]) for r in range(2))
                V.tensor_tensor(Bb[:, 0], Bn[:, 0], fr, ALU.mult)
                V.tensor_tensor(Bb[:, 1], Bn[:, 1], fr, ALU.mult)
                V.tensor_tensor(tb[:, 0], Bn[:, 1], fi, ALU.mult)
                link(V.tensor_tensor(tb[:, 1], Bn[:, 0], fi, ALU.mult))
                V.tensor_tensor(Bb[:, 0], Bb[:, 0], tb[:, 0], ALU.subtract)
                V.tensor_tensor(Bb[:, 1], Bb[:, 1], tb[:, 1], ALU.add).then_inc(S("bbar_ready"), 1)
                dve.wait_ge(S("bbar_ready"), 1)
                dve.wait_ge(S("ct_full"), 1)
                for r in range(2):
                    for b in range(2):
                        for h in range(2):
                            V.tensor_copy(Ct[h * 64:(h + 1) * 64, r, b * 16:(b + 1) * 16, :],
                                          PS[4 + 2 * r + b][h * 64:(h + 1) * 64, :].rearrange("p (g h c) -> p g h c", h=2, c=CH)[:, :, h, :])
                dve.wait_ge(S("h0_full"), 1)
                link(V.tensor_copy(H0.rearrange("p r b g -> p (r b g)"), PS[1][:, :]))
                V.memset(Ha[:, 0, :, :], 0.0).then_inc(S("ct_ready"), 1)
                dve.wait_ge(S("d_landed"), 16)
                for part in range(NPART):
                    gs = slice(part * PG, (part + 1) * PG)

                    def spread(table):
                        return table[:, :, gs].rearrange("p k g -> p g k").unsqueeze(3).broadcast_to([P, PG, 9, CH])

                    def rows(r):
                        return Ct[:, r, gs, :].unsqueeze(2).broadcast_to([P, PG, 9, CH])

                    t1 = tq[:, 0:PG * 9 * CH].rearrange("p (g k c) -> p g k c", g=PG, k=9)
                    if part:
                        dve.wait_ge(S("y_full"), PG * part + 2)
                    V.tensor_tensor(Q[:, 0], rows(0), spread(PK[:, 0]), ALU.mult)
                    link(V.tensor_tensor(t1, rows(1), spread(NPI), ALU.mult))
                    link(V.tensor_tensor(Q[:, 0], Q[:, 0], t1, ALU.add))
                    V.tensor_tensor(Q[:, 1], rows(0), spread(NPI), ALU.mult)
                    link(V.tensor_tensor(t1, rows(1), spread(NPR), ALU.mult))
                    V.tensor_tensor(Q[:, 1], Q[:, 1], t1, ALU.add).then_inc(S("q_ready"), 1)
                    with dve.Fori(0, PG // 2) as i:
                        for u in range(2):
                            n = part * PG + u
                            bb = Bb[:, :, bass.ds(i * 2 + n, 1), :].rearrange("p r a c -> p r (a c)").unsqueeze(2).broadcast_to([P, 2, L, CH])
                            rk = [RK[:, r, bass.ds(i * 2 + n, 1), :].rearrange("p a s -> p (a s)").unsqueeze(1).unsqueeze(3)
                                  .broadcast_to([P, 2, L, CH]) for r in range(2)]
                            dve.wait_ge(S("turned"), i * 2 + n + 1)
                            V.tensor_tensor(tA[u], bb, rk[0], ALU.mult)
                            V.tensor_tensor(tB[u], bb, rk[1], ALU.mult).then_inc(S("eb_parts"), 1)
                            dve.wait_ge(S("eb_parts"), i * 2 + n + 1)
                            V.tensor_tensor(EB[u][:, 0], tA[u][:, 0], tB[u][:, 1], ALU.subtract)
                            V.tensor_tensor(EB[u][:, 1], tB[u][:, 0], tA[u][:, 1], ALU.add).then_inc(S("eb_ready"), 1)
                        for u in range(2):
                            n = part * PG + u
                            dve.wait_ge(S("eg_full"), i * 2 + n + 3)
                            V.tensor_copy(ea[:, :, :, bass.ds(i * 2 + u, 1)].rearrange("p c r a -> p r (c a)"),
                                          PS[6][:, 0:2 * NCH].rearrange("p (r c) -> p r c", r=2)).then_inc(S("e_copied"), 1)
                    V.tensor_tensor(dI[0:32], C("chandiag", 32).unsqueeze(1).broadcast_to([32, PG, CH]),
                                    dcol[0:32, gs].unsqueeze(2).broadcast_to([32, PG, CH]), ALU.mult).then_inc(S("s5_order"), 1)
                    order[0] += 1
                    dve.wait_ge(S("s5_order"), order[0])
                    dve.wait_ge(S("g_copied"), PG * (part + 1) + 1)
                    V.tensor_tensor(Ga[0:32, :, 0:CH], Ga[0:32, :, 0:CH], dI[0:32], ALU.add).then_inc(S("g_diag"), 1)
                    dve.wait_ge(S("e_copied"), PG * (part + 1) + 1)
                    dve.wait_ge(S("g_diag"), part + 1)
                    a8r = PK[:, 0, L, gs].unsqueeze(1).broadcast_to([P, 2, PG])
                    if part:
                        dve.wait_ge(S("h_staged"), PG * part)
                    V.tensor_copy(Ha[:, NPC:NCH, :, :].rearrange("p b r g -> p r b g")[:, 0], H0[:, 0, :, gs])
                    link(V.tensor_copy(Ha[:, NPC:NCH, :, :].rearrange("p b r g -> p r b g")[:, 1], H0[:, 1, :, gs]))

                    with dve.Fori(0, NPC - 1) as i:
                        def at(buf, k):
                            return buf[:, bass.ds(i + k, 1), :, :].rearrange("p a r g -> p (a r) g")
                        base = part * 3 * (NPC - 1)
                        V.tensor_tensor(sc[:, 0], a8r, at(Ha, 0), ALU.mult)
                        V.tensor_tensor(sc[:, 1, 0, :], NPI[:, L, gs], at(Ha, 0)[:, 1, :], ALU.mult)
                        V.tensor_tensor(sc[:, 1, 1, :], PK[:, 1, L, gs], at(Ha, 0)[:, 0, :], ALU.mult).then_inc(S("scan_order"), 1)
                        dve.wait_ge(S("scan_order"), i * 3 + (base + 1))
                        V.tensor_tensor(sc[:, 2], sc[:, 0], at(ea, 0), ALU.add).then_inc(S("scan_order"), 1)
                        dve.wait_ge(S("scan_order"), i * 3 + (base + 2))
                        V.tensor_tensor(at(Ha, 1), sc[:, 2], sc[:, 1], ALU.add).then_inc(S("scan_order"), 1)
                        dve.wait_ge(S("scan_order"), i * 3 + (base + 3))
                    last = NPC - 1
                    V.tensor_tensor(sc[:, 0], a8r, Ha[:, last], ALU.mult)
                    V.tensor_tensor(sc[:, 1, 0, :], NPI[:, L, gs], Ha[:, last, 1, :], ALU.mult)
                    link(V.tensor_tensor(sc[:, 1, 1, :], PK[:, 1, L, gs], Ha[:, last, 0, :], ALU.mult))
                    link(V.tensor_tensor(sc[:, 2], sc[:, 0], ea[:, last], ALU.add))
                    link(V.tensor_tensor(FinP[:, :, gs], sc[:, 2], sc[:, 1], ALU.add))
                    ser, sei = (ea[:, NPC:NCH, r, :] for r in range(2))
                    pr, npi, pi = (x[:, L, gs].unsqueeze(1).broadcast_to([P, NB, PG]) for x in (PK[:, 0], NPI, PK[:, 1]))
                    s1, s2 = (tq[:, k * 64:(k + 1) * 64].rearrange("p (b g) -> p b g", b=NB) for k in range(2))
                    for r, (x, y) in enumerate(((npi, 1), (pi, 0))):
                        V.tensor_tensor(s1, pr, H0[:, r, :, gs], ALU.mult)
                        link(V.tensor_tensor(s2, x, H0[:, y, :, gs], ALU.mult))
                        link(V.tensor_tensor(s1, s1, s2, ALU.add))
                        link(V.tensor_tensor(FinS[:, r, :, gs], s1, (ser, sei)[r], ALU.add))
                    dve.sem_inc(S("h_done"), 1)
                dve.sem_inc(S("fin_ready"), 1)
                for r in range(2):
                    dve.wait_ge(S("fin_full"), r + 1)
                    V.tensor_copy(stg_fin[:, r, 0:2, :], PS[6][:, 0:256].rearrange("p (t n) -> p t n", t=2))
                    V.tensor_copy(stg_fin[0:GH, r, 2, :], PS[6][0:GH, 256:384]).then_inc(S("fin_copied"), 1)

        take = scratch(keep)
        yn = take(3 * SSMW).rearrange("p (t n) -> p t n", t=3)
        with program() as block:
            @block.sync
            def _(sp):
                sp.wait_ge(S("y_stored"), 16 * NPART)
                for t in range(3):
                    sp.dma_start(yn[0:TOK[t], t, :], y_dram[t * P:t * P + TOK[t]]).then_inc(S("yn_landed"), 16)

            @block.tensor
            def _(pe):
                pe.wait_ge(S("yn_landed"), 48)
                for n in range(6):
                    t, c = n // 2, n % 2
                    if n >= 4:
                        pe.wait_ge(S("ys_ready"), n - 3)
                    for j in range(4):
                        tr = nc.tensor.transpose(PS[4 + n % 4][:, j * P:j * P + TOK[t]],
                                                 yn[0:TOK[t], t, (4 * c + j) * P:(4 * c + j + 1) * P], ident[0:TOK[t], 0:TOK[t]])
                    tr.then_inc(S("ys_full"), 1)

            @block.scalar
            def _(act):
                for n in range(6):
                    t, c = n // 2, n % 2
                    act.wait_ge(S("ys_full"), n + 1)
                    nc.scalar.activation(ysT[:, 4 * c:4 * c + 4, t * P:t * P + TOK[t]],
                                         PS[4 + n % 4][:, :].rearrange("p (j n) -> p j n", j=4)[:, :, 0:TOK[t]],
                                         ACT.Gelu_apprx_tanh).then_inc(S("ys_ready"), 1)

        take = scratch(keep)
        kvp = take(2 * 1536).rearrange("p (t n) -> p t n", t=2)
        Sb = [take(4 * SEQ).rearrange("p (h k) -> p h k", h=4) for _ in range(2)]
        PTs = [take(4 * SEQ).rearrange("p (b h q) -> p b h q", b=2, h=4) for _ in range(2)]
        oacc = take(2 * 1024).rearrange("p (t h d) -> p t h d", t=2, h=NH)
        ot = [take(256).rearrange("p (h d) -> p h d", h=4) for _ in range(2)]
        nmx, rs, wgt = (take(64).rearrange("p (n h) -> p n h", h=4) for _ in range(3))
        pcol = take(4).rearrange("p (v m) -> p v m", v=2)
        pe32 = take(2 * P).rearrange("p (v d s) -> p v d s", v=2, d=2)
        pl32 = take(2)
        pl = take(2 * 2 * 16).rearrange("p (a c) -> p a c", a=4)
        Gp = take(4 * 32).rearrange("p (a c) -> p a c", a=4)
        Gr = take(2 * P).rearrange("p (g n c) -> p g n c", g=2, n=4)
        kcT = take(32).rearrange("p (g c) -> p g c", g=2)
        Vbd = take(4 * 256).rearrange("p (g n d) -> p g n d", g=4, n=4)
        Pc = take(512).rearrange("p (h c) -> p h c", h=NH)
        PcT = take(512)
        cm, cs_, cw = (take(NH) for _ in range(3))
        Sc = take(NH * NC_P).rearrange("p (h c) -> p h c", h=NH)
        work = [(qt, br, g) for qt in range(2) for br in range(2) for g in range(NKV)]
        NW = len(work)

        with program() as block:
            @block.sync
            def _(sp):
                for t in range(2):
                    sp.dma_start(kvp[:, t, 0:1024], kvr_prompt[0, 0, t * P:(t + 1) * P].rearrange("t a g d -> t (a g d)")).then_inc(S("kvp_landed"), 16)
                    sp.dma_start(kvp[:, t, 1024:1536], win_prompt[0, 0, t * P:(t + 1) * P].rearrange("t a g d -> t (a g d)")).then_inc(S("kvp_landed"), 16)
                sp.dma_start(x_dram, xT[:, :, :]).then_inc(S("x_spilled"), 16)
                sp.wait_ge(S("x_spilled"), 16)

            @block.gpsimd
            def _(pool):
                nc.gpsimd.memset(phi[:, :, :], 0.0).then_inc(S("phi_zero"), 1)
                nc.gpsimd.memset(Gp, 0.0).then_inc(S("pads_zero"), 1)
                nc.gpsimd.memset(Vbd, 0.0).then_inc(S("pads_zero"), 1)
                nc.gpsimd.memset(Pc, 0.0).then_inc(S("pads_zero"), 1)
                nc.gpsimd.tensor_copy(qs[:, :, :], qT[:, :, SEQ:NT]).then_inc(S("qs_ready"), 1)
                nc.gpsimd.tensor_copy(ks[:, 0:2, :], kvT[:, 4:6, SEQ:NT]).then_inc(S("qs_ready"), 1)
                nc.gpsimd.tensor_copy(ks[:, 2:4, :], kvT[:, 8:10, SEQ:NT]).then_inc(S("qs_ready"), 1)

            @block.scalar
            def _(act):
                for n in range(8):
                    act.dma_start(pcol[n * 16:(n + 1) * 16, :, :], w_pool[0].rearrange("v (m s) -> s v m", s=16)).then_inc(S("pool_landed"), 16)
                act.dma_start(pl32[0:32, :], w_pool[0].rearrange("v l -> l v")).then_inc(S("pool_landed"), 16)
                for d in range(2):
                    act.dma_start(pe32[0:32, :, d, :], w_pe[0].rearrange("v l d -> l v d")).then_inc(S("pool_landed"), 16)
                act.wait_ge(S("phi_zero"), 1)
                for h in range(2):
                    act.dma_start(phi[h * 64:(h + 1) * 64, :, h * 64:(h + 1) * 64], w_phi[0].rearrange("v a b -> a v b")).then_inc(S("phi_landed"), 16)
                act.wait_ge(S("pads_zero"), 3)
                act.wait_ge(S("ppool_ready"), 1)
                nc.scalar.activation(Gp[:, :, 0:NC_P], pl[:, :, 0:NC_P], ACT.Gelu_apprx_tanh).then_inc(S("pgelu_ready"), 1)
                for qt in range(2):
                    act.wait_ge(S("pc_shifted"), qt + 1)
                    nc.scalar.activation(Sc, Sc, ACT.Exp).then_inc(S("pc_exp"), 1)
                    act.wait_ge(S("pct_full"), qt + 1)
                    nc.scalar.copy(PcT, PS[7][:, :]).then_inc(S("pct_copied"), 1)
                for n in range(NW + 1):
                    if n < NW:
                        KE = P * (work[n][0] + 1)
                        act.wait_ge(S("pmax_ready"), n + 1)
                        for h in range(4):
                            ins = nc.scalar.activation(Sb[n % 2][:, h, 0:KE], Sb[n % 2][:, h, 0:KE], ACT.Exp,
                                                       bias=nmx[:, n, h:h + 1], accum_out=rs[:, n, h:h + 1])
                        ins.then_inc(S("p_ready"), 1)
                    if n >= 1:
                        m = n - 1
                        act.wait_ge(S("pt_full"), m + 1)
                        if m >= 2:
                            act.wait_ge(S("o_full"), m - 1)
                        for kb in range(work[m][0] + 1):
                            ins = nc.scalar.copy(PTs[m % 2][:, kb].rearrange("p h q -> p (h q)"), PS[4 + kb][:, :])
                        ins.then_inc(S("pt_copied"), 1)

            @block.tensor
            def _(pe):
                pe.wait_ge(S("pool_landed"), 176)
                for v in range(2):
                    mm = pe.matmul(PS[5][:, v:v + 1], pe32[0:32, v].rearrange("p d s -> p (d s)"), pl32[0:32, v:v + 1], start=True, stop=True)
                mm.then_inc(S("pec_full"), 1)
                pe.wait_ge(S("poolw_ready"), 1)
                pe.wait_ge(S("kvp_landed"), 64)
                for t in range(2):
                    for a in range(4):
                        mm = pe.matmul(PS[6][:, a * 32:(a + 1) * 32].rearrange("p (m t n) -> p m t n", m=2, t=2)[:, :, t, :],
                                       kvp[:, t, a * P:(a + 1) * P], poolw[:, a // 2].rearrange("p m n -> p (m n)"), start=True, stop=True)
                mm.then_inc(S("ppool_full"), 1)
                pe.wait_ge(S("pgr_ready"), 1)
                pe.wait_ge(S("phi_landed"), 32)
                for g in range(2):
                    pe.matmul(PS[7][:, g * 16:g * 16 + NC_P], phi[:, 0, :], Gp[:, g, 0:NC_P], start=True, stop=True)
                for g in range(2):
                    mm = pe.matmul(PS[7][:, 64 + g * P:64 + (g + 1) * P], Gr[:, g].rearrange("p n c -> p (n c)"), phi[:, 1, :], start=True, stop=True)
                mm.then_inc(S("pcv_full"), 1)
                pe.wait_ge(S("pcv_copied"), 1)
                for qt in range(2):
                    for h in range(NH):
                        g, n = h // 4, h % 4
                        a = (g % 2) * 64
                        mm = pe.matmul(PS[(6, 0)[g % 2]][:, h * 32:h * 32 + NC_P], qT[a:a + 64, (g // 2) * 4 + n, qt * P:(qt + 1) * P],
                                       kcT[a:a + 64, g // 2, 0:NC_P], start=True, stop=True)
                    mm.then_inc(S("pcs_full"), 1)
                    pe.wait_ge(S("pc_ready"), qt + 1)
                    for g in range(4):
                        tr = nc.tensor.transpose(PS[7][:, g * P:(g + 1) * P], Pc[:, 4 * g:4 * g + 4, :].rearrange("p h c -> p (h c)"), ident)
                    tr.then_inc(S("pct_full"), 1)
                    pe.wait_ge(S("pct_copied"), qt + 1)
                    if qt:
                        pe.wait_ge(S("pco_done"), qt)
                    for g in range(4):
                        mm = pe.matmul(PS[4 + g // 2][:, (g % 2) * 256:(g % 2 + 1) * 256], PcT[:, g * P:(g + 1) * P],
                                       Vbd[:, g].rearrange("p n d -> p (n d)"), start=True, stop=True)
                    mm.then_inc(S("pco_full"), 1)
                pe.wait_ge(S("pco_done"), 2)
                for n in range(NW + 2):
                    if n < NW:
                        qt, br, g = work[n]
                        KE = P * (qt + 1)
                        if n >= 2:
                            pe.wait_ge(S("s_read"), n - 1)
                        a = (g % 2) * 64
                        for h in range(4):
                            mm = pe.matmul(PS[2 * (n % 2) + h // 2][:, (h % 2) * 256:(h % 2) * 256 + KE],
                                           qT[a:a + 64, (g // 2) * 4 + h, qt * P:(qt + 1) * P],
                                           kvT[a:a + 64, 4 + 4 * br + g // 2, 0:KE], start=True, stop=True)
                        mm.then_inc(S("s_full"), 1)
                    if 1 <= n <= NW:
                        m = n - 1
                        qt = work[m][0]
                        pe.wait_ge(S("p_ready"), m + 1)
                        if m:
                            pe.wait_ge(S("pt_copied"), m)
                        for kb in range(qt + 1):
                            for h in range(4):
                                tr = nc.tensor.transpose(PS[4 + kb][:, h * P:(h + 1) * P], Sb[m % 2][:, h, kb * P:(kb + 1) * P], ident)
                        tr.then_inc(S("pt_full"), 1)
                    if n >= 2:
                        m = n - 2
                        qt, br, g = work[m]
                        pe.wait_ge(S("pt_copied"), m + 1)
                        if m >= 2:
                            pe.wait_ge(S("o_done"), m - 1)
                        for h in range(4):
                            for kb in range(qt + 1):
                                mm = pe.matmul(PS[6 + m % 2][:, h * 64:(h + 1) * 64], PTs[m % 2][:, kb, h, :],
                                               kvp[:, kb, (768 if br == 0 else 1280) + g * 64:(768 if br == 0 else 1280) + (g + 1) * 64],
                                               start=kb == 0, stop=kb == qt)
                        mm.then_inc(S("o_full"), 1)
                pe.wait_ge(S("o_done"), NW)
                for n in range(4):
                    t, c = n // 2, n % 2
                    for j in range(4):
                        tr = nc.tensor.transpose(PS[n][:, j * P:(j + 1) * P],
                                                 oacc[:, t, 2 * (4 * c + j):2 * (4 * c + j) + 2, :].rearrange("p h d -> p (h d)"), ident)
                    tr.then_inc(S("ot_full"), 1)

            @block.vector
            def _(dve):
                V = nc.vector
                order = [0]

                def link(ins):
                    order[0] += 1
                    ins.then_inc(S("p_order"), 1)
                    dve.wait_ge(S("p_order"), order[0])

                dve.wait_ge(S("pool_landed"), 176)
                V.tensor_tensor(poolw[:, :, :, :], pcol.unsqueeze(3).broadcast_to([P, 2, 2, 8]),
                                C("submask").unsqueeze(1).unsqueeze(1).broadcast_to([P, 2, 2, 8]), ALU.mult).then_inc(S("poolw_ready"), 1)
                dve.wait_ge(S("pec_full"), 1)
                link(V.tensor_copy(pec[:, :], PS[5][:, 0:2]))
                dve.wait_ge(S("ppool_full"), 1)
                parts = PS[6][:, 0:P].rearrange("p (a m c) -> p a m c", a=4, m=2)
                for v in range(2):
                    V.tensor_scalar(pl[:, 2 * v:2 * v + 2, 0:NC_P], parts[:, 2 * v:2 * v + 2, 0, 0:NC_P], pec[:, v:v + 1], None, ALU.add).then_inc(S("p_order"), 1)
                order[0] += 2
                dve.wait_ge(S("p_order"), order[0])
                V.tensor_tensor(pl[:, :, 0:NC_P], pl[:, :, 0:NC_P], parts[:, :, 1, 1:NC_P + 1], ALU.add).then_inc(S("ppool_ready"), 1)
                dve.wait_ge(S("pgelu_ready"), 1)
                V.tensor_copy(Gr, Gp[:, 2:4, :].unsqueeze(2).broadcast_to([P, 2, 4, 32])).then_inc(S("pgr_ready"), 1)
                dve.wait_ge(S("pcv_full"), 1)
                V.tensor_copy(kcT[:, :, 0:NC_P], PS[7][:, 0:32].rearrange("p (g c) -> p g c", g=2)[:, :, 0:NC_P])
                for n in range(4):
                    ins = V.tensor_copy(Vbd[n * 32:(n + 1) * 32, :, n, :], PS[7][n * 32:(n + 1) * 32, 64:320].rearrange("p (g d) -> p g d", g=4))
                ins.then_inc(S("pcv_copied"), 1)
                for qt in range(2):
                    dve.wait_ge(S("pcs_full"), qt + 1)
                    bias = C("biascp")[:, qt * 240:(qt + 1) * 240].rearrange("p (h c) -> p h c", h=NH)
                    valid = C("validcp")[:, qt * NC_P:(qt + 1) * NC_P].unsqueeze(1).broadcast_to([P, NH, NC_P])
                    for par in range(2):
                        for g in (par, par + 2):
                            hs = slice(4 * g, 4 * g + 4)
                            ins = V.tensor_tensor(Sc[:, hs, :], PS[(6, 0)[par]][:, :].rearrange("p (h c) -> p h c", h=NH)[:, hs, 0:NC_P],
                                                  bias[:, hs, :], ALU.add)
                    link(ins)
                    link(V.tensor_reduce(cm, Sc, AX_X, ALU.max))
                    V.tensor_tensor(Sc, Sc, cm.unsqueeze(2).broadcast_to([P, NH, NC_P]), ALU.subtract).then_inc(S("pc_shifted"), 1)
                    dve.wait_ge(S("pc_exp"), qt + 1)
                    link(V.tensor_reduce(cs_, Sc, AX_X, ALU.add))
                    V.tensor_tensor(Pc[:, :, 0:NC_P], Sc, valid, ALU.mult).then_inc(S("pc_ready"), 1)
                    link(V.reciprocal(cs_, cs_))
                    if qt:
                        dve.wait_ge(S("pco_done"), qt)
                    link(V.tensor_tensor(cw, cs_, gN[:, qt, 0:NH], ALU.mult))
                    dve.wait_ge(S("pco_full"), qt + 1)
                    for b in range(2):
                        ins = V.tensor_tensor(oacc[:, qt, 8 * b:8 * b + 8, :], PS[4 + b][:, :].rearrange("p (h d) -> p h d", h=8),
                                              cw[:, 8 * b:8 * b + 8].unsqueeze(2).broadcast_to([P, 8, 64]), ALU.mult)
                    ins.then_inc(S("pco_done"), 1)
                dve.wait_ge(S("pco_done"), 2)
                for n in range(NW + 2):
                    if n < NW:
                        qt, br, g = work[n]
                        KE = P * (qt + 1)
                        dve.wait_ge(S("s_full"), n + 1)
                        if n >= 2:
                            dve.wait_ge(S("pt_full"), n - 1)
                        for h in range(4):
                            ins = V.scalar_tensor_tensor(out=Sb[n % 2][:, h, 0:KE], in0=C("distp")[:, SEQ - KE:SEQ], scalar=-slope(4 * g + h),
                                                         in1=PS[2 * (n % 2) + h // 2][:, (h % 2) * 256:(h % 2) * 256 + KE], op0=ALU.mult, op1=ALU.add)
                        ins.then_inc(S("s_read"), 1)
                        dve.wait_ge(S("s_read"), n + 1)
                        V.tensor_reduce(nmx[:, n, :], Sb[n % 2][:, :, 0:KE], AX_X, ALU.max, negate=True).then_inc(S("pmax_ready"), 1)
                    if n >= 2:
                        m = n - 2
                        qt, br, g = work[m]
                        dve.wait_ge(S("o_full"), m + 1)
                        dve.wait_ge(S("p_ready"), m + 1)
                        link(V.reciprocal(rs[:, m, :], rs[:, m, :]))
                        link(V.tensor_tensor(wgt[:, m, :], rs[:, m, :], gN[:, qt, (br + 1) * NH + 4 * g:(br + 1) * NH + 4 * g + 4], ALU.mult))
                        link(V.tensor_tensor(ot[m % 2], PS[6 + m % 2][:, 0:256].rearrange("p (h d) -> p h d", h=4),
                                             wgt[:, m, :].unsqueeze(2).broadcast_to([P, 4, 64]), ALU.mult))
                        V.tensor_tensor(oacc[:, qt, 4 * g:4 * g + 4, :], oacc[:, qt, 4 * g:4 * g + 4, :], ot[m % 2], ALU.add).then_inc(S("o_done"), 1)
                for n in range(4):
                    t, c = n // 2, n % 2
                    dve.wait_ge(S("ot_full"), n + 1)
                    V.tensor_copy(oT[:, 4 * c:4 * c + 4, t * P:(t + 1) * P], PS[n][:, :].rearrange("p (j q) -> p j q", j=4)).then_inc(S("ot_ready"), 1)
                dve.wait_ge(S("ot_ready"), 4)

        take = scratch()
        RP = 4
        pageA = [xT[:, :, :].rearrange("p k n -> p (k n)")[:, s * 768:(s + 1) * 768] for s in range(RP)]
        Vs = take(NPG * 256).rearrange("p (g n) -> p g n", g=NPG)
        KTs = take(2 * PAST).rearrange("p (g k) -> p g k", g=2)
        Ss = take(PAST + NQ)
        Sw = take(WIN + NQ)
        PT2 = [take(512) for _ in range(2)]
        wn = take(4 * 512).rearrange("p (t n) -> p t n", t=4)
        KwT = take(2 * WIN).rearrange("p (g k) -> p g k", g=2)
        kb = take(PAST + WIN + 2 * NQ)
        vnew = take(2 * 256).rearrange("p (a n) -> p a n", a=2)
        plS = take(4 * NC_S).rearrange("p (a c) -> p a c", a=4)
        kcs = take(2 * P).rearrange("p (g c) -> p g c", g=2)
        vcs = take(256)
        Pcs = take(NC_S)
        pcT = take(P)
        qst = take(2 * 64).rearrange("p (g r) -> p g r", g=2)
        kst = take(4 * NQ).rearrange("p (a q) -> p a q", a=4)
        gw = take(3)
        mx3, rs3, rw3 = (take(3) for _ in range(3))
        imp0, imp1, msk = (take(NBLK) for _ in range(3))
        top = take(16)
        waits = take(1)
        od = take(P).rearrange("p (u d) -> p u d", u=2)
        ptab = take(NB * NPG).bitcast(I32)

        with program() as block:
            @block.sync
            def _(sp):
                sp.dma_start(ptab[0:1, :], page_table.rearrange("b g -> (b g)").rearrange("(o n) -> o n", o=1)).then_inc(S("ptab_landed"), 16)
                sp.dma_start(kb, kbias).then_inc(S("kb_landed"), 16)
                sp.wait_ge(S("ptab_landed"), 16)
                n_pool = cache_kv.shape[1]
                rows = cache_kv[0].rearrange("n t a g d -> n t (a g d)")
                with sp.Fori(0, NB) as b:
                    def page(p):
                        return sp.value_load(ptab[0:1, bass.ds(b * NPG + p, 1)], min_val=0, max_val=n_pool - 1)

                    for p in range(NPG):
                        sp.wait_ge(S("page_used"), b * NPG + p + 1)
                        sp.dma_start(pageA[p % RP], rows[bass.ds(page(p), 1), :, 0:768].rearrange("o t n -> (o t) n")).then_inc(S(f"page_landed{p % RP}"), 16)
                    sp.wait_ge(S("so_full"), b + 1)
                    sp.dma_start(wn, state_win[0, bass.ds(b, 1)].rearrange("o (t p) a g d -> p (o t) (a g d)", p=P)).then_inc(S("wn_landed"), 16)
                    sp.dma_start(vnew[0:NQ, 0, :], kvr_sample[0, bass.ds(b, 1), :, 3].rearrange("o t g d -> (o t) (g d)")).then_inc(S("wn_landed"), 16)
                    sp.dma_start(vnew[0:NQ, 1, :], win_sample[0, bass.ds(b, 1), WIN - NQ:WIN, 1].rearrange("o t g d -> (o t) (g d)")).then_inc(S("wn_landed"), 16)
                    for p in range(NPG):
                        sp.dma_start(Vs[:, p, :], rows[bass.ds(page(p), 1), :, 768:1024].rearrange("o t n -> (o t) n")).then_inc(S("v_landed"), 16)

            @block.gpsimd
            def _(pool):
                with pool.Fori(0, NB) as b:
                    pool.wait_ge(S("so_done"), b + 1)
                    for g in range(2):
                        nc.gpsimd.tensor_tensor(qst[:, g, :].rearrange("p (h n q) -> p h n q", h=2, n=4),
                                                qs[:, 4 * g:4 * g + 4, bass.ds(b * NQ, NQ)].unsqueeze(1).broadcast_to([P, 2, 4, NQ]),
                                                C("half").unsqueeze(2).unsqueeze(3).broadcast_to([P, 2, 4, NQ]), ALU.mult)
                    nc.gpsimd.tensor_copy(kst, ks[:, :, bass.ds(b * NQ, NQ)])
                    nc.gpsimd.tensor_copy(gw, gS[:, :, bass.ds(b, 1)].rearrange("p r a -> p (r a)")).then_inc(S("q_staged"), 1)

            @block.tensor
            def _(pe):
                pe.sem_inc(S("page_used"), RP)
                pe.sem_inc(S("so_full"), 1)
                with pe.Fori(0, NB) as b:
                    pe.wait_ge(S("so_done"), b + 1)
                    for p in range(NPG):
                        pe.wait_ge(S(f"page_landed{p % RP}"), b * (16 * NPG // RP) + 16 * (p // RP + 1))
                        if p % 2 == 0:
                            pe.wait_ge(S("kt_copied"), b * 8 + (p // 2 + 1))
                        for g in range(2):
                            tr = nc.tensor.transpose(PS[6 + p // 2 % 2][:, (p % 2 * 2 + g) * P:(p % 2 * 2 + g + 1) * P],
                                                     pageA[p % RP][:, 512 + g * P:512 + (g + 1) * P], ident)
                        if p % 2:
                            tr.then_inc(S("kt_full"), 1)
                        for a in range(4):
                            mm = pe.matmul(PS[4 + a // 2][:, a % 2 * 256:a % 2 * 256 + 256].rearrange("p (m c) -> p m c", m=2)[:, :, p * 8:p * 8 + 8],
                                           pageA[p % RP][:, a * P:(a + 1) * P], poolw[:, a // 2].rearrange("p m n -> p (m n)"), start=True, stop=True)
                        mm.then_inc(S("page_used"), 1)
                    pe.wait_ge(S("sgelu_ready"), b + 1)
                    pe.wait_ge(S("kt_copied"), b * 8 + 10)
                    for g in range(2):
                        pe.matmul(PS[6][:, g * P:g * P + NC_S], phi[:, 0, :], plS[:, g, :], start=True, stop=True)
                    for g in range(2):
                        mm = pe.matmul(PS[6][0:NC_S, 256 + g * P:256 + (g + 1) * P], plS[:, 2 + g, :], phi[:, 1, :], start=True, stop=True)
                    mm.then_inc(S("cv_full"), 1)
                    pe.wait_ge(S("q_staged"), b + 1)
                    pe.wait_ge(S("cv_copied"), b + 1)
                    for g in range(2):
                        mm = pe.matmul(PS[7][g * 64:(g + 1) * 64, 0:NC_S], qst[:, g, :], kcs[:, g, 0:NC_S], start=True, stop=True)
                    mm.then_inc(S("cs_full"), 1)
                    for c in range(5):
                        if c >= 2:
                            pe.wait_ge(S("sel_read"), b * 5 + (c - 1))
                        for g in range(2):
                            if c < 4:
                                mm = pe.matmul(PS[4 + c % 2][g * 64:(g + 1) * 64, :], qst[:, g, :], KTs[:, g, c * 512:(c + 1) * 512], start=True, stop=True)
                            else:
                                mm = pe.matmul(PS[4][g * 64:(g + 1) * 64, 0:NQ], qst[:, g, :],
                                               kst[:, g, :], start=True, stop=True)
                        mm.then_inc(S("sel_full"), 1)
                    pe.wait_ge(S("cp_ready"), b + 1)
                    nc.tensor.transpose(PS[6][0:NC_S, 0:P], Pcs, ident).then_inc(S("pcT_full"), 1)
                    pe.wait_ge(S("pcT_copied"), b + 1)
                    pe.wait_ge(S("sel_read"), b * 5 + 4)
                    mm = pe.matmul(PS[5][:, 0:256], pcT[0:NC_S, :], vcs[0:NC_S, :], start=True, stop=True)
                    mm.then_inc(S("oc_full"), 1)
                    pe.matmul(PS[7][:, 0:NBLK], pcT[0:NC_S, :], C("overlap", NC_S), start=True, stop=True).then_inc(S("imp_full"), 1)
                    pe.wait_ge(S("imp_copied"), b + 1)
                    pe.matmul(PS[7][:, 64:64 + NBLK], C("same"), imp0, start=True, stop=True).then_inc(S("impsum_full"), 1)
                    pe.wait_ge(S("wn_landed"), b * 48 + 48)
                    pe.wait_ge(S("imp_read"), b + 1)
                    for t in range(4):
                        for g in range(2):
                            tr = nc.tensor.transpose(PS[6 + t // 2][:, (t % 2 * 2 + g) * P:(t % 2 * 2 + g + 1) * P],
                                                     wn[:, t, g * P:(g + 1) * P], ident)
                        if t % 2:
                            tr.then_inc(S("kw_full"), 1)
                    pe.wait_ge(S("oc_done"), b + 1)
                    pe.wait_ge(S("kw_copied"), b * 2 + 2)
                    for g in range(2):
                        mm = pe.matmul(PS[5][g * 64:(g + 1) * 64, :], qst[:, g, :], KwT[:, g, :], start=True, stop=True)
                    pe.wait_ge(S("sel_read"), b * 5 + 5)
                    for g in range(2):
                        mm = pe.matmul(PS[4][g * 64:(g + 1) * 64, 0:NQ], qst[:, g, :], kst[:, 2 + g, :], start=True, stop=True)
                    mm.then_inc(S("w_full"), 1)
                    pe.wait_ge(S("w_read"), b + 1)
                    pe.wait_ge(S("v_landed"), b * (16 * NPG) + 16 * NPG)
                    for n in range(7):
                        if n < 6:
                            pe.wait_ge(S("sp_ready"), b * 2 + (1 if n < 4 else 2))
                            pe.wait_ge(S("spt_copied"), b * 6 + (n + 1))
                            bank = PS[6 + n % 2]
                            if n < 5:
                                for j in range(4):
                                    src = Ss[:, (4 * n + j) * P:(4 * n + j + 1) * P] if n < 4 else Sw[:, j * P:(j + 1) * P]
                                    tr = nc.tensor.transpose(bank[:, j * P:(j + 1) * P], src, ident)
                            else:
                                nc.tensor.transpose(bank[0:NQ, 0:P], Ss[:, PAST:PAST + NQ], ident)
                                tr = nc.tensor.transpose(bank[0:NQ, P:2 * P], Sw[:, WIN:WIN + NQ], ident)
                            tr.then_inc(S("spt_full"), 1)
                        if n >= 1:
                            m = n - 1
                            pe.wait_ge(S("spt_copied"), b * 6 + (m + 3))
                            if m < 5:
                                for j in range(4):
                                    mm = pe.matmul(PS[5 if m < 4 else 4][:, 0:256], PT2[m % 2][:, j * P:(j + 1) * P],
                                                   Vs[:, 4 * m + j, :] if m < 4 else wn[:, j, 256:512],
                                                   start=j == 0 and m in (0, 4), stop=False)
                                mm.then_inc(S("pv_used"), 1)
                            else:
                                pe.matmul(PS[5][:, 0:256], PT2[m % 2][0:NQ, 0:P], vnew[0:NQ, 0, :], start=False, stop=True)
                                mm = pe.matmul(PS[4][:, 0:256], PT2[m % 2][0:NQ, P:2 * P], vnew[0:NQ, 1, :], start=False, stop=True)
                                mm.then_inc(S("so_full"), 1)
                    pe.wait_ge(S("od_ready"), b + 1)
                    nc.tensor.transpose(PS[6][:, 0:P], od.rearrange("p u d -> p (u d)"), ident).then_inc(S("odT_full"), 1)

            @block.scalar
            def _(act):
                act.sem_inc(S("kt_copied"), 2)
                act.sem_inc(S("spt_copied"), 2)
                act.sem_inc(S("so_done"), 1)
                with act.Fori(0, NB) as b:
                    for n in range(8):
                        act.wait_ge(S("kt_full"), b * 8 + (n + 1))
                        nc.scalar.copy(KTs[:, :, n * 256:(n + 1) * 256].rearrange("p g (t k) -> p t g k", t=2),
                                       PS[6 + n % 2][:, :].rearrange("p (t g k) -> p t g k", t=2, g=2)).then_inc(S("kt_copied"), 1)
                    act.wait_ge(S("pooled_ready"), b + 1)
                    nc.scalar.activation(plS, plS, ACT.Gelu_apprx_tanh).then_inc(S("sgelu_ready"), 1)
                    act.wait_ge(S("cv_full"), b + 1)
                    nc.scalar.copy(kcs[:, :, 0:NC_S], PS[6][:, 0:256].rearrange("p (g c) -> p g c", g=2)[:, :, 0:NC_S])
                    nc.scalar.copy(vcs[0:NC_S, :], PS[6][0:NC_S, 256:512]).then_inc(S("cv_copied"), 1)
                    act.wait_ge(S("cmax_ready"), b + 1)
                    nc.scalar.activation(Pcs, Pcs, ACT.Exp, bias=mx3[:, 0:1], accum_out=rs3[:, 0:1]).then_inc(S("cexp_ready"), 1)
                    act.wait_ge(S("pcT_full"), b + 1)
                    nc.scalar.copy(pcT[0:NC_S, :], PS[6][0:NC_S, 0:P]).then_inc(S("pcT_copied"), 1)
                    for n in range(2):
                        act.wait_ge(S("kw_full"), b * 2 + (n + 1))
                        nc.scalar.copy(KwT[:, :, n * 256:(n + 1) * 256].rearrange("p g (t k) -> p t g k", t=2),
                                       PS[6 + n][:, :].rearrange("p (t g k) -> p t g k", t=2, g=2)).then_inc(S("kw_copied"), 1)
                    act.wait_ge(S("smax_ready"), b * 2 + 1)
                    nc.scalar.activation(Ss, Ss, ACT.Exp, bias=mx3[:, 1:2], accum_out=rs3[:, 1:2]).then_inc(S("sp_ready"), 1)
                    act.wait_ge(S("smax_ready"), b * 2 + 2)
                    nc.scalar.activation(Sw, Sw, ACT.Exp, bias=mx3[:, 2:3], accum_out=rs3[:, 2:3]).then_inc(S("sp_ready"), 1)
                    for n in range(6):
                        act.wait_ge(S("spt_full"), b * 6 + (n + 1))
                        if n >= 2:
                            act.wait_ge(S("pv_used"), b * 5 + (n - 1))
                        if n < 5:
                            nc.scalar.copy(PT2[n % 2], PS[6 + n % 2][:, :]).then_inc(S("spt_copied"), 1)
                        else:
                            nc.scalar.copy(PT2[n % 2][0:NQ, 0:256], PS[6 + n % 2][0:NQ, 0:256]).then_inc(S("spt_copied"), 1)
                    act.wait_ge(S("odT_full"), b + 1)
                    for h in range(2):
                        ins = nc.scalar.copy(oT[h * 64:(h + 1) * 64, :, bass.ds(b * NQ + SEQ, NQ)],
                                             PS[6][h * 64:(h + 1) * 64, 0:P].rearrange("p (t h q) -> p t h q", h=2, q=NQ)[:, :, h, :])
                    ins.then_inc(S("so_done"), 1)

            @block.vector
            def _(dve):
                V = nc.vector
                dve.wait_ge(S("kb_landed"), 16)
                NL = 15
                with dve.Fori(0, NB) as b:
                    order = [0]

                    def link(ins):
                        order[0] += 1
                        ins.then_inc(S("s_order"), 1)
                        dve.wait_ge(S("s_order"), b * NL + order[0])

                    dve.wait_ge(S("page_used"), b * NPG + NPG + RP)
                    for v in range(2):
                        parts = PS[4 + v][:, :].rearrange("p (g m c) -> p g m c", g=2, m=2)
                        link(V.tensor_scalar(plS[:, 2 * v:2 * v + 2, :], parts[:, :, 0, 0:NC_S], pec[:, v:v + 1], None, ALU.add))
                        ins = V.tensor_tensor(plS[:, 2 * v:2 * v + 2, :], plS[:, 2 * v:2 * v + 2, :], parts[:, :, 1, 1:NC_S + 1], ALU.add)
                    ins.then_inc(S("pooled_ready"), 1)
                    dve.wait_ge(S("cs_full"), b + 1)
                    link(V.tensor_tensor(Pcs, PS[7][:, 0:NC_S], C("biascs"), ALU.add))
                    V.tensor_reduce(mx3[:, 0:1], Pcs, AX_X, ALU.max, negate=True).then_inc(S("cmax_ready"), 1)
                    for c in range(5):
                        w = 512 if c < 4 else NQ
                        dve.wait_ge(S("sel_full"), b * 5 + (c + 1))
                        V.tensor_tensor(Ss[:, c * 512:c * 512 + w], PS[4 + c % 2][:, 0:w], kb[:, c * 512:c * 512 + w], ALU.add).then_inc(S("sel_read"), 1)
                        if c == 0:
                            dve.wait_ge(S("cexp_ready"), b + 1)
                            link(V.reciprocal(rs3[:, 0:1], rs3[:, 0:1]))
                            V.tensor_scalar(Pcs, Pcs, rs3[:, 0:1], None, ALU.mult).then_inc(S("cp_ready"), 1)
                    dve.wait_ge(S("imp_full"), b + 1)
                    V.tensor_copy(imp0, PS[7][:, 0:NBLK]).then_inc(S("imp_copied"), 1)
                    dve.wait_ge(S("oc_full"), b + 1)
                    for g in range(4):
                        r = slice(g * 32, (g + 1) * 32)
                        ins = V.tensor_scalar(od[r, 0, :], PS[5][r, g * 64:(g + 1) * 64], gw[r, 0:1], None, ALU.mult)
                    ins.then_inc(S("oc_done"), 1)
                    dve.wait_ge(S("impsum_full"), b + 1)
                    V.tensor_copy(imp1, PS[7][:, 64:64 + NBLK]).then_inc(S("imp_read"), 1)
                    dve.wait_ge(S("imp_read"), b + 1)
                    V.memset(imp1[:, 0:1], FORCED)
                    link(V.memset(imp1[:, NBLK - 2:NBLK], FORCED))
                    V.memset(waits, 0.0)
                    link(V.max(top[:, 0:8], imp1))
                    V.memset(waits, 0.0)
                    link(V.match_replace(imp0, top[:, 0:8], imp1, -BIG))
                    V.memset(waits, 0.0)
                    link(V.max(top[:, 8:16], imp0))
                    V.memset(waits, 0.0)
                    link(V.match_replace(imp1, top[:, 8:16], imp0, -BIG))
                    link(V.tensor_scalar(msk, imp1, -1.0, -BIG, ALU.is_gt, ALU.mult))
                    blocks = Ss[:, 0:PAST].rearrange("p (s k) -> p s k", k=64)
                    link(V.tensor_tensor(blocks, blocks, msk[:, 0:32].unsqueeze(2).broadcast_to([P, 32, 64]), ALU.add))
                    V.tensor_reduce(mx3[:, 1:2], Ss, AX_X, ALU.max, negate=True).then_inc(S("smax_ready"), 1)
                    dve.wait_ge(S("w_full"), b + 1)
                    V.tensor_tensor(Sw[:, 0:WIN], PS[5][:, :], kb[:, PAST + NQ:PAST + NQ + WIN], ALU.add)
                    V.tensor_tensor(Sw[:, WIN:WIN + NQ], PS[4][:, 0:NQ], kb[:, PAST + NQ + WIN:], ALU.add).then_inc(S("w_read"), 1)
                    dve.wait_ge(S("w_read"), b + 1)
                    V.tensor_reduce(mx3[:, 2:3], Sw, AX_X, ALU.max, negate=True).then_inc(S("smax_ready"), 1)
                    dve.wait_ge(S("sp_ready"), b * 2 + 2)
                    link(V.reciprocal(rs3[:, 1:3], rs3[:, 1:3]))
                    link(V.tensor_tensor(rw3[:, 1:3], rs3[:, 1:3], gw[:, 1:3], ALU.mult))
                    dve.wait_ge(S("so_full"), b + 2)
                    for br in range(2):
                        for g in range(4):
                            r = slice(g * 32, (g + 1) * 32)
                            ins = V.scalar_tensor_tensor(out=od[r, 0, :], in0=PS[5 - br][r, g * 64:(g + 1) * 64], scalar=rw3[r, 1 + br:2 + br],
                                                         in1=od[r, 0, :], op0=ALU.mult, op1=ALU.add)
                        link(ins)
                    V.tensor_copy(od[:, 1, :], od[:, 0, :]).then_inc(S("od_ready"), 1)
                    assert order[0] == NL, order[0]

        take = scratch()
        hid = take(FT * NT).rearrange("p (t n) -> p t n", t=FT)
        sgm = hid[:, 0:32, :]
        yT = take(KT * NT).rearrange("p (t n) -> p t n", t=KT)
        mT = yT
        sB = take(4 * NT).rearrange("p (t n) -> p t n", t=4)
        yrow = [take(1024) for _ in range(2)]
        outputs = [(y_prompt[0, 0:P], P), (y_prompt[0, P:SEQ], P), (y_sample.rearrange("b t d -> (b t) d"), TOK[2])]

        def norm_squares_after(act, nm, name):
            act.wait_ge(S(name), KT)
            norm_squares(act, nm, xT)

        def tile_of(buf, t):
            return buf[:, bass.ds(t, 1), :].rearrange("p a n -> p (a n)")

        with program() as block:
            @block.sync
            def _(sp):
                sp.dma_start(xT[:, :, :], x_dram).then_inc(S("x_back"), 16)
                for job in (job_mg, job_ao, job_glu, job_out, job_ffn, job_down):
                    stream(sp, job)
                for t, (dst, rows) in enumerate(outputs):
                    for c in range(2):
                        sp.wait_ge(S("y_copied_out"), 4 * t + 2 * c + 2)
                        sp.dma_start(dst[:, c * 1024:(c + 1) * 1024], yrow[c][0:rows, :]).then_inc(S(f"yrow_stored{c}"), 16)
                for c in range(2):
                    sp.wait_ge(S(f"yrow_stored{c}"), 48)

            @block.tensor
            def _(pe):
                products(pe, job_mg, hT)
                products(pe, job_ao, oT)
                products(pe, job_glu, ysT)
                pe.wait_ge(S("m_ready"), 16 + 2)
                products(pe, job_out, mT)
                norm_sum(pe, norm2)
                pe.wait_ge(S("h2_ready"), KT)
                products(pe, job_ffn, hT)
                pe.wait_ge(S("hid_ready"), FT + 2)
                products(pe, job_down, hid)
                norm_sum(pe, norm3)
                pe.wait_ge(S("y_ready"), KT)
                for n in range(12):
                    t, c = n // 4, n % 4
                    if n >= 2:
                        pe.wait_ge(S("y_copied_out"), n - 1)
                    for j in range(4):
                        tr = nc.tensor.transpose(PS[4 + n % 2][0:TOK[t], j * P:(j + 1) * P], yT[:, 4 * c + j, t * P:t * P + TOK[t]], ident)
                    tr.then_inc(S("y_turned"), 1)

            @block.scalar
            def _(act):
                act.sem_inc(S("sb_used"), 2)
                act.sem_inc(S("hid_ready"), 2)
                with act.Fori(0, job_mg.n) as i:
                    for b in range(4):
                        full(act, job_mg, b, i)
                        nc.scalar.activation(sgm[:, bass.ds(i * 4 + b, 1), :].rearrange("p a n -> p (a n)"), PS[b][:, 0:NT], ACT.Sigmoid)\
                            .then_inc(S(f"bank_free{b}"), 1)
                with act.Fori(0, job_glu.n) as i:
                    for j in range(2):
                        full(act, job_glu, 2 + j, i)
                        act.wait_ge(S("sb_used"), i * 2 + (j + 1))
                        nc.scalar.activation(sB[:, j, :], PS[2 + j][:, 0:NT], ACT.Sigmoid).then_inc(S(f"bank_free{2 + j}"), 1)
                norm_squares_after(act, norm2, "x2_ready")
                norm_root(act, norm2)
                with act.Fori(0, job_ffn.n) as i:
                    for j in range(2):
                        full(act, job_ffn, j, i)
                        act.wait_ge(S("hid_ready"), i * 2 + (j + 1))
                        nc.scalar.activation(sB[:, j, :], PS[j][:, 0:NT], ACT.Silu).then_inc(S(f"bank_free{j}"), 1)
                norm_squares_after(act, norm3, "x3_ready")
                norm_root(act, norm3)

            @block.vector
            def _(dve):
                V = nc.vector
                dve.wait_ge(S("bank_free3"), job_mg.base["bank_free3"] + 8 + 1)
                with dve.Fori(0, job_ao.n) as i:
                    for b in range(4):
                        full(dve, job_ao, b, i)
                        V.tensor_tensor(tile_of(mT, i * 4 + b), PS[b][:, 0:NT], tile_of(sgm, i * 4 + b), ALU.mult).then_inc(S(f"bank_free{b}"), 1)
                dve.sem_inc(S("m_ready"), 2)
                with dve.Fori(0, job_glu.n) as i:
                    for j in range(2):
                        full(dve, job_glu, j, i)
                        dve.wait_ge(S(f"bank_free{2 + j}"), job_glu.value(f"bank_free{2 + j}", i, 2))
                        dve.wait_ge(S("m_ready"), i * 2 + (j + 1))
                        V.tensor_tensor(sB[:, 2 + j, :], PS[j][:, 0:NT], sB[:, j, :], ALU.mult).then_inc(S(f"bank_free{j}"), 1)
                        dve.wait_ge(S(f"bank_free{j}"), job_glu.value(f"bank_free{j}", i, 2))
                        V.tensor_tensor(sB[:, 2 + j, :], sB[:, 2 + j, :], tile_of(sgm, i * 2 + (16 + j)), ALU.mult).then_inc(S("sb_used"), 1)
                        dve.wait_ge(S("sb_used"), i * 2 + (j + 3))
                        V.tensor_tensor(tile_of(mT, i * 2 + j), tile_of(mT, i * 2 + j), sB[:, 2 + j, :], ALU.add).then_inc(S("m_ready"), 1)
                dve.wait_ge(S("x_back"), 16)
                with dve.Fori(0, job_out.n) as i:
                    for b in range(4):
                        full(dve, job_out, b, i)
                        V.tensor_tensor(tile_of(xT, i * 4 + b), tile_of(xT, i * 4 + b), PS[b][:, 0:NT], ALU.add).then_inc(S(f"bank_free{b}"), 1)
                dve.wait_ge(S("bank_free3"), job_out.base["bank_free3"] + 4 + 1)
                dve.sem_inc(S("x2_ready"), KT)
                norm_scale(dve, norm2, xT, hT, 1, "h2_ready")
                with dve.Fori(0, job_ffn.n) as i:
                    for j in range(2):
                        full(dve, job_ffn, 2 + j, i)
                        dve.wait_ge(S(f"bank_free{j}"), job_ffn.value(f"bank_free{j}", i, 2))
                        V.tensor_tensor(tile_of(hid, i * 2 + j), PS[2 + j][:, 0:NT], sB[:, j, :], ALU.mult).then_inc(S("hid_ready"), 1)
                        dve.wait_ge(S("hid_ready"), i * 2 + (j + 3))
                        dve.sem_inc(S(f"bank_free{2 + j}"), 1)
                with dve.Fori(0, job_down.n) as i:
                    for j in range(2):
                        full(dve, job_down, j, i)
                        V.tensor_tensor(tile_of(xT, i * 2 + j), tile_of(xT, i * 2 + j), PS[j][:, 0:NT], ALU.add).then_inc(S(f"bank_free{j}"), 1)
                dve.wait_ge(S("bank_free1"), job_down.base["bank_free1"] + 8 + 1)
                dve.sem_inc(S("x3_ready"), KT)
                norm_scale(dve, norm3, xT, yT, 2, "y_ready")
                for n in range(12):
                    t, c = n // 4, n % 4
                    dve.wait_ge(S("y_turned"), n + 1)
                    if t:
                        dve.wait_ge(S(f"yrow_stored{c // 2}"), 16 * t)
                    V.tensor_copy(yrow[c // 2][0:TOK[t], (c % 2) * 512:(c % 2 + 1) * 512], PS[4 + n % 2][0:TOK[t], :]).then_inc(S("y_copied_out"), 1)


_INS = ["x_prompt", "x_sample", "cache_kv", "state_win", "state_ssm_re", "state_ssm_im", "page_table", "g_mix", "w_in",
        "w_cmp_pe", "w_cmp_pool", "w_cmp_phi", "w_attn_out", "ssm_lam_re", "ssm_lam_im", "ssm_log_dt", "ssm_b_re",
        "ssm_b_im", "ssm_c_re", "ssm_c_im", "ssm_d", "w_glu", "w_out", "g_ffn", "w_gate", "w_up", "w_down", "g_final"]
_MATRICES = {"w_in", "w_attn_out", "w_glu", "w_out", "w_gate", "w_up", "w_down"}
_OUTS = [(1, SEQ, DM), (NB, NQ, DM), (1, 1, SEQ, 4, NKV, HD), (1, 1, SEQ, 2, NKV, HD), (1, 1, NG, NS), (1, 1, NG, NS),
         (1, NB, NQ, 4, NKV, HD), (1, NB, WIN, 2, NKV, HD), (1, NB, NG, NS), (1, NB, NG, NS)]


def kernel(**inputs):
    import concourse.bacc as _bacc
    from concourse.bass_utils import run_bass_kernel_spmd as _run

    nc = _bacc.Bacc("TRN2", target_bir_lowering=False, num_devices=1)
    arrays, ins, outs = {}, [], []
    given = {name: np.ascontiguousarray(inputs[name]) for name in _INS}
    given["small_constants"] = small_constants()[0]
    given["key_biases"] = key_biases()
    for name, a in given.items():
        arrays[f"in_{name}_dram"] = a
        ap = nc.dram_tensor(f"in_{name}_dram", a.shape, mybir.dt.from_np(a.dtype), kind="ExternalInput").ap()
        ins.append(ap[0] if name in _MATRICES else ap)
    for i, shape in enumerate(_OUTS):
        outs.append(nc.dram_tensor(f"out_{i}_dram", shape, F32, kind="ExternalOutput").ap())
    build(nc, ins, outs)
    r = _run(nc, [arrays], core_ids=[0])
    return tuple(r.results[0][f"out_{i}_dram"] for i in range(len(_OUTS)))
```

```python
from contextlib import ExitStack, contextmanager

import numpy as np
import concourse.bass as bass
from concourse import mybir

F32 = mybir.dt.float32
F32R = mybir.dt.float32r
I32 = mybir.dt.int32
ALU = mybir.AluOpType
ACT = mybir.ActivationFunctionType
AX_X = mybir.AxisListType.X

P = 128
DM = 2048
SEQ = 256
NB, NQ = 8, 8
NT = SEQ + NB * NQ
KT = DM // P
NH, HD, NKV, GRP = 16, 64, 4, 4
PAST, PAGE = 2048, 128
NPG = PAST // PAGE
WIN = 512
NG, NS, CH = 64, 64, 16
SSMW = NG * CH
DFF = 5632
FT = DFF // P
L = 8
NCH = NT // L
NPC = SEQ // L
GH = NG // 2
HGH = GH // 2
EPS = 1e-6
BIG = 1e30
FORCED = 1e4
NC_P = 15
NC_S = 127
NBLK = 33
SC = 0.125
C_Q, C_KV, C_GT, C_U, C_MG = 0, 1024, 2560, 2608, 3632
TWO_PI_HI = 6.28125
TWO_PI_LO = float(np.float32(2 * np.pi - 6.28125))
MAGIC = 12582912.0


def slope(h):
    return float(2.0 ** (-8.0 * (h + 1) / NH))


def small_constants():
    r = np.arange(P)
    parts = {}
    parts["ident"] = np.eye(P)
    parts["same"] = ((r[:, None] // 32 == r[None, :] // 32) & (r[:, None] % 8 == r[None, :] % 8))
    k = np.arange(SEQ)
    d = 128 + r[:, None] - k[None, :]
    parts["half"] = r[:, None] // 64 == np.arange(2)[None, :]
    parts["distp"] = np.where(d >= 0, d, BIG)
    end = np.arange(NC_P) * 16 + 31
    bias, valid = [], []
    for qt in range(2):
        q = qt * 128 + r
        dist = q[:, None] - end[None, :]
        ok = dist >= 0
        valid.append(ok)
        for h in range(NH):
            bias.append(np.where(ok, -np.float32(slope(h)) * dist, -BIG))
    parts["biascp"] = np.concatenate(bias, 1)
    parts["validcp"] = np.concatenate(valid, 1)
    c = np.arange(P) * 16
    s = np.arange(NBLK) * 64
    parts["overlap"] = (c[:, None] < s[None, :] + 64) & (c[:, None] + 31 >= s[None, :])
    m = np.zeros((P, 3, P))
    for br in range(3):
        for h in range(NH):
            m[br * NH + h, br, h * 8:h * 8 + 8] = 1
    parts["gatesel"] = m.reshape(P, -1)
    parts["qmask"] = r[:, None] % 8 == np.arange(8)[None, :]
    parts["submask"] = r[:, None] // 16 == np.arange(8)[None, :]
    parts["chandiag"] = r[:, None] % 16 == np.arange(16)[None, :]
    h, q = r // 8, r % 8
    sl = np.array([slope(x) for x in h], np.float32)[:, None]
    parts["biascs"] = -sl * (2048 + q[:, None] - (np.arange(NC_S) * 16 + 31)[None, :]).astype(np.float32)
    at, cols = {}, 0
    for name, a in parts.items():
        at[name] = (cols, cols + a.shape[1])
        cols += a.shape[1]
    return np.concatenate([np.asarray(a, np.float32) for a in parts.values()], 1), at


def key_biases():
    r = np.arange(P)
    q = r % 8
    sl = np.array([slope(x) for x in r // 8], np.float32)[:, None]
    d = 2048 + q[:, None] - np.arange(PAST + NQ)[None, :]
    sel = np.where(d >= 0, -sl * d.astype(np.float32), -BIG)
    d = 512 + q[:, None] - np.arange(WIN + NQ)[None, :]
    win = np.where((d >= 0) & (d < WIN), -sl * d.astype(np.float32), -BIG)
    return np.concatenate([sel, win], 1).astype(np.float32)


_, CAT = small_constants()
CW = max(b for _, b in CAT.values())


def build(nc, ins, outs):
    (x_prompt, x_sample, cache_kv, state_win, h0_re, h0_im, page_table, g_mix, w_in, w_pe, w_pool, w_phi,
     w_ao, lam_re, lam_im, log_dt, b_re, b_im, c_re, c_im, ssm_d, w_glu, w_out, g_ffn, w_gate, w_up,
     w_down, g_final, consts, kbias) = ins
    (y_prompt, y_sample, kvr_prompt, win_prompt, sre_prompt, sim_prompt, kvr_sample, win_sample,
     sre_sample, sim_sample) = outs
    with ExitStack() as ctx:
        def sb(name, shape, dt=F32):
            return ctx.enter_context(nc.sbuf_tensor(name, shape, dt))

        sems, blocks = {}, [0]

        lasting = ("raw_landed", "hi_ready", "split_ready", "tile_full", "bank_free", "square_", "mean_ready", "root_ready", "rstd_ready",
                   "stored", "y_stored", "x_spilled", "sg_stored")
        def S(name):
            if name not in sems:
                sems[name] = nc.alloc_semaphore(name if name.startswith(lasting) else f"{name}_{blocks[0]}")
            return sems[name]

        @contextmanager
        def program():
            with nc.Block() as block:
                yield block
            own = [n for n in sems if not n.startswith(lasting)]
            nc.clear_and_free_semaphores([sems.pop(n) for n in own])
            nc.all_engine_barrier()
            blocks[0] += 1

        PS = [ctx.enter_context(nc.psum_tensor(f"bank{i}", [P, 512], F32)) for i in range(8)]
        ctx.enter_context(nc.allow_non_contiguous_dma(reason="small parameter tables"))

        actr = sb("actr", [P, 2, KT, NT], F32R)
        cst = sb("cst", [P, CW])
        ones = sb("ones", [P, P])
        xT = sb("xT", [P, KT, NT])
        oT = sb("oT", [P, 8, NT])
        ysT = sb("ysT", [P, 8, NT])
        gcol = sb("gcol", [P, 48])
        gN = sb("gN", [P, 2, 48])
        gS = sb("gS", [P, 3, NB])
        poolw = sb("poolw", [P, 2, 2, 8])
        pec = sb("pec", [P, 2])
        phi = sb("phi", [P, 2, P])
        qs = sb("qs", [P, 8, NB * NQ])
        ks = sb("ks", [P, 4, NB * NQ])
        rstd = sb("rstd", [P, NT])
        sq = sb("sq", [P, 2, NT])
        kept = ctx.enter_context(ExitStack())
        raw, w_hi, w_lo = [], [], []
        place = {}

        def open_weights(stack, name):
            for s in range(2):
                for slots, kind, dt in ((raw, "raw", F32), (w_hi, "hi", F32R), (w_lo, "lo", F32R)):
                    slots[s:s + 1] = [stack.enter_context(nc.sbuf_tensor(f"{name}_{kind}{s}", [P, KT * P], dt))]

        def open_arena(stack, name):
            left = nc.sbuf_bytes_remaining
            size = (left() if callable(left) else left) // 4 - 16
            place["size"] = size; print(name, size)
            place["arena"] = stack.enter_context(nc.sbuf_tensor(name, [P, size], F32))

        def C(name, rows=P):
            a, b = CAT[name]
            return cst[0:rows, a:b]

        def scratch(region=None, size=None):
            if region is None:
                region, size = place["arena"][:, :], place["size"]
            at = [0]

            def take(width):
                a = at[0]
                at[0] += width
                assert at[0] <= size, at[0]
                return region[:, a:a + width]
            return take

        ident = C("ident")
        u_dram = nc.dram_tensor("u_scratch", [NT, SSMW], F32).ap()
        x_dram = nc.dram_tensor("x_scratch", [P, KT, NT], F32).ap()
        y_dram = nc.dram_tensor("y_scratch", [NT, SSMW], F32).ap()

        steps_before = [0]
        dmas_before = [0]

        class Job:
            def __init__(self, n, kt, columns, dmas=1, joined=False):
                self.n, self.kt, self.columns, self.dmas, self.joined = n, kt, columns, dmas, joined
                self.base, self.landed = steps_before[0], dmas_before[0]
                steps_before[0] += n
                dmas_before[0] += n * dmas * 16

        def load_tile(eng, job, i, s, slot_queue=None):
            eng.wait_ge(S(f"split_ready{s}"), i + (job.base + 1))
            slot = raw[s][:, 0:job.kt * P].rearrange("p (k c) -> p k c", k=job.kt)
            views = job.columns(i, s)
            w = P // len(views)
            for n, v in enumerate(views):
                eng.dma_start(slot[:, :, n * w:(n + 1) * w], v.rearrange("(k p) c -> p k c", p=P)).then_inc(S(f"raw_landed{s}"), 16)

        def stream(sp, job):
            with sp.Fori(0, job.n) as i:
                for s in range(2):
                    load_tile(sp, job, i, s)

        def round_tile(act, job, i, s):
            act.wait_ge(S(f"raw_landed{s}"), i * (16 * job.dmas) + (job.landed + 16 * job.dmas))
            act.wait_ge(S(f"tile_full{s}"), i + (job.base + 1))
            nc.scalar.copy(w_hi[s][:, 0:job.kt * P], raw[s][:, 0:job.kt * P]).then_inc(S(f"hi_ready{s}"), 1)

        def rest_tile(dve, job, i, s):
            dve.wait_ge(S(f"hi_ready{s}"), i + (job.base + 1))
            nc.vector.tensor_tensor(w_lo[s][:, 0:job.kt * P], raw[s][:, 0:job.kt * P], w_hi[s][:, 0:job.kt * P].bitcast(F32),
                                    ALU.subtract).then_inc(S(f"split_ready{s}"), 1)

        def multiply(pe, job, i, s, hi, lo, k0=0):
            pe.wait_ge(S(f"split_ready{s}"), i + (job.base + 2))
            if not (job.joined and s):
                pe.wait_ge(S(f"bank_free{s}"), i + (job.base + 1))
            bank = PS[0 if job.joined else s]
            first = not (job.joined and s)
            last = not (job.joined and not s)
            for k in range(job.kt):
                kk = k0 + k + (job.kt if job.joined and s else 0)
                for m, (w, x) in enumerate(((w_hi, hi), (w_hi, lo), (w_lo, hi))):
                    mm = pe.matmul(bank[:, 0:NT], w[s][:, k * P:(k + 1) * P], x[:, kk, :],
                                   start=first and k == 0 and m == 0, stop=last and k == job.kt - 1 and m == 2)
            mm.then_inc(S(f"tile_full{s}"), 1)

        def products(pe, job, hi, lo, k0=0):
            with pe.Fori(0, job.n) as i:
                for s in range(2):
                    multiply(pe, job, i, s, hi, lo, k0)

        def full(eng, job, i, s):
            eng.wait_ge(S(f"tile_full{s}"), i + (job.base + 2))

        def follow(eng, jobs, split, reads):
            def read(job, fn, i, s):
                if fn:
                    fn(i, s)

            split(eng, jobs[0], 0, 0)
            for n, (job, fn) in enumerate(zip(jobs, reads)):
                if job.n > 1:
                    with eng.Fori(0, job.n - 1) as i:
                        split(eng, job, i, 1)
                        read(job, fn, i, 0)
                        split(eng, job, i + 1, 0)
                        read(job, fn, i, 1)
                split(eng, job, job.n - 1, 1)
                read(job, fn, job.n - 1, 0)
                if n + 1 < len(jobs):
                    split(eng, jobs[n + 1], 0, 0)
                read(job, fn, job.n - 1, 1)

        def plain(w, col0=0):
            return lambda i, s: [w[:, bass.ds(i * 256 + (s * P + col0), P)]]

        def halves(i, s):
            return [w_in[s * 1024:(s + 1) * 1024, C_GT:C_GT + P]]

        FC, FK = 4, FT // 4

        def q_job_columns(gp):
            return lambda i, s: [w_in[:, bass.ds(i * 2 * HD + (8 * gp + 4 * half + s) * HD, HD)] for half in range(2)]

        job_q = [Job(2, KT, q_job_columns(gp), dmas=2) for gp in range(2)]
        job_kv = Job(6, KT, plain(w_in, C_KV))
        job_gt = Job(1, 8, halves, joined=True)
        job_u = Job(4, KT, plain(w_in, C_U))
        job_mg = Job(16, KT, plain(w_in, C_MG))
        job_ao = Job(8, 8, plain(w_ao))
        job_glu = Job(16, 8, lambda i, s: [w_glu[:, bass.ds(i * P + s * DM, P)]])
        job_out = Job(8, KT, plain(w_out))
        job_ffn, job_down = [], []
        for c in range(FC):
            job_ffn.append(Job(FK, KT, lambda i, s, c=c: [(w_gate, w_up)[s][:, bass.ds(i * P + c * FK * P, P)]]))
            job_down.append(Job(8, FK, lambda i, s, c=c: [w_down[c * FK * P:(c + 1) * FK * P, bass.ds(i * 256 + s * P, P)]]))

        norms = [0]

        class Norm:
            def __init__(self):
                self.n = norms[0]
                norms[0] += 1

        def norm_squares(act, nm, src):
            for k in range(KT):
                if nm.n * KT + k >= 2:
                    act.wait_ge(S("square_used"), nm.n * KT + k - 1)
                nc.scalar.activation(sq[:, k % 2, :], src[:, k, :], ACT.Square).then_inc(S("square_ready"), 1)

        def norm_sum(pe, nm):
            if nm.n:
                pe.wait_ge(S("mean_ready"), nm.n)
            for k in range(KT):
                pe.wait_ge(S("square_ready"), nm.n * KT + k + 1)
                mm = pe.matmul(PS[7][:, 0:NT], ones[:, :], sq[:, k % 2, :], start=k == 0, stop=k == KT - 1)
                mm.then_inc(S("square_used"), 1)

        def norm_rstd(dve, nm):
            dve.wait_ge(S("square_used"), (nm.n + 1) * KT)
            nc.vector.tensor_scalar(rstd[:, :], PS[7][:, 0:NT], 1.0 / DM, EPS, ALU.mult, ALU.add).then_inc(S("mean_ready"), 1)
            dve.wait_ge(S("root_ready"), nm.n + 1)
            nc.vector.reciprocal(rstd[:, :], rstd[:, :]).then_inc(S("rstd_ready"), 1)
            dve.wait_ge(S("rstd_ready"), nm.n + 1)

        def norm_scale(dve, src, dst, gc, k, done):
            nc.vector.scalar_tensor_tensor(out=dst, in0=src[:, k, :], scalar=gcol[:, gc * KT + k:gc * KT + k + 1],
                                           in1=rstd[:, :], op0=ALU.mult, op1=ALU.mult).then_inc(S(done), 1)

        def norm_split_rest(dve, src, gc):
            norm_scale(dve, src, sq[:, 0, :], gc, 0, "normed")
            for k in range(KT):
                if k + 1 < KT:
                    if k:
                        dve.wait_ge(S("h_ready"), k)
                    norm_scale(dve, src, sq[:, (k + 1) % 2, :], gc, k + 1, "normed")
                dve.wait_ge(S("h_rounded"), k + 1)
                nc.vector.tensor_tensor(actr[:, 1, k, :], sq[:, k % 2, :], actr[:, 0, k, :].bitcast(F32), ALU.subtract).then_inc(S("h_ready"), 1)

        def norm_split_round(act):
            for k in range(KT):
                act.wait_ge(S("normed"), k + 1)
                nc.scalar.copy(actr[:, 0, k, :], sq[:, k % 2, :]).then_inc(S("h_rounded"), 1)

        def norm_root(act, nm):
            act.wait_ge(S("mean_ready"), nm.n + 1)
            nc.scalar.activation(rstd[:, :], rstd[:, :], ACT.Sqrt).then_inc(S("root_ready"), 1)

        norm1, norm2, norm3 = Norm(), Norm(), Norm()

        kvT = kept.enter_context(nc.sbuf_tensor("kvT", [P, 12, NT], F32))
        qT = kept.enter_context(nc.sbuf_tensor("qT", [P, 8, NT], F32))
        uT = oT
        phase = ExitStack()
        open_weights(phase, "w1")
        open_arena(phase, "arena1")
        take = scratch()
        xrow = take(3 * DM).rearrange("p (t n) -> p t n", t=3)
        gT = take(NT)
        grow = take(P)
        TOK = [P, P, NT - 2 * P]

        with program() as block:
            @block.sync
            def _(sp):
                sp.dma_start(xrow[:, 0, :], x_prompt[0, 0:P, :]).then_inc(S("x_landed"), 16)
                sp.dma_start(xrow[:, 1, :], x_prompt[0, P:SEQ, :]).then_inc(S("x_landed"), 16)
                sp.dma_start(xrow[0:TOK[2], 2, :], x_sample.rearrange("b t d -> (b t) d")).then_inc(S("x_landed"), 16)
                for job in (*job_q, job_kv, job_gt, job_u):
                    stream(sp, job)

            @block.gpsimd
            def _(pool):
                nc.gpsimd.memset(ones[:, :], 1.0).then_inc(S("ones_ready"), 1)

            @block.tensor
            def _(pe):
                pe.wait_ge(S("consts_landed"), 16)
                pe.wait_ge(S("grow_landed"), 48)
                nc.tensor.transpose(PS[6][:, 0:48], grow[0:48, :], ident[0:48, 0:48]).then_inc(S("gcol_full"), 1)
                pe.wait_ge(S("x_landed"), 48)
                n = 0
                for t in range(3):
                    for c in range(KT // 4):
                        if n >= 2:
                            pe.wait_ge(S("xt_copied"), n - 1)
                        for j in range(4):
                            k = 4 * c + j
                            tr = nc.tensor.transpose(PS[4 + n % 2][:, j * P:j * P + TOK[t]],
                                                     xrow[0:TOK[t], t, k * P:(k + 1) * P], ident[0:TOK[t], 0:TOK[t]])
                        tr.then_inc(S("xt_full"), 1)
                        n += 1
                pe.wait_ge(S("ones_ready"), 1)
                norm_sum(pe, norm1)
                pe.sem_inc(S("tile_full0"), 1)
                pe.sem_inc(S("tile_full1"), 1)
                pe.wait_ge(S("h_ready"), KT)
                for job in (*job_q, job_kv, job_gt, job_u):
                    products(pe, job, actr[:, 0], actr[:, 1])
                pe.wait_ge(S("gate_ready"), 1)
                for t in range(2):
                    tr = nc.tensor.transpose(PS[4][:, t * 48:(t + 1) * 48], gT[0:48, t * P:(t + 1) * P], ident[0:48, 0:48])
                tr.then_inc(S("gn_full"), 1)
                for br in range(3):
                    sel = C("gatesel", 48)[:, br * P:(br + 1) * P]
                    mm = pe.matmul(PS[5][:, br * 64:(br + 1) * 64], sel, gT[0:48, SEQ:NT], start=True, stop=True)
                mm.then_inc(S("gs_full"), 1)

            @block.scalar
            def _(act):
                act.dma_start(cst[:, :], consts).then_inc(S("consts_landed"), 16)
                for n, g in enumerate((g_mix, g_ffn, g_final)):
                    src = g if n == 2 else g[0]
                    act.dma_start(grow[n * KT:(n + 1) * KT, :], src.rearrange("(k p) -> k p", p=P)).then_inc(S("grow_landed"), 16)
                for b in range(2):
                    act.sem_inc(S(f"bank_free{b}"), 1)
                act.wait_ge(S("xt_copied"), 12)
                norm_squares(act, norm1, xT)
                norm_root(act, norm1)
                norm_split_round(act)

                def keep_in(dst, t0, scale):
                    def read(i, s):
                        full(act, read.job, i, s)
                        nc.scalar.activation(dst[:, bass.ds(i * 2 + (t0 + s), 1), :].rearrange("p a n -> p (a n)"), PS[s][:, 0:NT],
                                             ACT.Copy, scale=scale).then_inc(S(f"bank_free{s}"), 1)
                    return read

                def gates(i, s):
                    if s:
                        full(act, job_gt, i, s)
                        nc.scalar.activation(gT[0:48, :], PS[0][0:48, 0:NT], ACT.Sigmoid).then_inc(S("bank_free0"), 1)
                        act.wait_ge(S("bank_free0"), job_gt.base + 2)
                        act.sem_inc(S("gate_ready"), 1)
                        act.sem_inc(S("bank_free1"), 1)

                jobs = (*job_q, job_kv, job_gt, job_u)
                reads = (keep_in(qT, 0, SC), keep_in(qT, 4, SC), keep_in(kvT, 0, 1.0), gates, keep_in(uT, 0, 1.0))
                for job, read in zip(jobs, reads):
                    read.job = job
                follow(act, jobs, round_tile, reads)

            @block.vector
            def _(dve):
                dve.wait_ge(S("gcol_full"), 1)
                nc.vector.tensor_copy(gcol[:, :], PS[6][:, 0:48]).then_inc(S("gcol_copied"), 1)
                n = 0
                for t in range(3):
                    for c in range(KT // 4):
                        dve.wait_ge(S("xt_full"), n + 1)
                        nc.vector.tensor_copy(xT[:, 4 * c:4 * c + 4, t * P:t * P + TOK[t]],
                                              PS[4 + n % 2][:, :].rearrange("p (j n) -> p j n", j=4)[:, :, 0:TOK[t]])\
                            .then_inc(S("xt_copied"), 1)
                        n += 1
                norm_rstd(dve, norm1)
                norm_split_rest(dve, xT, 0)
                for s in range(2):
                    dve.sem_inc(S(f"split_ready{s}"), 1)
                jobs = (*job_q, job_kv, job_gt, job_u)
                follow(dve, jobs, rest_tile, (None,) * len(jobs))
                dve.wait_ge(S("gn_full"), 1)
                nc.vector.tensor_copy(gN[:, :, :], PS[4][:, 0:96].rearrange("p (t c) -> p t c", t=2)).then_inc(S("gn_ready"), 1)
                dve.wait_ge(S("gs_full"), 1)
                for br in range(3):
                    nc.vector.tensor_tensor(sq[:, 0, br * 64:(br + 1) * 64].rearrange("p (b q) -> p b q", q=NQ),
                                            PS[5][:, br * 64:(br + 1) * 64].rearrange("p (b q) -> p b q", q=NQ),
                                            C("qmask").unsqueeze(1).broadcast_to([P, NB, NQ]), ALU.mult)\
                        .then_inc(S("gs_masked"), 1)
                dve.wait_ge(S("gs_masked"), 3)
                nc.vector.tensor_reduce(gS[:, :, :], sq[:, 0, 0:192].rearrange("p (r b q) -> p r b q", r=3, q=NQ), AX_X, ALU.add)\
                    .then_inc(S("gs_ready"), 1)

        phase.close()
        open_arena(phase, "arena2")
        take = scratch()
        kvn = take(3 * 1536).rearrange("p (t n) -> p t n", t=3)
        un = take(3 * SSMW).rearrange("p (t n) -> p t n", t=3)
        turns = [(kvT, t, c, kvn) for t in range(3) for c in range(3)] + [(uT, t, c, un) for t in range(3) for c in range(2)]
        with program() as block:
            @block.tensor
            def _(pe):
                for n, (src, t, c, _) in enumerate(turns):
                    if n >= 4:
                        pe.wait_ge(S(("turned_dve", "turned_act")[n % 2]), n // 2 - 1)
                    for j in range(4):
                        tr = nc.tensor.transpose(PS[4 + n % 4][0:TOK[t], j * P:(j + 1) * P],
                                                 src[:, 4 * c + j, t * P:t * P + TOK[t]], ident)
                    tr.then_inc(S("turn_full"), 1)

            def copy_turns(eng, parity, copy, done):
                for n, (_, t, c, dst) in enumerate(turns):
                    if n % 2 == parity:
                        eng.wait_ge(S("turn_full"), n + 1)
                        copy(dst[0:TOK[t], t, c * 512:(c + 1) * 512], PS[4 + n % 4][0:TOK[t], :]).then_inc(S(done), 1)

            @block.vector
            def _(dve):
                copy_turns(dve, 0, nc.vector.tensor_copy, "turned_dve")

            @block.scalar
            def _(act):
                copy_turns(act, 1, nc.scalar.copy, "turned_act")

            @block.sync
            def _(sp):
                sp.wait_ge(S("turned_dve"), 5)
                sp.wait_ge(S("turned_act"), 4)
                for t in range(2):
                    sp.dma_start(kvr_prompt[0, 0, t * P:(t + 1) * P].rearrange("t a g d -> t (a g d)"),
                                 kvn[:, t, 0:1024]).then_inc(S("stored"), 16)
                    sp.dma_start(win_prompt[0, 0, t * P:(t + 1) * P].rearrange("t a g d -> t (a g d)"),
                                 kvn[:, t, 1024:1536]).then_inc(S("stored"), 16)
                sp.dma_start(kvr_sample[0].rearrange("b t a g d -> (b t) (a g d)"), kvn[0:64, 2, 0:1024]).then_inc(S("stored"), 16)
                for b in range(NB):
                    sp.dma_start(win_sample[0, b, WIN - NQ:WIN].rearrange("t a g d -> t (a g d)"),
                                 kvn[b * NQ:(b + 1) * NQ, 2, 1024:1536]).then_inc(S("stored"), 16)
                    sp.dma_start(win_sample[0, b, 0:WIN - NQ].rearrange("t a g d -> t (a g d)"),
                                 state_win[0, b, NQ:WIN].rearrange("t a g d -> t (a g d)")).then_inc(S("stored"), 16)
                sp.wait_ge(S("turned_dve"), 8)
                sp.wait_ge(S("turned_act"), 7)
                for t in range(3):
                    sp.dma_start(u_dram[t * P:t * P + TOK[t]], un[0:TOK[t], t, :]).then_inc(S("u_stored"), 16)
                sp.wait_ge(S("u_stored"), 48)
                sp.wait_ge(S("stored"), 21 * 16)

        PG, NPART = 8, GH // 8
        take = scratch()
        urows = take(L * PG * 32).rearrange("p (s c) -> p s c", s=L)
        Q = take(2 * PG * 9 * CH).rearrange("p (r g k c) -> p r g k c", r=2, g=PG, k=9)
        tq = take(2 * PG * 9 * CH)
        Tt = take(2 * PG * P).rearrange("p (h g n) -> p h g n", h=2, g=PG)
        Ga = take(PG * P).rearrange("p (g n) -> p g n", g=PG)
        UTa = take(PG * 80).rearrange("p (g n) -> p g n", g=PG)
        ea = take(NCH * 2 * PG).rearrange("p (c r g) -> p c r g", c=NCH, r=2)
        Ha = take(NCH * 2 * PG).rearrange("p (c r g) -> p c r g", c=NCH, r=2)
        Bb = take(2 * GH * CH).rearrange("p (r g c) -> p r g c", r=2, g=GH)
        Ct = take(2 * GH * CH).rearrange("p (r g c) -> p r g c", r=2, g=GH)
        PK = take(2 * 9 * GH).rearrange("p (r k g) -> p r k g", r=2, k=9)
        NPI = take(9 * GH).rearrange("p (k g) -> p k g", k=9)
        NPR = take(9 * GH).rearrange("p (k g) -> p k g", k=9)
        RK = take(2 * GH * L).rearrange("p (r g s) -> p r g s", r=2, g=GH)
        H0 = take(2 * NB * GH).rearrange("p (r b g) -> p r b g", r=2, b=NB)
        FinS = take(2 * NB * GH).rearrange("p (r b g) -> p r b g", r=2, b=NB)
        FinP = take(2 * GH).rearrange("p (r g) -> p r g", r=2)
        dcol = take(GH)
        dI = take(PG * CH).rearrange("p (g c) -> p g c", g=PG)
        ust = [take(256).rearrange("p (h s c) -> p h s c", h=2, s=L) for _ in range(2)]
        take_ys = scratch(ysT[:, :, :].rearrange("p k n -> p (k n)"), 8 * NT)
        stg_fin = take_ys(2 * 3 * P).rearrange("p (r t n) -> p r t n", r=2, t=3)
        EB = [take_ys(256).rearrange("p (r s c) -> p r s c", r=2, s=L) for _ in range(2)]
        tA = [take_ys(256).rearrange("p (r s c) -> p r s c", r=2, s=L) for _ in range(2)]
        tB = [take_ys(256).rearrange("p (r s c) -> p r s c", r=2, s=L) for _ in range(2)]
        stg = [take(336) for _ in range(2)]
        Bst = [take(64).rearrange("p (r h c) -> p r h c", r=2, h=2) for _ in range(2)]
        Hst = [take(160).rearrange("p (h r n) -> p h r n", h=2, r=2) for _ in range(2)]
        UTst = [take(80) for _ in range(2)]
        sc = take(3 * 2 * PG).rearrange("p (t r g) -> p t r g", t=3, r=2)
        par = ysT[:, :, :].rearrange("p k n -> p (k n)")
        Cn = par[:, 0:2048].rearrange("p (r t d s) -> p r t d s", r=2, t=8, d=2)
        h0n = oT[:, :, :].rearrange("p k n -> p (k n)")[:, 0:512].rearrange("p (r t n) -> p r t n", r=2, t=2)
        lamn = oT[:, :, :].rearrange("p k n -> p (k n)")[:, 512:896].rearrange("p (a n) -> p a n", a=3)
        ldn = oT[:, :, :].rearrange("p k n -> p (k n)")[:, 896:898]
        Bn = oT[:, :, :].rearrange("p k n -> p (k n)")[:, 1024:2048].rearrange("p (r g c) -> p r g c", r=2, g=GH)
        tp = oT[:, :, :].rearrange("p k n -> p (k n)")[:, 2048:2560].rearrange("p (t g) -> p t g", t=16)
        tb = tq[:, 0:1024].rearrange("p (t g c) -> p t g c", t=2, g=GH)

        with program() as block:
            @block.sync
            def _(sp):
                for r, c in enumerate((c_re, c_im)):
                    for d in range(2):
                        sp.dma_start(Cn[:, r, :, d, :], c[0].rearrange("(t g) c p -> (g c) t p", g=8)).then_inc(S("cn_landed"), 16)
                for r, h in enumerate((h0_re, h0_im)):
                    sp.dma_start(h0n[:, r, :, :], h[0].rearrange("b g p -> (b g p)").rearrange("(t a n) -> a t n", a=P, n=P))\
                        .then_inc(S("h0_landed"), 16)
                for part in range(NPART):
                    if part:
                        sp.wait_ge(S("y_stored"), 16 * part)
                    sp.dma_start(urows[0:NCH, :, :], u_dram.rearrange("(a s) c -> a s c", s=L)[:, :, part * PG * 32:(part + 1) * PG * 32])\
                        .then_inc(S("u_landed"), 16)
                    sp.wait_ge(S("g_diag"), part + 1)
                    sp.wait_ge(S("t_zero"), 1)
                    if part:
                        sp.wait_ge(S("y_copied"), PG * part + 2)
                    for s in range(L):
                        for h in range(2):
                            sp.dma_start(Tt[s * CH:(s + 1) * CH, h, :, s * CH:P], Ga[h * CH:(h + 1) * CH, :, 0:P - s * CH])\
                                .then_inc(S("t_landed"), 16)
                    sp.wait_ge(S("y_copied"), PG * (part + 1) + 2)
                    sp.dma_start(y_dram.rearrange("(a s) c -> a s c", s=L)[:, :, part * PG * 32:(part + 1) * PG * 32],
                                 urows[0:NCH, :, :]).then_inc(S("y_stored"), 16)
                for r, (op, os) in enumerate(((sre_prompt, sre_sample), (sim_prompt, sim_sample))):
                    sp.wait_ge(S("fin_copied"), r + 1)
                    for t in range(2):
                        sp.dma_start(os[0].rearrange("b g p -> (b g p)").rearrange("(t a n) -> t a n", a=P, n=P)[t],
                                     stg_fin[:, r, t, :]).then_inc(S("stored"), 16)
                    sp.dma_start(op[0, 0].rearrange("(g h) p -> g (h p)", h=2), stg_fin[0:GH, r, 2, :]).then_inc(S("stored"), 16)
                sp.wait_ge(S("stored"), (21 + 6) * 16)

            @block.gpsimd
            def _(pool):
                nc.gpsimd.memset(Tt, 0.0).then_inc(S("t_zero"), 1)
                pool.wait_ge(S("bbar_ready"), 1)
                for part in range(NPART):
                    pool.wait_ge(S("u_landed"), 16 * (part + 1))
                    with pool.Fori(0, PG // 2) as i:
                        for u in range(2):
                            n = part * PG + u
                            pool.wait_ge(S("turned"), i * 2 + n + 1)
                            pool.wait_ge(S("eg_full"), i * 2 + n + 1)
                            src = urows[0:NCH, :, bass.ds(i * 64 + u * 32, 32)].rearrange("p s (h c) -> p h s c", h=2)
                            nc.gpsimd.tensor_copy(ust[u][0:NCH], src)
                            nc.gpsimd.tensor_tensor(Bst[u], Bb[:, :, bass.ds(i * 2 + n, 1), :].broadcast_to([P, 2, 2, CH]),
                                                    C("half").unsqueeze(1).unsqueeze(3).broadcast_to([P, 2, 2, CH]), ALU.mult)\
                                .then_inc(S("u_staged"), 1)
                    pool.wait_ge(S("h_done"), part + 1)
                    with pool.Fori(0, PG // 2) as i:
                        for u in range(2):
                            n = part * PG + u
                            pool.wait_ge(S("y_full"), i * 2 + n + 1)
                            nc.gpsimd.tensor_copy(UTst[u], UTa[:, bass.ds(i * 2 + u, 1), :].rearrange("p a n -> p (a n)"))
                            nc.gpsimd.tensor_tensor(Hst[u], Ha[:, :, :, bass.ds(i * 2 + u, 1)].rearrange("p c r a -> p a r c").broadcast_to([P, 2, 2, NCH]),
                                                    C("half").unsqueeze(2).unsqueeze(3).broadcast_to([P, 2, 2, NCH]), ALU.mult)\
                                .then_inc(S("h_staged"), 1)

            @block.tensor
            def _(pe):
                for name, k in (("turned", 2), ("eg_full", 2), ("y_full", 2)):
                    pe.sem_inc(S(name), k)
                pe.wait_ge(S("ldt_rows"), 1)
                for a in range(3):
                    tr = nc.tensor.transpose(PS[0][:, a * GH:(a + 1) * GH], lamn[0:GH, a, :], ident[0:GH, 0:GH])
                tr.then_inc(S("lam_full"), 1)
                pe.wait_ge(S("cn_landed"), 64)
                for r in range(2):
                    for t in range(8):
                        tr = nc.tensor.transpose(PS[4 + 2 * r + t // 4][:, (t % 4) * P:(t % 4 + 1) * P],
                                                 Cn[:, r, t, :, :].rearrange("p d s -> p (d s)"), ident)
                tr.then_inc(S("ct_full"), 1)
                pe.wait_ge(S("h0_landed"), 32)
                for r in range(2):
                    for t in range(2):
                        tr = nc.tensor.transpose(PS[1][:, (2 * r + t) * P:(2 * r + t + 1) * P], h0n[:, r, t, :], ident)
                tr.then_inc(S("h0_full"), 1)
                pe.wait_ge(S("ct_ready"), 1)
                for part in range(NPART):
                    pe.wait_ge(S("q_ready"), part + 1)
                    with pe.Fori(0, PG // 2) as i:
                        for u in range(2):
                            n = part * PG + u
                            pe.wait_ge(S("u_staged"), i * 2 + n + 1)
                            pe.wait_ge(S("eb_ready"), i * 2 + n + 1)
                            for r in range(2):
                                nc.tensor.transpose(PS[4 + u][:, r * P:(r + 1) * P], EB[u][:, r].rearrange("p s c -> p (s c)"), ident)
                            for h in range(2):
                                tr = nc.tensor.transpose(PS[4 + u][:, 256 + h * NCH:256 + (h + 1) * NCH],
                                                         ust[u][0:NCH, h].rearrange("p s c -> p (s c)"), ident[0:NCH, 0:NCH])
                            tr.then_inc(S("turned"), 1)
                        for u in range(2):
                            n = part * PG + u
                            pe.wait_ge(S("eg_staged"), i * 2 + n + 1)
                            pe.wait_ge(S("e_copied"), i * 2 + n + 1)
                            pe.wait_ge(S("g_copied"), i * 2 + n + 1)
                            for h in range(2):
                                for r in range(2):
                                    pe.matmul(PS[6][h * 64:(h + 1) * 64, r * NCH:(r + 1) * NCH],
                                              stg[u][:, r * P + h * 64:r * P + (h + 1) * 64],
                                              stg[u][:, 256 + h * NCH:256 + (h + 1) * NCH], start=True, stop=True)
                            for r in range(2):
                                mm = pe.matmul(PS[7][0:32, 0:P], Bst[u][:, r].rearrange("p h c -> p (h c)"),
                                               Q[:, r, bass.ds(i * 2 + u, 1), 0:L, :].rearrange("p a k c -> p (a k c)"),
                                               start=r == 0, stop=r == 1)
                            mm.then_inc(S("eg_full"), 1)
                    pe.wait_ge(S("t_landed"), 256 * (part + 1))
                    with pe.Fori(0, PG // 2) as i:
                        for u in range(2):
                            n = part * PG + u
                            pe.wait_ge(S("h_staged"), i * 2 + n + 1)
                            pe.wait_ge(S("y_copied"), i * 2 + n + 1)
                            for h in range(2):
                                out = PS[4 + u][0:NCH, h * P:(h + 1) * P]
                                pe.matmul(out, UTst[u][:, h * NCH:(h + 1) * NCH],
                                          Tt[:, h, bass.ds(i * 2 + u, 1), :].rearrange("p a n -> p (a n)"), start=True, stop=False)
                                for r in range(2):
                                    mm = pe.matmul(out, Hst[u][:, h, r, :],
                                                   Q[:, r, bass.ds(i * 2 + u, 1), 1:L + 1, :].rearrange("p a k c -> p (a k c)"),
                                                   start=False, stop=r == 1)
                            mm.then_inc(S("y_full"), 1)
                pe.wait_ge(S("fin_ready"), 1)
                for r in range(2):
                    if r:
                        pe.wait_ge(S("fin_copied"), r)
                    for t in range(2):
                        nc.tensor.transpose(PS[6][:, t * P:(t + 1) * P], FinS[:, r, 4 * t:4 * t + 4, :].rearrange("p b g -> p (b g)"), ident)
                    nc.tensor.transpose(PS[6][0:GH, 256:384], FinP[:, r, :], ident).then_inc(S("fin_full"), 1)

            @block.scalar
            def _(act):
                act.sem_inc(S("g_copied"), 1)
                act.sem_inc(S("y_copied"), 2)
                for a, lam in enumerate((lam_re, lam_im)):
                    act.dma_start(lamn[0:GH, a, :], lam[0].rearrange("(g h) p -> g (h p)", h=2)).then_inc(S("lam_landed"), 16)
                act.dma_start(ldn[0:GH, :], log_dt[0].rearrange("(g h) -> g h", h=2)).then_inc(S("lam_landed"), 16)
                for r, b in enumerate((b_re, b_im)):
                    for h in range(2):
                        act.dma_start(Bn[h * 64:(h + 1) * 64, r, :, :], b[0].rearrange("(g h) p c -> h p g c", h=2)[h])\
                            .then_inc(S("bn_landed"), 16)
                act.dma_start(dcol[0:32, :], ssm_d[0].rearrange("(g a) -> a g", a=32)).then_inc(S("d_landed"), 16)
                act.wait_ge(S("lam_ready"), 1)
                nc.scalar.activation(tp[:, 3, :], tp[:, 2, :], ACT.Exp).then_inc(S("dt_ready"), 1)
                act.wait_ge(S("arg_ready"), 1)
                nc.scalar.activation(tp[:, 6, :], tp[:, 4, :], ACT.Exp).then_inc(S("mag_ready"), 1)
                act.wait_ge(S("arg_ready"), 2)
                nc.scalar.activation(tp[:, 9, :], tp[:, 7, :], ACT.Sin)
                nc.scalar.activation(tp[:, 10, :], tp[:, 8, :], ACT.Sin).then_inc(S("sin_ready"), 1)
                for part in range(NPART):
                    with act.Fori(0, PG // 2) as i:
                        for u in range(2):
                            n = part * PG + u
                            act.wait_ge(S("turned"), i * 2 + n + 3)
                            act.wait_ge(S("eg_full"), i * 2 + n + 1)
                            nc.scalar.copy(UTa[:, bass.ds(i * 2 + u, 1), :].rearrange("p a n -> p (a n)"), PS[4 + u][:, 256:336])
                            nc.scalar.copy(stg[u], PS[4 + u][:, 0:336]).then_inc(S("eg_staged"), 1)
                        for u in range(2):
                            n = part * PG + u
                            act.wait_ge(S("eg_full"), i * 2 + n + 3)
                            nc.scalar.copy(Ga[0:32, bass.ds(i * 2 + u, 1), :].rearrange("p a n -> p (a n)"), PS[7][0:32, 0:P])\
                                .then_inc(S("g_copied"), 1)
                    with act.Fori(0, PG // 2) as i:
                        for u in range(2):
                            n = part * PG + u
                            act.wait_ge(S("y_full"), i * 2 + n + 3)
                            nc.scalar.copy(urows[0:NCH, :, bass.ds(i * 64 + u * 32, 32)].rearrange("p s (h c) -> p h s c", h=2),
                                           PS[4 + u][0:NCH, 0:256].rearrange("p (h s c) -> p h s c", h=2, s=L)).then_inc(S("y_copied"), 1)

            @block.vector
            def _(dve):
                V = nc.vector
                order = [0]

                def link(ins):
                    order[0] += 1
                    ins.then_inc(S("s5_order"), 1)
                    dve.wait_ge(S("s5_order"), order[0])

                dve.sem_inc(S("e_copied"), 1)
                dve.wait_ge(S("lam_landed"), 48)
                V.tensor_copy(lamn[0:GH, 2, :].rearrange("p (h s) -> p h s", h=2),
                              ldn[0:GH, :].unsqueeze(2).broadcast_to([GH, 2, 64])).then_inc(S("ldt_rows"), 1)
                dve.wait_ge(S("lam_full"), 1)
                V.tensor_copy(tp[:, 0:3, :], PS[0][:, 0:96].rearrange("p (a g) -> p a g", a=3)).then_inc(S("lam_ready"), 1)
                dve.wait_ge(S("lam_ready"), 1)
                dve.wait_ge(S("dt_ready"), 1)
                V.tensor_tensor(tp[:, 4, :], tp[:, 0, :], tp[:, 3, :], ALU.mult).then_inc(S("arg_ready"), 1)
                link(V.tensor_tensor(tp[:, 5, :], tp[:, 1, :], tp[:, 3, :], ALU.mult))
                link(V.tensor_scalar(tp[:, 7, :], tp[:, 5, :], float(1 / (2 * np.pi)), MAGIC, ALU.mult, ALU.add))
                link(V.tensor_scalar(tp[:, 7, :], tp[:, 7, :], MAGIC, None, ALU.subtract))
                link(V.scalar_tensor_tensor(out=tp[:, 8, :], in0=tp[:, 7, :], scalar=-TWO_PI_HI, in1=tp[:, 5, :], op0=ALU.mult, op1=ALU.add))
                link(V.scalar_tensor_tensor(out=tp[:, 11, :], in0=tp[:, 7, :], scalar=-TWO_PI_LO, in1=tp[:, 8, :], op0=ALU.mult, op1=ALU.add))
                link(V.tensor_scalar(tp[:, 7, :], tp[:, 11, :], 3.1415925, -3.1415925, ALU.min, ALU.max))
                link(V.tensor_scalar(tp[:, 12, :], tp[:, 7, :], -1.0, None, ALU.mult))
                link(V.tensor_tensor(tp[:, 13, :], tp[:, 12, :], tp[:, 7, :], ALU.max))
                V.tensor_scalar(tp[:, 8, :], tp[:, 13, :], -1.0, float(np.pi / 2), ALU.mult, ALU.add).then_inc(S("arg_ready"), 1)
                dve.wait_ge(S("sin_ready"), 1)
                dve.wait_ge(S("mag_ready"), 1)
                V.tensor_tensor(PK[:, 0, 1, :], tp[:, 6, :], tp[:, 10, :], ALU.mult)
                link(V.tensor_tensor(PK[:, 1, 1, :], tp[:, 6, :], tp[:, 9, :], ALU.mult))
                V.memset(PK[:, 0, 0, :], 1.0)
                V.memset(PK[:, 1, 0, :], 0.0)
                V.tensor_scalar(tp[:, 7, :], PK[:, 0, 1, :], -1.0, None, ALU.add)
                V.tensor_tensor(tp[:, 8, :], tp[:, 0, :], tp[:, 0, :], ALU.mult)
                link(V.tensor_tensor(tp[:, 9, :], tp[:, 1, :], tp[:, 1, :], ALU.mult))
                link(V.tensor_tensor(tp[:, 8, :], tp[:, 8, :], tp[:, 9, :], ALU.add))
                V.reciprocal(tp[:, 9, :], tp[:, 8, :])
                V.tensor_tensor(tp[:, 10, :], tp[:, 7, :], tp[:, 0, :], ALU.mult)
                V.tensor_tensor(tp[:, 11, :], PK[:, 1, 1, :], tp[:, 1, :], ALU.mult)
                V.tensor_tensor(tp[:, 12, :], PK[:, 1, 1, :], tp[:, 0, :], ALU.mult)
                link(V.tensor_tensor(tp[:, 13, :], tp[:, 7, :], tp[:, 1, :], ALU.mult))
                V.tensor_tensor(tp[:, 10, :], tp[:, 10, :], tp[:, 11, :], ALU.add)
                link(V.tensor_tensor(tp[:, 12, :], tp[:, 12, :], tp[:, 13, :], ALU.subtract))
                V.tensor_tensor(tp[:, 14, :], tp[:, 10, :], tp[:, 9, :], ALU.mult)
                link(V.tensor_tensor(tp[:, 15, :], tp[:, 12, :], tp[:, 9, :], ALU.mult))
                for k in range(1, L):
                    V.tensor_tensor(tp[:, 7, :], PK[:, 0, k, :], PK[:, 0, 1, :], ALU.mult)
                    V.tensor_tensor(tp[:, 8, :], PK[:, 1, k, :], PK[:, 1, 1, :], ALU.mult)
                    V.tensor_tensor(tp[:, 10, :], PK[:, 0, k, :], PK[:, 1, 1, :], ALU.mult)
                    link(V.tensor_tensor(tp[:, 11, :], PK[:, 1, k, :], PK[:, 0, 1, :], ALU.mult))
                    V.tensor_tensor(PK[:, 0, k + 1, :], tp[:, 7, :], tp[:, 8, :], ALU.subtract)
                    link(V.tensor_tensor(PK[:, 1, k + 1, :], tp[:, 10, :], tp[:, 11, :], ALU.add))
                V.tensor_scalar(NPI, PK[:, 1], -1.0, None, ALU.mult)
                link(V.tensor_scalar(NPR, PK[:, 0], -1.0, None, ALU.mult))
                for s in range(L):
                    V.tensor_copy(RK[:, :, :, s], PK[:, :, L - 1 - s, :])
                dve.wait_ge(S("bn_landed"), 64)
                fr, fi = (tp[:, 14 + r, :].unsqueeze(2).broadcast_to([P, GH, CH]) for r in range(2))
                V.tensor_tensor(Bb[:, 0], Bn[:, 0], fr, ALU.mult)
                V.tensor_tensor(Bb[:, 1], Bn[:, 1], fr, ALU.mult)
                V.tensor_tensor(tb[:, 0], Bn[:, 1], fi, ALU.mult)
                link(V.tensor_tensor(tb[:, 1], Bn[:, 0], fi, ALU.mult))
                V.tensor_tensor(Bb[:, 0], Bb[:, 0], tb[:, 0], ALU.subtract)
                V.tensor_tensor(Bb[:, 1], Bb[:, 1], tb[:, 1], ALU.add).then_inc(S("bbar_ready"), 1)
                dve.wait_ge(S("bbar_ready"), 1)
                dve.wait_ge(S("ct_full"), 1)
                for r in range(2):
                    for b in range(2):
                        for h in range(2):
                            V.tensor_copy(Ct[h * 64:(h + 1) * 64, r, b * 16:(b + 1) * 16, :],
                                          PS[4 + 2 * r + b][h * 64:(h + 1) * 64, :].rearrange("p (g h c) -> p g h c", h=2, c=CH)[:, :, h, :])
                dve.wait_ge(S("h0_full"), 1)
                link(V.tensor_copy(H0.rearrange("p r b g -> p (r b g)"), PS[1][:, :]))
                V.memset(Ha[:, 0, :, :], 0.0).then_inc(S("ct_ready"), 1)
                dve.wait_ge(S("d_landed"), 16)
                for part in range(NPART):
                    gs = slice(part * PG, (part + 1) * PG)

                    def spread(table):
                        return table[:, :, gs].rearrange("p k g -> p g k").unsqueeze(3).broadcast_to([P, PG, 9, CH])

                    def rows(r):
                        return Ct[:, r, gs, :].unsqueeze(2).broadcast_to([P, PG, 9, CH])

                    t1 = tq[:, 0:PG * 9 * CH].rearrange("p (g k c) -> p g k c", g=PG, k=9)
                    if part:
                        dve.wait_ge(S("y_full"), PG * part + 2)
                    V.tensor_tensor(Q[:, 0], rows(0), spread(PK[:, 0]), ALU.mult)
                    link(V.tensor_tensor(t1, rows(1), spread(NPI), ALU.mult))
                    link(V.tensor_tensor(Q[:, 0], Q[:, 0], t1, ALU.add))
                    V.tensor_tensor(Q[:, 1], rows(0), spread(NPI), ALU.mult)
                    link(V.tensor_tensor(t1, rows(1), spread(NPR), ALU.mult))
                    V.tensor_tensor(Q[:, 1], Q[:, 1], t1, ALU.add).then_inc(S("q_ready"), 1)
                    with dve.Fori(0, PG // 2) as i:
                        for u in range(2):
                            n = part * PG + u
                            bb = Bb[:, :, bass.ds(i * 2 + n, 1), :].rearrange("p r a c -> p r (a c)").unsqueeze(2).broadcast_to([P, 2, L, CH])
                            rk = [RK[:, r, bass.ds(i * 2 + n, 1), :].rearrange("p a s -> p (a s)").unsqueeze(1).unsqueeze(3)
                                  .broadcast_to([P, 2, L, CH]) for r in range(2)]
                            dve.wait_ge(S("turned"), i * 2 + n + 1)
                            V.tensor_tensor(tA[u], bb, rk[0], ALU.mult)
                            V.tensor_tensor(tB[u], bb, rk[1], ALU.mult).then_inc(S("eb_parts"), 1)
                            dve.wait_ge(S("eb_parts"), i * 2 + n + 1)
                            V.tensor_tensor(EB[u][:, 0], tA[u][:, 0], tB[u][:, 1], ALU.subtract)
                            V.tensor_tensor(EB[u][:, 1], tB[u][:, 0], tA[u][:, 1], ALU.add).then_inc(S("eb_ready"), 1)
                        for u in range(2):
                            n = part * PG + u
                            dve.wait_ge(S("eg_full"), i * 2 + n + 3)
                            V.tensor_copy(ea[:, :, :, bass.ds(i * 2 + u, 1)].rearrange("p c r a -> p r (c a)"),
                                          PS[6][:, 0:2 * NCH].rearrange("p (r c) -> p r c", r=2)).then_inc(S("e_copied"), 1)
                    V.tensor_tensor(dI[0:32], C("chandiag", 32).unsqueeze(1).broadcast_to([32, PG, CH]),
                                    dcol[0:32, gs].unsqueeze(2).broadcast_to([32, PG, CH]), ALU.mult).then_inc(S("s5_order"), 1)
                    order[0] += 1
                    dve.wait_ge(S("s5_order"), order[0])
                    dve.wait_ge(S("g_copied"), PG * (part + 1) + 1)
                    V.tensor_tensor(Ga[0:32, :, 0:CH], Ga[0:32, :, 0:CH], dI[0:32], ALU.add).then_inc(S("g_diag"), 1)
                    dve.wait_ge(S("e_copied"), PG * (part + 1) + 1)
                    dve.wait_ge(S("g_diag"), part + 1)
                    a8r = PK[:, 0, L, gs].unsqueeze(1).broadcast_to([P, 2, PG])
                    if part:
                        dve.wait_ge(S("h_staged"), PG * part)
                    V.tensor_copy(Ha[:, NPC:NCH, :, :].rearrange("p b r g -> p r b g")[:, 0], H0[:, 0, :, gs])
                    link(V.tensor_copy(Ha[:, NPC:NCH, :, :].rearrange("p b r g -> p r b g")[:, 1], H0[:, 1, :, gs]))

                    with dve.Fori(0, NPC - 1) as i:
                        def at(buf, k):
                            return buf[:, bass.ds(i + k, 1), :, :].rearrange("p a r g -> p (a r) g")
                        base = part * 3 * (NPC - 1)
                        V.tensor_tensor(sc[:, 0], a8r, at(Ha, 0), ALU.mult)
                        V.tensor_tensor(sc[:, 1, 0, :], NPI[:, L, gs], at(Ha, 0)[:, 1, :], ALU.mult)
                        V.tensor_tensor(sc[:, 1, 1, :], PK[:, 1, L, gs], at(Ha, 0)[:, 0, :], ALU.mult).then_inc(S("scan_order"), 1)
                        dve.wait_ge(S("scan_order"), i * 3 + (base + 1))
                        V.tensor_tensor(sc[:, 2], sc[:, 0], at(ea, 0), ALU.add).then_inc(S("scan_order"), 1)
                        dve.wait_ge(S("scan_order"), i * 3 + (base + 2))
                        V.tensor_tensor(at(Ha, 1), sc[:, 2], sc[:, 1], ALU.add).then_inc(S("scan_order"), 1)
                        dve.wait_ge(S("scan_order"), i * 3 + (base + 3))
                    last = NPC - 1
                    V.tensor_tensor(sc[:, 0], a8r, Ha[:, last], ALU.mult)
                    V.tensor_tensor(sc[:, 1, 0, :], NPI[:, L, gs], Ha[:, last, 1, :], ALU.mult)
                    link(V.tensor_tensor(sc[:, 1, 1, :], PK[:, 1, L, gs], Ha[:, last, 0, :], ALU.mult))
                    link(V.tensor_tensor(sc[:, 2], sc[:, 0], ea[:, last], ALU.add))
                    link(V.tensor_tensor(FinP[:, :, gs], sc[:, 2], sc[:, 1], ALU.add))
                    ser, sei = (ea[:, NPC:NCH, r, :] for r in range(2))
                    pr, npi, pi = (x[:, L, gs].unsqueeze(1).broadcast_to([P, NB, PG]) for x in (PK[:, 0], NPI, PK[:, 1]))
                    s1, s2 = (tq[:, k * 64:(k + 1) * 64].rearrange("p (b g) -> p b g", b=NB) for k in range(2))
                    for r, (x, y) in enumerate(((npi, 1), (pi, 0))):
                        V.tensor_tensor(s1, pr, H0[:, r, :, gs], ALU.mult)
                        link(V.tensor_tensor(s2, x, H0[:, y, :, gs], ALU.mult))
                        link(V.tensor_tensor(s1, s1, s2, ALU.add))
                        link(V.tensor_tensor(FinS[:, r, :, gs], s1, (ser, sei)[r], ALU.add))
                    dve.sem_inc(S("h_done"), 1)
                dve.sem_inc(S("fin_ready"), 1)
                for r in range(2):
                    dve.wait_ge(S("fin_full"), r + 1)
                    V.tensor_copy(stg_fin[:, r, 0:2, :], PS[6][:, 0:256].rearrange("p (t n) -> p t n", t=2))
                    V.tensor_copy(stg_fin[0:GH, r, 2, :], PS[6][0:GH, 256:384]).then_inc(S("fin_copied"), 1)

        take = scratch()
        yn = take(3 * SSMW).rearrange("p (t n) -> p t n", t=3)
        with program() as block:
            @block.sync
            def _(sp):
                sp.wait_ge(S("y_stored"), 16 * NPART)
                for t in range(3):
                    sp.dma_start(yn[0:TOK[t], t, :], y_dram[t * P:t * P + TOK[t]]).then_inc(S("yn_landed"), 16)

            @block.tensor
            def _(pe):
                pe.wait_ge(S("yn_landed"), 48)
                for n in range(6):
                    t, c = n // 2, n % 2
                    if n >= 4:
                        pe.wait_ge(S("ys_ready"), n - 3)
                    for j in range(4):
                        tr = nc.tensor.transpose(PS[4 + n % 4][:, j * P:j * P + TOK[t]],
                                                 yn[0:TOK[t], t, (4 * c + j) * P:(4 * c + j + 1) * P], ident[0:TOK[t], 0:TOK[t]])
                    tr.then_inc(S("ys_full"), 1)

            @block.scalar
            def _(act):
                for n in range(6):
                    t, c = n // 2, n % 2
                    act.wait_ge(S("ys_full"), n + 1)
                    nc.scalar.activation(ysT[:, 4 * c:4 * c + 4, t * P:t * P + TOK[t]],
                                         PS[4 + n % 4][:, :].rearrange("p (j n) -> p j n", j=4)[:, :, 0:TOK[t]],
                                         ACT.Gelu_apprx_tanh).then_inc(S("ys_ready"), 1)

        take = scratch()
        kvp = take(2 * 1536).rearrange("p (t n) -> p t n", t=2)
        Sb = [take(4 * SEQ).rearrange("p (h k) -> p h k", h=4) for _ in range(2)]
        PTs = [take(4 * SEQ).rearrange("p (b h q) -> p b h q", b=2, h=4) for _ in range(2)]
        oacc = take(2 * 1024).rearrange("p (t h d) -> p t h d", t=2, h=NH)
        ot = [take(256).rearrange("p (h d) -> p h d", h=4) for _ in range(2)]
        nmx, rs, wgt = (take(64).rearrange("p (n h) -> p n h", h=4) for _ in range(3))
        pcol = take(4).rearrange("p (v m) -> p v m", v=2)
        pe32 = take(2 * P).rearrange("p (v d s) -> p v d s", v=2, d=2)
        pl32 = take(2)
        pl = take(2 * 2 * 16).rearrange("p (a c) -> p a c", a=4)
        Gp = take(4 * 32).rearrange("p (a c) -> p a c", a=4)
        Gr = take(2 * P).rearrange("p (g n c) -> p g n c", g=2, n=4)
        kcT = take(32).rearrange("p (g c) -> p g c", g=2)
        Vbd = take(4 * 256).rearrange("p (g n d) -> p g n d", g=4, n=4)
        Pc = take(512).rearrange("p (h c) -> p h c", h=NH)
        PcT = take(512)
        cm, cs_, cw = (take(NH) for _ in range(3))
        Sc = take(NH * NC_P).rearrange("p (h c) -> p h c", h=NH)
        work = [(qt, br, g) for qt in range(2) for br in range(2) for g in range(NKV)]
        NW = len(work)

        with program() as block:
            @block.sync
            def _(sp):
                for t in range(2):
                    sp.dma_start(kvp[:, t, 0:1024], kvr_prompt[0, 0, t * P:(t + 1) * P].rearrange("t a g d -> t (a g d)")).then_inc(S("kvp_landed"), 16)
                    sp.dma_start(kvp[:, t, 1024:1536], win_prompt[0, 0, t * P:(t + 1) * P].rearrange("t a g d -> t (a g d)")).then_inc(S("kvp_landed"), 16)
                sp.dma_start(x_dram, xT[:, :, :]).then_inc(S("x_spilled"), 16)
                sp.wait_ge(S("x_spilled"), 16)

            @block.gpsimd
            def _(pool):
                nc.gpsimd.memset(phi[:, :, :], 0.0).then_inc(S("phi_zero"), 1)
                nc.gpsimd.memset(Gp, 0.0).then_inc(S("pads_zero"), 1)
                nc.gpsimd.memset(Vbd, 0.0).then_inc(S("pads_zero"), 1)
                nc.gpsimd.memset(Pc, 0.0).then_inc(S("pads_zero"), 1)
                nc.gpsimd.tensor_copy(qs[:, :, :], qT[:, :, SEQ:NT]).then_inc(S("qs_ready"), 1)
                nc.gpsimd.tensor_copy(ks[:, 0:2, :], kvT[:, 4:6, SEQ:NT]).then_inc(S("qs_ready"), 1)
                nc.gpsimd.tensor_copy(ks[:, 2:4, :], kvT[:, 8:10, SEQ:NT]).then_inc(S("qs_ready"), 1)

            @block.scalar
            def _(act):
                for n in range(8):
                    act.dma_start(pcol[n * 16:(n + 1) * 16, :, :], w_pool[0].rearrange("v (m s) -> s v m", s=16)).then_inc(S("pool_landed"), 16)
                act.dma_start(pl32[0:32, :], w_pool[0].rearrange("v l -> l v")).then_inc(S("pool_landed"), 16)
                for d in range(2):
                    act.dma_start(pe32[0:32, :, d, :], w_pe[0].rearrange("v l d -> l v d")).then_inc(S("pool_landed"), 16)
                act.wait_ge(S("phi_zero"), 1)
                for h in range(2):
                    act.dma_start(phi[h * 64:(h + 1) * 64, :, h * 64:(h + 1) * 64], w_phi[0].rearrange("v a b -> a v b")).then_inc(S("phi_landed"), 16)
                act.wait_ge(S("pads_zero"), 3)
                act.wait_ge(S("ppool_ready"), 1)
                nc.scalar.activation(Gp[:, :, 0:NC_P], pl[:, :, 0:NC_P], ACT.Gelu_apprx_tanh).then_inc(S("pgelu_ready"), 1)
                for qt in range(2):
                    act.wait_ge(S("pc_shifted"), qt + 1)
                    nc.scalar.activation(Sc, Sc, ACT.Exp).then_inc(S("pc_exp"), 1)
                    act.wait_ge(S("pct_full"), qt + 1)
                    nc.scalar.copy(PcT, PS[7][:, :]).then_inc(S("pct_copied"), 1)
                for n in range(NW + 1):
                    if n < NW:
                        KE = P * (work[n][0] + 1)
                        act.wait_ge(S("pmax_ready"), n + 1)
                        for h in range(4):
                            ins = nc.scalar.activation(Sb[n % 2][:, h, 0:KE], Sb[n % 2][:, h, 0:KE], ACT.Exp,
                                                       bias=nmx[:, n, h:h + 1], accum_out=rs[:, n, h:h + 1])
                        ins.then_inc(S("p_ready"), 1)
                    if n >= 1:
                        m = n - 1
                        act.wait_ge(S("pt_full"), m + 1)
                        if m >= 2:
                            act.wait_ge(S("o_full"), m - 1)
                        for kb in range(work[m][0] + 1):
                            ins = nc.scalar.copy(PTs[m % 2][:, kb].rearrange("p h q -> p (h q)"), PS[4 + kb][:, :])
                        ins.then_inc(S("pt_copied"), 1)

            @block.tensor
            def _(pe):
                pe.wait_ge(S("pool_landed"), 176)
                for v in range(2):
                    mm = pe.matmul(PS[5][:, v:v + 1], pe32[0:32, v].rearrange("p d s -> p (d s)"), pl32[0:32, v:v + 1], start=True, stop=True)
                mm.then_inc(S("pec_full"), 1)
                pe.wait_ge(S("poolw_ready"), 1)
                pe.wait_ge(S("kvp_landed"), 64)
                for t in range(2):
                    for a in range(4):
                        mm = pe.matmul(PS[6][:, a * 32:(a + 1) * 32].rearrange("p (m t n) -> p m t n", m=2, t=2)[:, :, t, :],
                                       kvp[:, t, a * P:(a + 1) * P], poolw[:, a // 2].rearrange("p m n -> p (m n)"), start=True, stop=True)
                mm.then_inc(S("ppool_full"), 1)
                pe.wait_ge(S("pgr_ready"), 1)
                pe.wait_ge(S("phi_landed"), 32)
                for g in range(2):
                    pe.matmul(PS[7][:, g * 16:g * 16 + NC_P], phi[:, 0, :], Gp[:, g, 0:NC_P], start=True, stop=True)
                for g in range(2):
                    mm = pe.matmul(PS[7][:, 64 + g * P:64 + (g + 1) * P], Gr[:, g].rearrange("p n c -> p (n c)"), phi[:, 1, :], start=True, stop=True)
                mm.then_inc(S("pcv_full"), 1)
                pe.wait_ge(S("pcv_copied"), 1)
                for qt in range(2):
                    for h in range(NH):
                        g, n = h // 4, h % 4
                        a = (g % 2) * 64
                        mm = pe.matmul(PS[(6, 0)[g % 2]][:, h * 32:h * 32 + NC_P], qT[a:a + 64, (g // 2) * 4 + n, qt * P:(qt + 1) * P],
                                       kcT[a:a + 64, g // 2, 0:NC_P], start=True, stop=True)
                    mm.then_inc(S("pcs_full"), 1)
                    pe.wait_ge(S("pc_ready"), qt + 1)
                    for g in range(4):
                        tr = nc.tensor.transpose(PS[7][:, g * P:(g + 1) * P], Pc[:, 4 * g:4 * g + 4, :].rearrange("p h c -> p (h c)"), ident)
                    tr.then_inc(S("pct_full"), 1)
                    pe.wait_ge(S("pct_copied"), qt + 1)
                    if qt:
                        pe.wait_ge(S("pco_done"), qt)
                    for g in range(4):
                        mm = pe.matmul(PS[4 + g // 2][:, (g % 2) * 256:(g % 2 + 1) * 256], PcT[:, g * P:(g + 1) * P],
                                       Vbd[:, g].rearrange("p n d -> p (n d)"), start=True, stop=True)
                    mm.then_inc(S("pco_full"), 1)
                pe.wait_ge(S("pco_done"), 2)
                for n in range(NW + 2):
                    if n < NW:
                        qt, br, g = work[n]
                        KE = P * (qt + 1)
                        if n >= 2:
                            pe.wait_ge(S("s_read"), n - 1)
                        a = (g % 2) * 64
                        for h in range(4):
                            mm = pe.matmul(PS[2 * (n % 2) + h // 2][:, (h % 2) * 256:(h % 2) * 256 + KE],
                                           qT[a:a + 64, (g // 2) * 4 + h, qt * P:(qt + 1) * P],
                                           kvT[a:a + 64, 4 + 4 * br + g // 2, 0:KE], start=True, stop=True)
                        mm.then_inc(S("s_full"), 1)
                    if 1 <= n <= NW:
                        m = n - 1
                        qt = work[m][0]
                        pe.wait_ge(S("p_ready"), m + 1)
                        if m:
                            pe.wait_ge(S("pt_copied"), m)
                        for kb in range(qt + 1):
                            for h in range(4):
                                tr = nc.tensor.transpose(PS[4 + kb][:, h * P:(h + 1) * P], Sb[m % 2][:, h, kb * P:(kb + 1) * P], ident)
                        tr.then_inc(S("pt_full"), 1)
                    if n >= 2:
                        m = n - 2
                        qt, br, g = work[m]
                        pe.wait_ge(S("pt_copied"), m + 1)
                        if m >= 2:
                            pe.wait_ge(S("o_done"), m - 1)
                        for h in range(4):
                            for kb in range(qt + 1):
                                mm = pe.matmul(PS[6 + m % 2][:, h * 64:(h + 1) * 64], PTs[m % 2][:, kb, h, :],
                                               kvp[:, kb, (768 if br == 0 else 1280) + g * 64:(768 if br == 0 else 1280) + (g + 1) * 64],
                                               start=kb == 0, stop=kb == qt)
                        mm.then_inc(S("o_full"), 1)
                pe.wait_ge(S("o_done"), NW)
                for n in range(4):
                    t, c = n // 2, n % 2
                    for j in range(4):
                        tr = nc.tensor.transpose(PS[n][:, j * P:(j + 1) * P],
                                                 oacc[:, t, 2 * (4 * c + j):2 * (4 * c + j) + 2, :].rearrange("p h d -> p (h d)"), ident)
                    tr.then_inc(S("ot_full"), 1)

            @block.vector
            def _(dve):
                V = nc.vector
                order = [0]

                def link(ins):
                    order[0] += 1
                    ins.then_inc(S("p_order"), 1)
                    dve.wait_ge(S("p_order"), order[0])

                dve.wait_ge(S("pool_landed"), 176)
                V.tensor_tensor(poolw[:, :, :, :], pcol.unsqueeze(3).broadcast_to([P, 2, 2, 8]),
                                C("submask").unsqueeze(1).unsqueeze(1).broadcast_to([P, 2, 2, 8]), ALU.mult).then_inc(S("poolw_ready"), 1)
                dve.wait_ge(S("pec_full"), 1)
                link(V.tensor_copy(pec[:, :], PS[5][:, 0:2]))
                dve.wait_ge(S("ppool_full"), 1)
                parts = PS[6][:, 0:P].rearrange("p (a m c) -> p a m c", a=4, m=2)
                for v in range(2):
                    V.tensor_scalar(pl[:, 2 * v:2 * v + 2, 0:NC_P], parts[:, 2 * v:2 * v + 2, 0, 0:NC_P], pec[:, v:v + 1], None, ALU.add).then_inc(S("p_order"), 1)
                order[0] += 2
                dve.wait_ge(S("p_order"), order[0])
                V.tensor_tensor(pl[:, :, 0:NC_P], pl[:, :, 0:NC_P], parts[:, :, 1, 1:NC_P + 1], ALU.add).then_inc(S("ppool_ready"), 1)
                dve.wait_ge(S("pgelu_ready"), 1)
                V.tensor_copy(Gr, Gp[:, 2:4, :].unsqueeze(2).broadcast_to([P, 2, 4, 32])).then_inc(S("pgr_ready"), 1)
                dve.wait_ge(S("pcv_full"), 1)
                V.tensor_copy(kcT[:, :, 0:NC_P], PS[7][:, 0:32].rearrange("p (g c) -> p g c", g=2)[:, :, 0:NC_P])
                for n in range(4):
                    ins = V.tensor_copy(Vbd[n * 32:(n + 1) * 32, :, n, :], PS[7][n * 32:(n + 1) * 32, 64:320].rearrange("p (g d) -> p g d", g=4))
                ins.then_inc(S("pcv_copied"), 1)
                for qt in range(2):
                    dve.wait_ge(S("pcs_full"), qt + 1)
                    bias = C("biascp")[:, qt * 240:(qt + 1) * 240].rearrange("p (h c) -> p h c", h=NH)
                    valid = C("validcp")[:, qt * NC_P:(qt + 1) * NC_P].unsqueeze(1).broadcast_to([P, NH, NC_P])
                    for par in range(2):
                        for g in (par, par + 2):
                            hs = slice(4 * g, 4 * g + 4)
                            ins = V.tensor_tensor(Sc[:, hs, :], PS[(6, 0)[par]][:, :].rearrange("p (h c) -> p h c", h=NH)[:, hs, 0:NC_P],
                                                  bias[:, hs, :], ALU.add)
                    link(ins)
                    link(V.tensor_reduce(cm, Sc, AX_X, ALU.max))
                    V.tensor_tensor(Sc, Sc, cm.unsqueeze(2).broadcast_to([P, NH, NC_P]), ALU.subtract).then_inc(S("pc_shifted"), 1)
                    dve.wait_ge(S("pc_exp"), qt + 1)
                    link(V.tensor_reduce(cs_, Sc, AX_X, ALU.add))
                    V.tensor_tensor(Pc[:, :, 0:NC_P], Sc, valid, ALU.mult).then_inc(S("pc_ready"), 1)
                    link(V.reciprocal(cs_, cs_))
                    if qt:
                        dve.wait_ge(S("pco_done"), qt)
                    link(V.tensor_tensor(cw, cs_, gN[:, qt, 0:NH], ALU.mult))
                    dve.wait_ge(S("pco_full"), qt + 1)
                    for b in range(2):
                        ins = V.tensor_tensor(oacc[:, qt, 8 * b:8 * b + 8, :], PS[4 + b][:, :].rearrange("p (h d) -> p h d", h=8),
                                              cw[:, 8 * b:8 * b + 8].unsqueeze(2).broadcast_to([P, 8, 64]), ALU.mult)
                    ins.then_inc(S("pco_done"), 1)
                dve.wait_ge(S("pco_done"), 2)
                for n in range(NW + 2):
                    if n < NW:
                        qt, br, g = work[n]
                        KE = P * (qt + 1)
                        dve.wait_ge(S("s_full"), n + 1)
                        if n >= 2:
                            dve.wait_ge(S("pt_full"), n - 1)
                        for h in range(4):
                            ins = V.scalar_tensor_tensor(out=Sb[n % 2][:, h, 0:KE], in0=C("distp")[:, SEQ - KE:SEQ], scalar=-slope(4 * g + h),
                                                         in1=PS[2 * (n % 2) + h // 2][:, (h % 2) * 256:(h % 2) * 256 + KE], op0=ALU.mult, op1=ALU.add)
                        ins.then_inc(S("s_read"), 1)
                        dve.wait_ge(S("s_read"), n + 1)
                        V.tensor_reduce(nmx[:, n, :], Sb[n % 2][:, :, 0:KE], AX_X, ALU.max, negate=True).then_inc(S("pmax_ready"), 1)
                    if n >= 2:
                        m = n - 2
                        qt, br, g = work[m]
                        dve.wait_ge(S("o_full"), m + 1)
                        dve.wait_ge(S("p_ready"), m + 1)
                        link(V.reciprocal(rs[:, m, :], rs[:, m, :]))
                        link(V.tensor_tensor(wgt[:, m, :], rs[:, m, :], gN[:, qt, (br + 1) * NH + 4 * g:(br + 1) * NH + 4 * g + 4], ALU.mult))
                        link(V.tensor_tensor(ot[m % 2], PS[6 + m % 2][:, 0:256].rearrange("p (h d) -> p h d", h=4),
                                             wgt[:, m, :].unsqueeze(2).broadcast_to([P, 4, 64]), ALU.mult))
                        V.tensor_tensor(oacc[:, qt, 4 * g:4 * g + 4, :], oacc[:, qt, 4 * g:4 * g + 4, :], ot[m % 2], ALU.add).then_inc(S("o_done"), 1)
                for n in range(4):
                    t, c = n // 2, n % 2
                    dve.wait_ge(S("ot_full"), n + 1)
                    V.tensor_copy(oT[:, 4 * c:4 * c + 4, t * P:(t + 1) * P], PS[n][:, :].rearrange("p (j q) -> p j q", j=4)).then_inc(S("ot_ready"), 1)
                dve.wait_ge(S("ot_ready"), 4)

        phase.close()
        kept.close()
        open_arena(phase, "arena3")
        take = scratch()
        RP = 4
        pageA = [xT[:, :, :].rearrange("p k n -> p (k n)")[:, s * 768:(s + 1) * 768] for s in range(RP)]
        Vs = take(NPG * 256).rearrange("p (g n) -> p g n", g=NPG)
        KTs = take(2 * PAST).rearrange("p (g k) -> p g k", g=2)
        Ss = take(PAST + NQ)
        Sw = take(WIN + NQ)
        PT2 = [take(512) for _ in range(2)]
        wn = take(4 * 512).rearrange("p (t n) -> p t n", t=4)
        KwT = take(2 * WIN).rearrange("p (g k) -> p g k", g=2)
        kb = take(PAST + WIN + 2 * NQ)
        vnew = take(2 * 256).rearrange("p (a n) -> p a n", a=2)
        plS = take(4 * NC_S).rearrange("p (a c) -> p a c", a=4)
        kcs = take(2 * P).rearrange("p (g c) -> p g c", g=2)
        vcs = take(256)
        Pcs = take(NC_S)
        pcT = take(P)
        qst = take(2 * 64).rearrange("p (g r) -> p g r", g=2)
        kst = take(4 * NQ).rearrange("p (a q) -> p a q", a=4)
        gw = take(3)
        mx3, rs3, rw3 = (take(3) for _ in range(3))
        imp0, imp1, msk = (take(NBLK) for _ in range(3))
        top = take(16)
        waits = take(1)
        od = take(P).rearrange("p (u d) -> p u d", u=2)
        ptab = take(NB * NPG).bitcast(I32)

        with program() as block:
            @block.sync
            def _(sp):
                sp.dma_start(ptab[0:1, :], page_table.rearrange("b g -> (b g)").rearrange("(o n) -> o n", o=1)).then_inc(S("ptab_landed"), 16)
                sp.dma_start(kb, kbias).then_inc(S("kb_landed"), 16)
                sp.wait_ge(S("ptab_landed"), 16)
                n_pool = cache_kv.shape[1]
                rows = cache_kv[0].rearrange("n t a g d -> n t (a g d)")
                with sp.Fori(0, NB) as b:
                    def page(p):
                        return sp.value_load(ptab[0:1, bass.ds(b * NPG + p, 1)], min_val=0, max_val=n_pool - 1)

                    for p in range(NPG):
                        sp.wait_ge(S("page_used"), b * NPG + p + 1)
                        sp.dma_start(pageA[p % RP], rows[bass.ds(page(p), 1), :, 0:768].rearrange("o t n -> (o t) n")).then_inc(S(f"page_landed{p % RP}"), 16)
                    sp.wait_ge(S("so_full"), b + 1)
                    sp.dma_start(wn, state_win[0, bass.ds(b, 1)].rearrange("o (t p) a g d -> p (o t) (a g d)", p=P)).then_inc(S("wn_landed"), 16)
                    sp.dma_start(vnew[0:NQ, 0, :], kvr_sample[0, bass.ds(b, 1), :, 3].rearrange("o t g d -> (o t) (g d)")).then_inc(S("wn_landed"), 16)
                    sp.dma_start(vnew[0:NQ, 1, :], win_sample[0, bass.ds(b, 1), WIN - NQ:WIN, 1].rearrange("o t g d -> (o t) (g d)")).then_inc(S("wn_landed"), 16)
                    for p in range(NPG):
                        sp.dma_start(Vs[:, p, :], rows[bass.ds(page(p), 1), :, 768:1024].rearrange("o t n -> (o t) n")).then_inc(S("v_landed"), 16)

            @block.gpsimd
            def _(pool):
                with pool.Fori(0, NB) as b:
                    pool.wait_ge(S("so_done"), b + 1)
                    for g in range(2):
                        nc.gpsimd.tensor_tensor(qst[:, g, :].rearrange("p (h n q) -> p h n q", h=2, n=4),
                                                qs[:, 4 * g:4 * g + 4, bass.ds(b * NQ, NQ)].unsqueeze(1).broadcast_to([P, 2, 4, NQ]),
                                                C("half").unsqueeze(2).unsqueeze(3).broadcast_to([P, 2, 4, NQ]), ALU.mult)
                    nc.gpsimd.tensor_copy(kst, ks[:, :, bass.ds(b * NQ, NQ)])
                    nc.gpsimd.tensor_copy(gw, gS[:, :, bass.ds(b, 1)].rearrange("p r a -> p (r a)")).then_inc(S("q_staged"), 1)

            @block.tensor
            def _(pe):
                pe.sem_inc(S("page_used"), RP)
                pe.sem_inc(S("so_full"), 1)
                with pe.Fori(0, NB) as b:
                    pe.wait_ge(S("so_done"), b + 1)
                    for p in range(NPG):
                        pe.wait_ge(S(f"page_landed{p % RP}"), b * (16 * NPG // RP) + 16 * (p // RP + 1))
                        if p % 2 == 0:
                            pe.wait_ge(S("kt_copied"), b * 8 + (p // 2 + 1))
                        for g in range(2):
                            tr = nc.tensor.transpose(PS[6 + p // 2 % 2][:, (p % 2 * 2 + g) * P:(p % 2 * 2 + g + 1) * P],
                                                     pageA[p % RP][:, 512 + g * P:512 + (g + 1) * P], ident)
                        if p % 2:
                            tr.then_inc(S("kt_full"), 1)
                        for a in range(4):
                            mm = pe.matmul(PS[4 + a // 2][:, a % 2 * 256:a % 2 * 256 + 256].rearrange("p (m c) -> p m c", m=2)[:, :, p * 8:p * 8 + 8],
                                           pageA[p % RP][:, a * P:(a + 1) * P], poolw[:, a // 2].rearrange("p m n -> p (m n)"), start=True, stop=True)
                        mm.then_inc(S("page_used"), 1)
                    pe.wait_ge(S("sgelu_ready"), b + 1)
                    pe.wait_ge(S("kt_copied"), b * 8 + 10)
                    for g in range(2):
                        pe.matmul(PS[6][:, g * P:g * P + NC_S], phi[:, 0, :], plS[:, g, :], start=True, stop=True)
                    for g in range(2):
                        mm = pe.matmul(PS[6][0:NC_S, 256 + g * P:256 + (g + 1) * P], plS[:, 2 + g, :], phi[:, 1, :], start=True, stop=True)
                    mm.then_inc(S("cv_full"), 1)
                    pe.wait_ge(S("q_staged"), b + 1)
                    pe.wait_ge(S("cv_copied"), b + 1)
                    for g in range(2):
                        mm = pe.matmul(PS[7][g * 64:(g + 1) * 64, 0:NC_S], qst[:, g, :], kcs[:, g, 0:NC_S], start=True, stop=True)
                    mm.then_inc(S("cs_full"), 1)
                    for c in range(5):
                        if c >= 2:
                            pe.wait_ge(S("sel_read"), b * 5 + (c - 1))
                        for g in range(2):
                            if c < 4:
                                mm = pe.matmul(PS[4 + c % 2][g * 64:(g + 1) * 64, :], qst[:, g, :], KTs[:, g, c * 512:(c + 1) * 512], start=True, stop=True)
                            else:
                                mm = pe.matmul(PS[4][g * 64:(g + 1) * 64, 0:NQ], qst[:, g, :],
                                               kst[:, g, :], start=True, stop=True)
                        mm.then_inc(S("sel_full"), 1)
                    pe.wait_ge(S("cp_ready"), b + 1)
                    nc.tensor.transpose(PS[6][0:NC_S, 0:P], Pcs, ident).then_inc(S("pcT_full"), 1)
                    pe.wait_ge(S("pcT_copied"), b + 1)
                    pe.wait_ge(S("sel_read"), b * 5 + 4)
                    mm = pe.matmul(PS[5][:, 0:256], pcT[0:NC_S, :], vcs[0:NC_S, :], start=True, stop=True)
                    mm.then_inc(S("oc_full"), 1)
                    pe.matmul(PS[7][:, 0:NBLK], pcT[0:NC_S, :], C("overlap", NC_S), start=True, stop=True).then_inc(S("imp_full"), 1)
                    pe.wait_ge(S("imp_copied"), b + 1)
                    pe.matmul(PS[7][:, 64:64 + NBLK], C("same"), imp0, start=True, stop=True).then_inc(S("impsum_full"), 1)
                    pe.wait_ge(S("wn_landed"), b * 48 + 48)
                    pe.wait_ge(S("imp_read"), b + 1)
                    for t in range(4):
                        for g in range(2):
                            tr = nc.tensor.transpose(PS[6 + t // 2][:, (t % 2 * 2 + g) * P:(t % 2 * 2 + g + 1) * P],
                                                     wn[:, t, g * P:(g + 1) * P], ident)
                        if t % 2:
                            tr.then_inc(S("kw_full"), 1)
                    pe.wait_ge(S("oc_done"), b + 1)
                    pe.wait_ge(S("kw_copied"), b * 2 + 2)
                    for g in range(2):
                        mm = pe.matmul(PS[5][g * 64:(g + 1) * 64, :], qst[:, g, :], KwT[:, g, :], start=True, stop=True)
                    pe.wait_ge(S("sel_read"), b * 5 + 5)
                    for g in range(2):
                        mm = pe.matmul(PS[4][g * 64:(g + 1) * 64, 0:NQ], qst[:, g, :], kst[:, 2 + g, :], start=True, stop=True)
                    mm.then_inc(S("w_full"), 1)
                    pe.wait_ge(S("w_read"), b + 1)
                    pe.wait_ge(S("v_landed"), b * (16 * NPG) + 16 * NPG)
                    for n in range(7):
                        if n < 6:
                            pe.wait_ge(S("sp_ready"), b * 2 + (1 if n < 4 else 2))
                            pe.wait_ge(S("spt_copied"), b * 6 + (n + 1))
                            bank = PS[6 + n % 2]
                            if n < 5:
                                for j in range(4):
                                    src = Ss[:, (4 * n + j) * P:(4 * n + j + 1) * P] if n < 4 else Sw[:, j * P:(j + 1) * P]
                                    tr = nc.tensor.transpose(bank[:, j * P:(j + 1) * P], src, ident)
                            else:
                                nc.tensor.transpose(bank[0:NQ, 0:P], Ss[:, PAST:PAST + NQ], ident)
                                tr = nc.tensor.transpose(bank[0:NQ, P:2 * P], Sw[:, WIN:WIN + NQ], ident)
                            tr.then_inc(S("spt_full"), 1)
                        if n >= 1:
                            m = n - 1
                            pe.wait_ge(S("spt_copied"), b * 6 + (m + 3))
                            if m < 5:
                                for j in range(4):
                                    mm = pe.matmul(PS[5 if m < 4 else 4][:, 0:256], PT2[m % 2][:, j * P:(j + 1) * P],
                                                   Vs[:, 4 * m + j, :] if m < 4 else wn[:, j, 256:512],
                                                   start=j == 0 and m in (0, 4), stop=False)
                                mm.then_inc(S("pv_used"), 1)
                            else:
                                pe.matmul(PS[5][:, 0:256], PT2[m % 2][0:NQ, 0:P], vnew[0:NQ, 0, :], start=False, stop=True)
                                mm = pe.matmul(PS[4][:, 0:256], PT2[m % 2][0:NQ, P:2 * P], vnew[0:NQ, 1, :], start=False, stop=True)
                                mm.then_inc(S("so_full"), 1)
                    pe.wait_ge(S("od_ready"), b + 1)
                    nc.tensor.transpose(PS[6][:, 0:P], od.rearrange("p u d -> p (u d)"), ident).then_inc(S("odT_full"), 1)

            @block.scalar
            def _(act):
                act.sem_inc(S("kt_copied"), 2)
                act.sem_inc(S("spt_copied"), 2)
                act.sem_inc(S("so_done"), 1)
                with act.Fori(0, NB) as b:
                    for n in range(8):
                        act.wait_ge(S("kt_full"), b * 8 + (n + 1))
                        nc.scalar.copy(KTs[:, :, n * 256:(n + 1) * 256].rearrange("p g (t k) -> p t g k", t=2),
                                       PS[6 + n % 2][:, :].rearrange("p (t g k) -> p t g k", t=2, g=2)).then_inc(S("kt_copied"), 1)
                    act.wait_ge(S("pooled_ready"), b + 1)
                    nc.scalar.activation(plS, plS, ACT.Gelu_apprx_tanh).then_inc(S("sgelu_ready"), 1)
                    act.wait_ge(S("cv_full"), b + 1)
                    nc.scalar.copy(kcs[:, :, 0:NC_S], PS[6][:, 0:256].rearrange("p (g c) -> p g c", g=2)[:, :, 0:NC_S])
                    nc.scalar.copy(vcs[0:NC_S, :], PS[6][0:NC_S, 256:512]).then_inc(S("cv_copied"), 1)
                    act.wait_ge(S("cmax_ready"), b + 1)
                    nc.scalar.activation(Pcs, Pcs, ACT.Exp, bias=mx3[:, 0:1], accum_out=rs3[:, 0:1]).then_inc(S("cexp_ready"), 1)
                    act.wait_ge(S("pcT_full"), b + 1)
                    nc.scalar.copy(pcT[0:NC_S, :], PS[6][0:NC_S, 0:P]).then_inc(S("pcT_copied"), 1)
                    for n in range(2):
                        act.wait_ge(S("kw_full"), b * 2 + (n + 1))
                        nc.scalar.copy(KwT[:, :, n * 256:(n + 1) * 256].rearrange("p g (t k) -> p t g k", t=2),
                                       PS[6 + n][:, :].rearrange("p (t g k) -> p t g k", t=2, g=2)).then_inc(S("kw_copied"), 1)
                    act.wait_ge(S("smax_ready"), b * 2 + 1)
                    nc.scalar.activation(Ss, Ss, ACT.Exp, bias=mx3[:, 1:2], accum_out=rs3[:, 1:2]).then_inc(S("sp_ready"), 1)
                    act.wait_ge(S("smax_ready"), b * 2 + 2)
                    nc.scalar.activation(Sw, Sw, ACT.Exp, bias=mx3[:, 2:3], accum_out=rs3[:, 2:3]).then_inc(S("sp_ready"), 1)
                    for n in range(6):
                        act.wait_ge(S("spt_full"), b * 6 + (n + 1))
                        if n >= 2:
                            act.wait_ge(S("pv_used"), b * 5 + (n - 1))
                        if n < 5:
                            nc.scalar.copy(PT2[n % 2], PS[6 + n % 2][:, :]).then_inc(S("spt_copied"), 1)
                        else:
                            nc.scalar.copy(PT2[n % 2][0:NQ, 0:256], PS[6 + n % 2][0:NQ, 0:256]).then_inc(S("spt_copied"), 1)
                    act.wait_ge(S("odT_full"), b + 1)
                    for h in range(2):
                        ins = nc.scalar.copy(oT[h * 64:(h + 1) * 64, :, bass.ds(b * NQ + SEQ, NQ)],
                                             PS[6][h * 64:(h + 1) * 64, 0:P].rearrange("p (t h q) -> p t h q", h=2, q=NQ)[:, :, h, :])
                    ins.then_inc(S("so_done"), 1)

            @block.vector
            def _(dve):
                V = nc.vector
                dve.wait_ge(S("kb_landed"), 16)
                NL = 15
                with dve.Fori(0, NB) as b:
                    order = [0]

                    def link(ins):
                        order[0] += 1
                        ins.then_inc(S("s_order"), 1)
                        dve.wait_ge(S("s_order"), b * NL + order[0])

                    dve.wait_ge(S("page_used"), b * NPG + NPG + RP)
                    for v in range(2):
                        parts = PS[4 + v][:, :].rearrange("p (g m c) -> p g m c", g=2, m=2)
                        link(V.tensor_scalar(plS[:, 2 * v:2 * v + 2, :], parts[:, :, 0, 0:NC_S], pec[:, v:v + 1], None, ALU.add))
                        ins = V.tensor_tensor(plS[:, 2 * v:2 * v + 2, :], plS[:, 2 * v:2 * v + 2, :], parts[:, :, 1, 1:NC_S + 1], ALU.add)
                    ins.then_inc(S("pooled_ready"), 1)
                    dve.wait_ge(S("cs_full"), b + 1)
                    link(V.tensor_tensor(Pcs, PS[7][:, 0:NC_S], C("biascs"), ALU.add))
                    V.tensor_reduce(mx3[:, 0:1], Pcs, AX_X, ALU.max, negate=True).then_inc(S("cmax_ready"), 1)
                    for c in range(5):
                        w = 512 if c < 4 else NQ
                        dve.wait_ge(S("sel_full"), b * 5 + (c + 1))
                        V.tensor_tensor(Ss[:, c * 512:c * 512 + w], PS[4 + c % 2][:, 0:w], kb[:, c * 512:c * 512 + w], ALU.add).then_inc(S("sel_read"), 1)
                        if c == 0:
                            dve.wait_ge(S("cexp_ready"), b + 1)
                            link(V.reciprocal(rs3[:, 0:1], rs3[:, 0:1]))
                            V.tensor_scalar(Pcs, Pcs, rs3[:, 0:1], None, ALU.mult).then_inc(S("cp_ready"), 1)
                    dve.wait_ge(S("imp_full"), b + 1)
                    V.tensor_copy(imp0, PS[7][:, 0:NBLK]).then_inc(S("imp_copied"), 1)
                    dve.wait_ge(S("oc_full"), b + 1)
                    for g in range(4):
                        r = slice(g * 32, (g + 1) * 32)
                        ins = V.tensor_scalar(od[r, 0, :], PS[5][r, g * 64:(g + 1) * 64], gw[r, 0:1], None, ALU.mult)
                    ins.then_inc(S("oc_done"), 1)
                    dve.wait_ge(S("impsum_full"), b + 1)
                    V.tensor_copy(imp1, PS[7][:, 64:64 + NBLK]).then_inc(S("imp_read"), 1)
                    dve.wait_ge(S("imp_read"), b + 1)
                    V.memset(imp1[:, 0:1], FORCED)
                    link(V.memset(imp1[:, NBLK - 2:NBLK], FORCED))
                    V.memset(waits, 0.0)
                    link(V.max(top[:, 0:8], imp1))
                    V.memset(waits, 0.0)
                    link(V.match_replace(imp0, top[:, 0:8], imp1, -BIG))
                    V.memset(waits, 0.0)
                    link(V.max(top[:, 8:16], imp0))
                    V.memset(waits, 0.0)
                    link(V.match_replace(imp1, top[:, 8:16], imp0, -BIG))
                    link(V.tensor_scalar(msk, imp1, -1.0, -BIG, ALU.is_gt, ALU.mult))
                    blocks = Ss[:, 0:PAST].rearrange("p (s k) -> p s k", k=64)
                    link(V.tensor_tensor(blocks, blocks, msk[:, 0:32].unsqueeze(2).broadcast_to([P, 32, 64]), ALU.add))
                    V.tensor_reduce(mx3[:, 1:2], Ss, AX_X, ALU.max, negate=True).then_inc(S("smax_ready"), 1)
                    dve.wait_ge(S("w_full"), b + 1)
                    V.tensor_tensor(Sw[:, 0:WIN], PS[5][:, :], kb[:, PAST + NQ:PAST + NQ + WIN], ALU.add)
                    V.tensor_tensor(Sw[:, WIN:WIN + NQ], PS[4][:, 0:NQ], kb[:, PAST + NQ + WIN:], ALU.add).then_inc(S("w_read"), 1)
                    dve.wait_ge(S("w_read"), b + 1)
                    V.tensor_reduce(mx3[:, 2:3], Sw, AX_X, ALU.max, negate=True).then_inc(S("smax_ready"), 1)
                    dve.wait_ge(S("sp_ready"), b * 2 + 2)
                    link(V.reciprocal(rs3[:, 1:3], rs3[:, 1:3]))
                    link(V.tensor_tensor(rw3[:, 1:3], rs3[:, 1:3], gw[:, 1:3], ALU.mult))
                    dve.wait_ge(S("so_full"), b + 2)
                    for br in range(2):
                        for g in range(4):
                            r = slice(g * 32, (g + 1) * 32)
                            ins = V.scalar_tensor_tensor(out=od[r, 0, :], in0=PS[5 - br][r, g * 64:(g + 1) * 64], scalar=rw3[r, 1 + br:2 + br],
                                                         in1=od[r, 0, :], op0=ALU.mult, op1=ALU.add)
                        link(ins)
                    V.tensor_copy(od[:, 1, :], od[:, 0, :]).then_inc(S("od_ready"), 1)
                    assert order[0] == NL, order[0]

        phase.close()
        open_weights(phase, "w2")
        last = phase.enter_context(ExitStack())
        open_arena(last, "arena4")
        take = scratch()
        sgm = take(32 * NT).rearrange("p (t n) -> p t n", t=32)
        mT = take(KT * NT).rearrange("p (t n) -> p t n", t=KT)
        sB = take(NT)
        tmp = take(NT)
        hi, lo = actr[:, 0], actr[:, 1]

        def tile_of(buf, t):
            return buf[:, bass.ds(t, 1), :].rearrange("p a n -> p (a n)")

        def add_to_x(dve, job):
            def read(i, s):
                full(dve, job, i, s)
                nc.vector.tensor_tensor(tile_of(xT, i * 2 + s), tile_of(xT, i * 2 + s), PS[s][:, 0:NT], ALU.add).then_inc(S(f"bank_free{s}"), 1)
            return read

        splits = [(oT[:, 0:4, :], 0), (oT[:, 4:8, :], 4), (ysT[:, 0:4, :], 8), (ysT[:, 4:8, :], 12)]
        m_splits = [(mT[:, t:t + 4, :], t) for t in range(0, KT, 4)]
        with program() as block:
            @block.sync
            def _(sp):
                sp.dma_start(xT[:, :, :], x_dram).then_inc(S("x_back"), 16)
                for job in (job_mg, job_ao, job_glu, job_out):
                    stream(sp, job)

            @block.tensor
            def _(pe):
                products(pe, job_mg, hi, lo)
                pe.wait_ge(S("oy_split"), 4)
                products(pe, job_ao, hi, lo)
                products(pe, job_glu, hi, lo, 8)
                pe.wait_ge(S("m_split"), 4)
                products(pe, job_out, hi, lo)

            @block.scalar
            def _(act):
                def gate(i, s):
                    full(act, job_mg, i, s)
                    nc.scalar.activation(tile_of(sgm, i * 2 + s), PS[s][:, 0:NT], ACT.Sigmoid).then_inc(S(f"bank_free{s}"), 1)

                def glu_gate(i, s):
                    if s:
                        full(act, job_glu, i, 1)
                        act.wait_ge(S("sb_used"), i + 1)
                        nc.scalar.activation(sB, PS[1][:, 0:NT], ACT.Sigmoid).then_inc(S("bank_free1"), 1)

                def round_all(pieces, done):
                    for src, t in pieces:
                        nc.scalar.copy(actr[:, 0, t:t + 4, :], src).then_inc(S(done), 1)

                follow(act, [job_mg], round_tile, [gate])
                round_all(splits, "oy_rounded")
                follow(act, [job_ao, job_glu], round_tile, [None, glu_gate])
                act.wait_ge(S("m_ready"), 17)
                round_all(m_splits, "m_rounded")
                follow(act, [job_out], round_tile, [None])

            @block.vector
            def _(dve):
                V = nc.vector

                def rest_all(pieces, rounded, done):
                    for n, (src, t) in enumerate(pieces):
                        dve.wait_ge(S(rounded), n + 1)
                        V.tensor_tensor(actr[:, 1, t:t + 4, :], src, actr[:, 0, t:t + 4, :].bitcast(F32), ALU.subtract).then_inc(S(done), 1)

                def branch_a(i, s):
                    full(dve, job_ao, i, s)
                    V.tensor_tensor(tile_of(mT, i * 2 + s), PS[s][:, 0:NT], tile_of(sgm, i * 2 + s), ALU.mult).then_inc(S(f"bank_free{s}"), 1)

                def branch_b(i, s):
                    if s == 0:
                        full(dve, job_glu, i, 0)
                        dve.wait_ge(S("m_ready"), i + 1)
                        V.tensor_tensor(tmp, PS[0][:, 0:NT], tile_of(sgm, i + 16), ALU.mult).then_inc(S("bank_free0"), 1)
                    else:
                        dve.wait_ge(S("bank_free1"), i + (job_glu.base + 2))
                        dve.wait_ge(S("bank_free0"), i + (job_glu.base + 2))
                        V.tensor_tensor(tmp, tmp, sB, ALU.mult).then_inc(S("sb_used"), 1)
                        dve.wait_ge(S("sb_used"), i + 2)
                        V.tensor_tensor(tile_of(mT, i), tile_of(mT, i), tmp, ALU.add).then_inc(S("m_ready"), 1)

                follow(dve, [job_mg], rest_tile, [None])
                for s in range(2):
                    dve.wait_ge(S(f"bank_free{s}"), job_ao.base + 1)
                rest_all(splits, "oy_rounded", "oy_split")
                dve.sem_inc(S("sb_used"), 1)
                dve.sem_inc(S("m_ready"), 1)
                follow(dve, [job_ao, job_glu], rest_tile, [branch_a, branch_b])
                rest_all(m_splits, "m_rounded", "m_split")
                dve.wait_ge(S("x_back"), 16)
                follow(dve, [job_out], rest_tile, [add_to_x(dve, job_out)])

        last.close()
        hid = phase.enter_context(nc.sbuf_tensor("hid", [P, 2, FK, NT], F32R))
        open_arena(phase, "arena5")
        take = scratch()
        yT = take(KT * NT).rearrange("p (t n) -> p t n", t=KT)
        sB = take(NT)
        tmp = take(NT)
        yrow = [take(1024) for _ in range(2)]
        outputs = [(y_prompt[0, 0:P], P), (y_prompt[0, P:SEQ], P), (y_sample.rearrange("b t d -> (b t) d"), TOK[2])]
        with program() as block:
            @block.sync
            def _(sp):
                for c in range(FC):
                    stream(sp, job_ffn[c])
                    stream(sp, job_down[c])
                for t, (dst, rows) in enumerate(outputs):
                    for c in range(2):
                        sp.wait_ge(S("y_copied_out"), 4 * t + 2 * c + 2)
                        sp.dma_start(dst[:, c * 1024:(c + 1) * 1024], yrow[c][0:rows, :]).then_inc(S(f"yrow_stored{c}"), 16)
                for c in range(2):
                    sp.wait_ge(S(f"yrow_stored{c}"), 48)

            @block.tensor
            def _(pe):
                norm_sum(pe, norm2)
                pe.wait_ge(S("h_ready"), KT)
                for c in range(FC):
                    products(pe, job_ffn[c], hi, lo)
                    pe.wait_ge(S("hid_ready"), FK * (c + 1) + 1)
                    products(pe, job_down[c], hid[:, 0], hid[:, 1])
                pe.wait_ge(S("x3_ready"), 1)
                norm_sum(pe, norm3)
                pe.wait_ge(S("y_ready"), KT)
                for n in range(12):
                    t, c = n // 4, n % 4
                    if n >= 2:
                        pe.wait_ge(S("y_copied_out"), n - 1)
                    for j in range(4):
                        tr = nc.tensor.transpose(PS[4 + n % 2][0:TOK[t], j * P:(j + 1) * P], yT[:, 4 * c + j, t * P:t * P + TOK[t]], ident)
                    tr.then_inc(S("y_turned"), 1)

            @block.scalar
            def _(act):
                norm_squares(act, norm2, xT)
                norm_root(act, norm2)
                norm_split_round(act)

                def silu(c):
                    def read(i, s):
                        if s == 0:
                            full(act, job_ffn[c], i, 0)
                            act.wait_ge(S("silu_used"), i + (FK * c + 1))
                            nc.scalar.activation(sB, PS[0][:, 0:NT], ACT.Silu).then_inc(S("bank_free0"), 1)
                    return read

                jobs, reads = [], []
                for c in range(FC):
                    jobs += [job_ffn[c], job_down[c]]
                    reads += [silu(c), None]
                follow(act, jobs, round_tile, reads)
                act.wait_ge(S("x3_ready"), 1)
                norm_squares(act, norm3, xT)
                norm_root(act, norm3)

            @block.vector
            def _(dve):
                V = nc.vector
                norm_rstd(dve, norm2)
                norm_split_rest(dve, xT, 1)
                dve.sem_inc(S("silu_used"), 1)
                dve.sem_inc(S("hid_ready"), 1)

                def gated(c):
                    def read(i, s):
                        if s:
                            n = FK * c
                            full(dve, job_ffn[c], i, 1)
                            dve.wait_ge(S("bank_free0"), i + (job_ffn[c].base + 2))
                            dve.wait_ge(S("hid_ready"), i + (n + 1))
                            V.tensor_tensor(tmp, PS[1][:, 0:NT], sB, ALU.mult).then_inc(S("silu_used"), 1)
                            dve.wait_ge(S("silu_used"), i + (n + 2))
                            V.tensor_copy(hid[:, 0, bass.ds(i, 1), :].rearrange("p a n -> p (a n)"), tmp).then_inc(S("bank_free1"), 1)
                            dve.wait_ge(S("bank_free1"), i + (job_ffn[c].base + 2))
                            V.tensor_tensor(hid[:, 1, bass.ds(i, 1), :].rearrange("p a n -> p (a n)"), tmp,
                                            hid[:, 0, bass.ds(i, 1), :].rearrange("p a n -> p (a n)").bitcast(F32), ALU.subtract).then_inc(S("hid_ready"), 1)
                    return read

                jobs, reads = [], []
                for c in range(FC):
                    jobs += [job_ffn[c], job_down[c]]
                    reads += [gated(c), add_to_x(dve, job_down[c])]
                follow(dve, jobs, rest_tile, reads)
                for s in range(2):
                    dve.wait_ge(S(f"bank_free{s}"), steps_before[0] + 1)
                dve.sem_inc(S("x3_ready"), 1)
                norm_rstd(dve, norm3)
                for k in range(KT):
                    norm_scale(dve, xT, yT[:, k, :], 2, k, "y_ready")
                for n in range(12):
                    t, c = n // 4, n % 4
                    dve.wait_ge(S("y_turned"), n + 1)
                    if t:
                        dve.wait_ge(S(f"yrow_stored{c // 2}"), 16 * t)
                    V.tensor_copy(yrow[c // 2][0:TOK[t], (c % 2) * 512:(c % 2 + 1) * 512], PS[4 + n % 2][0:TOK[t], :]).then_inc(S("y_copied_out"), 1)
        phase.close()


_INS = ["x_prompt", "x_sample", "cache_kv", "state_win", "state_ssm_re", "state_ssm_im", "page_table", "g_mix", "w_in",
        "w_cmp_pe", "w_cmp_pool", "w_cmp_phi", "w_attn_out", "ssm_lam_re", "ssm_lam_im", "ssm_log_dt", "ssm_b_re",
        "ssm_b_im", "ssm_c_re", "ssm_c_im", "ssm_d", "w_glu", "w_out", "g_ffn", "w_gate", "w_up", "w_down", "g_final"]
_MATRICES = {"w_in", "w_attn_out", "w_glu", "w_out", "w_gate", "w_up", "w_down"}
_OUTS = [(1, SEQ, DM), (NB, NQ, DM), (1, 1, SEQ, 4, NKV, HD), (1, 1, SEQ, 2, NKV, HD), (1, 1, NG, NS), (1, 1, NG, NS),
         (1, NB, NQ, 4, NKV, HD), (1, NB, WIN, 2, NKV, HD), (1, NB, NG, NS), (1, NB, NG, NS)]


def kernel(**inputs):
    import concourse.bacc as _bacc
    from concourse.bass_utils import run_bass_kernel_spmd as _run

    nc = _bacc.Bacc("TRN2", target_bir_lowering=False, num_devices=1)
    arrays, ins, outs = {}, [], []
    given = {name: np.ascontiguousarray(inputs[name]) for name in _INS}
    given["small_constants"] = small_constants()[0]
    given["key_biases"] = key_biases()
    for name, a in given.items():
        arrays[f"in_{name}_dram"] = a
        ap = nc.dram_tensor(f"in_{name}_dram", a.shape, mybir.dt.from_np(a.dtype), kind="ExternalInput").ap()
        ins.append(ap[0] if name in _MATRICES else ap)
    for i, shape in enumerate(_OUTS):
        outs.append(nc.dram_tensor(f"out_{i}_dram", shape, F32, kind="ExternalOutput").ap())
    build(nc, ins, outs)
    r = _run(nc, [arrays], core_ids=[0])
    return tuple(r.results[0][f"out_{i}_dram"] for i in range(len(_OUTS)))
```

```python
from contextlib import ExitStack, contextmanager

import numpy as np
import concourse.bass as bass
from concourse import mybir

F32 = mybir.dt.float32
F32R = mybir.dt.float32r
I32 = mybir.dt.int32
ALU = mybir.AluOpType
ACT = mybir.ActivationFunctionType
AX_X = mybir.AxisListType.X

P = 128
DM = 2048
SEQ = 256
NB, NQ = 8, 8
NT = SEQ + NB * NQ
KT = DM // P
NH, HD, NKV, GRP = 16, 64, 4, 4
PAST, PAGE = 2048, 128
NPG = PAST // PAGE
WIN = 512
NG, NS, CH = 64, 64, 16
SSMW = NG * CH
DFF = 5632
FT = DFF // P
L = 8
NCH = NT // L
NPC = SEQ // L
GH = NG // 2
EPS = 1e-6
BIG = 1e30
FORCED = 1e4
NC_P = 15
NC_S = 127
NBLK = 33
SC = 0.125
C_Q, C_KV, C_GT, C_U, C_MG = 0, 1024, 2560, 2608, 3632
TWO_PI_HI = 6.28125
TWO_PI_LO = float(np.float32(2 * np.pi - 6.28125))
MAGIC = 12582912.0


def slope(h):
    return float(2.0 ** (-8.0 * (h + 1) / NH))


def small_constants():
    r = np.arange(P)
    parts = {}
    parts["ident"] = np.eye(P)
    parts["same"] = ((r[:, None] // 32 == r[None, :] // 32) & (r[:, None] % 8 == r[None, :] % 8))
    k = np.arange(SEQ)
    d = 128 + r[:, None] - k[None, :]
    parts["half"] = r[:, None] // 64 == np.arange(2)[None, :]
    parts["distp"] = np.where(d >= 0, d, BIG)
    end = np.arange(NC_P) * 16 + 31
    bias, valid = [], []
    for qt in range(2):
        q = qt * 128 + r
        dist = q[:, None] - end[None, :]
        ok = dist >= 0
        valid.append(ok)
        for h in range(NH):
            bias.append(np.where(ok, -np.float32(slope(h)) * dist, -BIG))
    parts["biascp"] = np.concatenate(bias, 1)
    parts["validcp"] = np.concatenate(valid, 1)
    c = np.arange(P) * 16
    s = np.arange(NBLK) * 64
    parts["overlap"] = (c[:, None] < s[None, :] + 64) & (c[:, None] + 31 >= s[None, :])
    m = np.zeros((P, 3, P))
    for br in range(3):
        for h in range(NH):
            m[br * NH + h, br, h * 8:h * 8 + 8] = 1
    parts["gatesel"] = m.reshape(P, -1)
    parts["qmask"] = r[:, None] % 8 == np.arange(8)[None, :]
    parts["submask"] = r[:, None] // 16 == np.arange(8)[None, :]
    parts["chandiag"] = r[:, None] % 16 == np.arange(16)[None, :]
    h, q = r // 8, r % 8
    sl = np.array([slope(x) for x in h], np.float32)[:, None]
    parts["biascs"] = -sl * (2048 + q[:, None] - (np.arange(NC_S) * 16 + 31)[None, :]).astype(np.float32)
    at, cols = {}, 0
    for name, a in parts.items():
        at[name] = (cols, cols + a.shape[1])
        cols += a.shape[1]
    return np.concatenate([np.asarray(a, np.float32) for a in parts.values()], 1), at


def key_biases():
    r = np.arange(P)
    q = r % 8
    sl = np.array([slope(x) for x in r // 8], np.float32)[:, None]
    d = 2048 + q[:, None] - np.arange(PAST + NQ)[None, :]
    sel = np.where(d >= 0, -sl * d.astype(np.float32), -BIG)
    d = 512 + q[:, None] - np.arange(WIN + NQ)[None, :]
    win = np.where((d >= 0) & (d < WIN), -sl * d.astype(np.float32), -BIG)
    return np.concatenate([sel, win], 1).astype(np.float32)


_, CAT = small_constants()
CW = max(b for _, b in CAT.values())


def build(nc, ins, outs):
    (x_prompt, x_sample, cache_kv, state_win, h0_re, h0_im, page_table, g_mix, w_in, w_pe, w_pool, w_phi,
     w_ao, lam_re, lam_im, log_dt, b_re, b_im, c_re, c_im, ssm_d, w_glu, w_out, g_ffn, w_gate, w_up,
     w_down, g_final, consts, kbias) = ins
    (y_prompt, y_sample, kvr_prompt, win_prompt, sre_prompt, sim_prompt, kvr_sample, win_sample,
     sre_sample, sim_sample) = outs
    with ExitStack() as ctx:
        def sb(name, shape, dt=F32):
            return ctx.enter_context(nc.sbuf_tensor(name, shape, dt))

        sems, blocks = {}, [0]

        lasting = ("raw_landed", "hi_ready", "split_ready", "tile_full", "bank_free", "square_", "mean_ready",
                   "root_ready", "rstd_ready", "stored", "y_stored", "x_spilled", "sg_stored")

        def S(name):
            if name not in sems:
                sems[name] = nc.alloc_semaphore(name if name.startswith(lasting) else f"{name}_{blocks[0]}")
            return sems[name]

        @contextmanager
        def program():
            with nc.Block() as block:
                yield block
            own = [n for n in sems if not n.startswith(lasting)]
            nc.clear_and_free_semaphores([sems.pop(n) for n in own])
            nc.all_engine_barrier()
            blocks[0] += 1

        PS = [ctx.enter_context(nc.psum_tensor(f"bank{i}", [P, 512], F32)) for i in range(8)]
        ctx.enter_context(nc.allow_non_contiguous_dma(reason="small parameter tables"))

        actr = sb("actr", [P, 2, KT, NT], F32R)
        cst = sb("cst", [P, CW])
        ones = sb("ones", [P, P])
        xT = sb("xT", [P, KT, NT])
        oT = sb("oT", [P, 8, NT])
        ysT = sb("ysT", [P, 8, NT])
        gcol = sb("gcol", [P, 48])
        gN = sb("gN", [P, 2, 48])
        gS = sb("gS", [P, 3, NB])
        poolw = sb("poolw", [P, 2, 2, 8])
        pec = sb("pec", [P, 2])
        phi = sb("phi", [P, 2, P])
        qs = sb("qs", [P, 8, NB * NQ])
        ks = sb("ks", [P, 4, NB * NQ])
        rstd = sb("rstd", [P, NT])
        sq = sb("sq", [P, 2, NT])
        kept = ctx.enter_context(ExitStack())
        raw, w_hi, w_lo = [], [], []
        place = {}

        def open_weights(stack, name):
            for s in range(2):
                for slots, kind, dt in ((raw, "raw", F32), (w_hi, "hi", F32R), (w_lo, "lo", F32R)):
                    slots[s:s + 1] = [stack.enter_context(nc.sbuf_tensor(f"{name}_{kind}{s}", [P, KT * P], dt))]

        def open_arena(stack, name):
            left = nc.sbuf_bytes_remaining
            size = (left() if callable(left) else left) // 4 - 16
            place["size"] = size
            place["arena"] = stack.enter_context(nc.sbuf_tensor(name, [P, size], F32))

        def C(name, rows=P):
            a, b = CAT[name]
            return cst[0:rows, a:b]

        def scratch(region=None, size=None):
            if region is None:
                region, size = place["arena"][:, :], place["size"]
            at = [0]

            def take(width):
                a = at[0]
                at[0] += width
                assert at[0] <= size, at[0]
                return region[:, a:a + width]
            return take

        ident = C("ident")
        u_dram = nc.dram_tensor("u_scratch", [NT, SSMW], F32).ap()
        x_dram = nc.dram_tensor("x_scratch", [P, KT, NT], F32).ap()
        sg_dram = nc.dram_tensor("gate_scratch", [P, 32, NT], F32).ap()
        y_dram = nc.dram_tensor("y_scratch", [NT, SSMW], F32).ap()

        steps_before = [0]
        dmas_before = [0]

        class Job:
            def __init__(self, n, kt, columns, dmas=1, joined=False, wide=1):
                self.n, self.kt, self.columns, self.dmas, self.joined = n, kt, columns, dmas, joined
                self.wide, self.width = wide, wide * P
                self.base, self.landed = steps_before[0], dmas_before[0]
                steps_before[0] += n
                dmas_before[0] += n * dmas * 16

        def load_tile(eng, job, i, s, slot_queue=None):
            eng.wait_ge(S(f"split_ready{s}"), i + (job.base + 1))
            slot = raw[s][:, 0:job.kt * job.width].rearrange("p (k c) -> p k c", k=job.kt)
            views = job.columns(i, s)
            w = job.width // len(views)
            for n, v in enumerate(views):
                eng.dma_start(slot[:, :, n * w:(n + 1) * w], v.rearrange("(k p) c -> p k c", p=P)).then_inc(S(f"raw_landed{s}"), 16)

        def stream(sp, job):
            with sp.Fori(0, job.n) as i:
                for s in range(2):
                    load_tile(sp, job, i, s)

        def round_tile(act, job, i, s):
            act.wait_ge(S(f"raw_landed{s}"), i * (16 * job.dmas) + (job.landed + 16 * job.dmas))
            act.wait_ge(S(f"tile_full{s}"), i + (job.base + 1))
            nc.scalar.copy(w_hi[s][:, 0:job.kt * job.width], raw[s][:, 0:job.kt * job.width]).then_inc(S(f"hi_ready{s}"), 1)

        def rest_tile(dve, job, i, s):
            dve.wait_ge(S(f"hi_ready{s}"), i + (job.base + 1))
            nc.vector.tensor_tensor(w_lo[s][:, 0:job.kt * job.width], raw[s][:, 0:job.kt * job.width],
                                    w_hi[s][:, 0:job.kt * job.width].bitcast(F32),
                                    ALU.subtract).then_inc(S(f"split_ready{s}"), 1)

        def multiply(pe, job, i, s, hi, lo, k0=0):
            pe.wait_ge(S(f"split_ready{s}"), i + (job.base + 2))
            if not (job.joined and s):
                pe.wait_ge(S(f"bank_free{s}"), i + (job.base + 1))
            for side in range(job.wide):
                bank = PS[0 if job.joined else s + 2 * side]
                first = not (job.joined and s)
                final = not (job.joined and not s)
                for k in range(job.kt):
                    kk = k0 + k + (job.kt if job.joined and s else 0)
                    at = k * job.width + side * P
                    for m, (w, x) in enumerate(((w_hi, hi), (w_hi, lo), (w_lo, hi))):
                        mm = pe.matmul(bank[:, 0:NT], w[s][:, at:at + P], x[:, kk, :],
                                       start=first and k == 0 and m == 0, stop=final and k == job.kt - 1 and m == 2)
            mm.then_inc(S(f"tile_full{s}"), 1)

        def products(pe, job, hi, lo, k0=0):
            with pe.Fori(0, job.n) as i:
                for s in range(2):
                    multiply(pe, job, i, s, hi, lo, k0)

        def full(eng, job, i, s):
            eng.wait_ge(S(f"tile_full{s}"), i + (job.base + 2))

        def follow(eng, jobs, split, reads):
            def read(job, fn, i, s):
                if fn:
                    fn(i, s)

            split(eng, jobs[0], 0, 0)
            for n, (job, fn) in enumerate(zip(jobs, reads)):
                if job.n > 1:
                    with eng.Fori(0, job.n - 1) as i:
                        split(eng, job, i, 1)
                        read(job, fn, i, 0)
                        split(eng, job, i + 1, 0)
                        read(job, fn, i, 1)
                split(eng, job, job.n - 1, 1)
                read(job, fn, job.n - 1, 0)
                if n + 1 < len(jobs):
                    split(eng, jobs[n + 1], 0, 0)
                read(job, fn, job.n - 1, 1)

        def plain(w, col0=0):
            return lambda i, s: [w[:, bass.ds(i * 256 + (s * P + col0), P)]]

        def halves(i, s):
            return [w_in[s * 1024:(s + 1) * 1024, C_GT:C_GT + P]]

        FC, FK = 4, FT // 4

        def q_job_columns(gp):
            return lambda i, s: [w_in[:, bass.ds(i * 2 * HD + (8 * gp + 4 * half + s) * HD, HD)] for half in range(2)]

        job_q = [Job(2, KT, q_job_columns(gp), dmas=2) for gp in range(2)]
        job_kv = Job(6, KT, plain(w_in, C_KV))
        job_gt = Job(1, 8, halves, joined=True)
        job_u = Job(4, KT, plain(w_in, C_U))
        job_mg = Job(16, KT, plain(w_in, C_MG))
        job_ao = Job(4, 8, lambda i, s: [w_ao[:, bass.ds(i * 512 + s * 256, 256)]], wide=2)
        job_glu = Job(8, 8, lambda i, s: [w_glu[:, bass.ds(i * 256 + (s * P + c), P)] for c in (0, DM)], dmas=2, wide=2)
        job_out = Job(8, KT, plain(w_out))
        job_ffn, job_down = [], []
        for c in range(FC):
            job_ffn.append(Job(FK, KT, lambda i, s, c=c: [(w_gate, w_up)[s][:, bass.ds(i * P + c * FK * P, P)]]))
            job_down.append(Job(8, FK, lambda i, s, c=c: [w_down[c * FK * P:(c + 1) * FK * P, bass.ds(i * 256 + s * P, P)]]))

        norms = [0]

        class Norm:
            def __init__(self):
                self.n = norms[0]
                norms[0] += 1

        def norm_squares(act, nm, src):
            for k in range(KT):
                if nm.n * KT + k >= 2:
                    act.wait_ge(S("square_used"), nm.n * KT + k - 1)
                nc.scalar.activation(sq[:, k % 2, :], src[:, k, :], ACT.Square).then_inc(S("square_ready"), 1)

        def norm_sum(pe, nm):
            if nm.n:
                pe.wait_ge(S("mean_ready"), nm.n)
            for k in range(KT):
                pe.wait_ge(S("square_ready"), nm.n * KT + k + 1)
                mm = pe.matmul(PS[7][:, 0:NT], ones[:, :], sq[:, k % 2, :], start=k == 0, stop=k == KT - 1)
                mm.then_inc(S("square_used"), 1)

        def norm_rstd(dve, nm):
            dve.wait_ge(S("square_used"), (nm.n + 1) * KT)
            nc.vector.tensor_scalar(rstd[:, :], PS[7][:, 0:NT], 1.0 / DM, EPS, ALU.mult, ALU.add).then_inc(S("mean_ready"), 1)
            dve.wait_ge(S("root_ready"), nm.n + 1)
            nc.vector.reciprocal(rstd[:, :], rstd[:, :]).then_inc(S("rstd_ready"), 1)
            dve.wait_ge(S("rstd_ready"), nm.n + 1)

        def norm_scale(dve, src, dst, gc, k, done):
            nc.vector.scalar_tensor_tensor(out=dst, in0=src[:, k, :], scalar=gcol[:, gc * KT + k:gc * KT + k + 1],
                                           in1=rstd[:, :], op0=ALU.mult, op1=ALU.mult).then_inc(S(done), 1)

        def norm_split_scale(dve, src, gc):
            for k in range(KT):
                if k >= 2:
                    dve.wait_ge(S("h_ready"), k - 1)
                norm_scale(dve, src, sq[:, k % 2, :], gc, k, "normed")

        def norm_split_rest(pool):
            for k in range(KT):
                pool.wait_ge(S("h_rounded"), k + 1)
                nc.gpsimd.tensor_tensor(actr[:, 1, k, :], sq[:, k % 2, :], actr[:, 0, k, :].bitcast(F32), ALU.subtract).then_inc(S("h_ready"), 1)

        def norm_split_round(act):
            for k in range(KT):
                act.wait_ge(S("normed"), k + 1)
                nc.scalar.copy(actr[:, 0, k, :], sq[:, k % 2, :]).then_inc(S("h_rounded"), 1)

        def norm_root(act, nm):
            act.wait_ge(S("mean_ready"), nm.n + 1)
            nc.scalar.activation(rstd[:, :], rstd[:, :], ACT.Sqrt).then_inc(S("root_ready"), 1)

        norm1, norm2, norm3 = Norm(), Norm(), Norm()

        kvT = kept.enter_context(nc.sbuf_tensor("kvT", [P, 12, NT], F32))
        qT = kept.enter_context(nc.sbuf_tensor("qT", [P, 8, NT], F32))
        uT = oT
        phase = ExitStack()
        open_weights(phase, "w1")
        open_arena(phase, "arena1")
        take = scratch()
        xrow = take(3 * DM).rearrange("p (t n) -> p t n", t=3)
        gT = take(NT)
        grow = take(P)
        TOK = [P, P, NT - 2 * P]

        with program() as block:
            @block.sync
            def _(sp):
                sp.dma_start(xrow[:, 0, :], x_prompt[0, 0:P, :]).then_inc(S("x_landed"), 16)
                sp.dma_start(xrow[:, 1, :], x_prompt[0, P:SEQ, :]).then_inc(S("x_landed"), 16)
                sp.dma_start(xrow[0:TOK[2], 2, :], x_sample.rearrange("b t d -> (b t) d")).then_inc(S("x_landed"), 16)
                for n, job in enumerate((*job_q, job_kv, job_gt, job_u)):
                    stream(sp, job)
                    if n == 0:
                        sp.wait_ge(S("xt_copied"), 12)
                        sp.dma_start(x_dram, xT[:, :, :]).then_inc(S("x_spilled"), 16)

            @block.gpsimd
            def _(pool):
                nc.gpsimd.memset(ones[:, :], 1.0).then_inc(S("ones_ready"), 1)
                norm_split_rest(pool)

            @block.tensor
            def _(pe):
                pe.wait_ge(S("consts_landed"), 16)
                pe.wait_ge(S("grow_landed"), 48)
                nc.tensor.transpose(PS[6][:, 0:48], grow[0:48, :], ident[0:48, 0:48]).then_inc(S("gcol_full"), 1)
                pe.wait_ge(S("x_landed"), 48)
                n = 0
                for t in range(3):
                    for c in range(KT // 4):
                        if n >= 2:
                            pe.wait_ge(S("xt_copied"), n - 1)
                        for j in range(4):
                            k = 4 * c + j
                            tr = nc.tensor.transpose(PS[4 + n % 2][:, j * P:j * P + TOK[t]],
                                                     xrow[0:TOK[t], t, k * P:(k + 1) * P], ident[0:TOK[t], 0:TOK[t]])
                        tr.then_inc(S("xt_full"), 1)
                        n += 1
                pe.wait_ge(S("ones_ready"), 1)
                norm_sum(pe, norm1)
                pe.sem_inc(S("tile_full0"), 1)
                pe.sem_inc(S("tile_full1"), 1)
                pe.wait_ge(S("h_ready"), KT)
                for job in (*job_q, job_kv, job_gt, job_u):
                    products(pe, job, actr[:, 0], actr[:, 1])
                pe.wait_ge(S("gate_ready"), 1)
                for t in range(2):
                    tr = nc.tensor.transpose(PS[4][:, t * 48:(t + 1) * 48], gT[0:48, t * P:(t + 1) * P], ident[0:48, 0:48])
                tr.then_inc(S("gn_full"), 1)
                for br in range(3):
                    sel = C("gatesel", 48)[:, br * P:(br + 1) * P]
                    mm = pe.matmul(PS[5][:, br * 64:(br + 1) * 64], sel, gT[0:48, SEQ:NT], start=True, stop=True)
                mm.then_inc(S("gs_full"), 1)

            @block.scalar
            def _(act):
                act.dma_start(cst[:, :], consts).then_inc(S("consts_landed"), 16)
                for n, g in enumerate((g_mix, g_ffn, g_final)):
                    src = g if n == 2 else g[0]
                    act.dma_start(grow[n * KT:(n + 1) * KT, :], src.rearrange("(k p) -> k p", p=P)).then_inc(S("grow_landed"), 16)
                for b in range(2):
                    act.sem_inc(S(f"bank_free{b}"), 1)
                act.wait_ge(S("xt_copied"), 12)
                norm_squares(act, norm1, xT)
                norm_root(act, norm1)
                norm_split_round(act)

                def keep_in(dst, t0, scale):
                    def read(i, s):
                        full(act, read.job, i, s)
                        nc.scalar.activation(dst[:, bass.ds(i * 2 + (t0 + s), 1), :].rearrange("p a n -> p (a n)"), PS[s][:, 0:NT],
                                             ACT.Copy, scale=scale).then_inc(S(f"bank_free{s}"), 1)
                    return read

                def gates(i, s):
                    if s:
                        full(act, job_gt, i, s)
                        nc.scalar.activation(gT[0:48, :], PS[0][0:48, 0:NT], ACT.Sigmoid).then_inc(S("bank_free0"), 1)
                        act.wait_ge(S("bank_free0"), job_gt.base + 2)
                        act.sem_inc(S("gate_ready"), 1)
                        act.sem_inc(S("bank_free1"), 1)

                jobs = (*job_q, job_kv, job_gt, job_u)
                reads = (keep_in(qT, 0, SC), keep_in(qT, 4, SC), keep_in(kvT, 0, 1.0), gates, keep_in(uT, 0, 1.0))
                for job, read in zip(jobs, reads):
                    read.job = job
                follow(act, jobs, round_tile, reads)

            @block.vector
            def _(dve):
                for s in range(2):
                    dve.sem_inc(S(f"split_ready{s}"), 1)
                dve.wait_ge(S("gcol_full"), 1)
                nc.vector.tensor_copy(gcol[:, :], PS[6][:, 0:48]).then_inc(S("gcol_copied"), 1)
                n = 0
                for t in range(3):
                    for c in range(KT // 4):
                        dve.wait_ge(S("xt_full"), n + 1)
                        nc.vector.tensor_copy(xT[:, 4 * c:4 * c + 4, t * P:t * P + TOK[t]],
                                              PS[4 + n % 2][:, :].rearrange("p (j n) -> p j n", j=4)[:, :, 0:TOK[t]])\
                            .then_inc(S("xt_copied"), 1)
                        n += 1
                norm_rstd(dve, norm1)
                norm_split_scale(dve, xT, 0)
                jobs = (*job_q, job_kv, job_gt, job_u)
                follow(dve, jobs, rest_tile, (None,) * len(jobs))
                dve.wait_ge(S("gn_full"), 1)
                nc.vector.tensor_copy(gN[:, :, :], PS[4][:, 0:96].rearrange("p (t c) -> p t c", t=2)).then_inc(S("gn_ready"), 1)
                dve.wait_ge(S("gs_full"), 1)
                for br in range(3):
                    nc.vector.tensor_tensor(sq[:, 0, br * 64:(br + 1) * 64].rearrange("p (b q) -> p b q", q=NQ),
                                            PS[5][:, br * 64:(br + 1) * 64].rearrange("p (b q) -> p b q", q=NQ),
                                            C("qmask").unsqueeze(1).broadcast_to([P, NB, NQ]), ALU.mult)\
                        .then_inc(S("gs_masked"), 1)
                dve.wait_ge(S("gs_masked"), 3)
                nc.vector.tensor_reduce(gS[:, :, :], sq[:, 0, 0:192].rearrange("p (r b q) -> p r b q", r=3, q=NQ), AX_X, ALU.add)\
                    .then_inc(S("gs_ready"), 1)

        phase.close()
        open_arena(phase, "arena2")
        take = scratch()
        kvn = take(3 * 1536).rearrange("p (t n) -> p t n", t=3)
        un = take(3 * SSMW).rearrange("p (t n) -> p t n", t=3)
        turns = [(kvT, t, c, kvn) for t in range(3) for c in range(3)] + [(uT, t, c, un) for t in range(3) for c in range(2)]
        with program() as block:
            @block.tensor
            def _(pe):
                for n, (src, t, c, _) in enumerate(turns):
                    if n >= 4:
                        pe.wait_ge(S(("turned_dve", "turned_act")[n % 2]), n // 2 - 1)
                    for j in range(4):
                        tr = nc.tensor.transpose(PS[4 + n % 4][0:TOK[t], j * P:(j + 1) * P],
                                                 src[:, 4 * c + j, t * P:t * P + TOK[t]], ident)
                    tr.then_inc(S("turn_full"), 1)

            def copy_turns(eng, parity, copy, done):
                for n, (_, t, c, dst) in enumerate(turns):
                    if n % 2 == parity:
                        eng.wait_ge(S("turn_full"), n + 1)
                        copy(dst[0:TOK[t], t, c * 512:(c + 1) * 512], PS[4 + n % 4][0:TOK[t], :]).then_inc(S(done), 1)

            @block.vector
            def _(dve):
                copy_turns(dve, 0, nc.vector.tensor_copy, "turned_dve")

            @block.scalar
            def _(act):
                copy_turns(act, 1, nc.scalar.copy, "turned_act")

            @block.sync
            def _(sp):
                sp.wait_ge(S("turned_dve"), 5)
                sp.wait_ge(S("turned_act"), 4)
                for t in range(2):
                    sp.dma_start(kvr_prompt[0, 0, t * P:(t + 1) * P].rearrange("t a g d -> t (a g d)"),
                                 kvn[:, t, 0:1024]).then_inc(S("kv_stored"), 16)
                    sp.dma_start(win_prompt[0, 0, t * P:(t + 1) * P].rearrange("t a g d -> t (a g d)"),
                                 kvn[:, t, 1024:1536]).then_inc(S("kv_stored"), 16)
                sp.dma_start(kvr_sample[0].rearrange("b t a g d -> (b t) (a g d)"), kvn[0:64, 2, 0:1024]).then_inc(S("kv_stored"), 16)
                for b in range(NB):
                    sp.dma_start(win_sample[0, b, WIN - NQ:WIN].rearrange("t a g d -> t (a g d)"),
                                 kvn[b * NQ:(b + 1) * NQ, 2, 1024:1536]).then_inc(S("kv_stored"), 16)
                sp.wait_ge(S("turned_dve"), 8)
                sp.wait_ge(S("turned_act"), 7)
                for t in range(3):
                    sp.dma_start(u_dram[t * P:t * P + TOK[t]], un[0:TOK[t], t, :]).then_inc(S("u_stored"), 16)
                sp.wait_ge(S("u_stored"), 48)
                sp.wait_ge(S("kv_stored"), 13 * 16)
                sp.wait_ge(S("x_spilled"), 16)

        PG, NPART = 8, GH // 8
        take = scratch()
        urows = [take(L * PG * 32).rearrange("p (s c) -> p s c", s=L) for _ in range(2)]
        Q = [take(2 * PG * 9 * CH).rearrange("p (r g k c) -> p r g k c", r=2, g=PG, k=9) for _ in range(2)]
        Tt = [take(2 * PG * P).rearrange("p (h g n) -> p h g n", h=2, g=PG) for _ in range(2)]
        Ga_flat = take(PG * P)
        Ga = Ga_flat.rearrange("p (g n) -> p g n", g=PG)
        UTa_flat = take(GH * 80)
        UTa = UTa_flat.rearrange("p (g n) -> p g n", g=GH)
        Bb = take(2 * GH * CH).rearrange("p (r g c) -> p r g c", r=2, g=GH)
        Ct = take(2 * GH * CH).rearrange("p (r g c) -> p r g c", r=2, g=GH)
        PK = take(2 * 9 * GH).rearrange("p (r k g) -> p r k g", r=2, k=9)
        NPI = take(9 * GH).rearrange("p (k g) -> p k g", k=9)
        NPR = take(9 * GH).rearrange("p (k g) -> p k g", k=9)
        RK = take(2 * GH * L).rearrange("p (r g s) -> p r g s", r=2, g=GH)
        H0 = take(2 * NB * GH).rearrange("p (r b g) -> p r b g", r=2, b=NB)
        FinP = take(2 * GH).rearrange("p (r g) -> p r g", r=2)
        dcol = take(GH)
        ust = [take(256).rearrange("p (h s c) -> p h s c", h=2, s=L) for _ in range(2)]
        Bst = [take(64).rearrange("p (r h c) -> p r h c", r=2, h=2) for _ in range(2)]
        stg = [take(336) for _ in range(2)]
        sc = take(3 * 2 * GH).rearrange("p (t r g) -> p t r g", t=3, r=2)
        take_x = scratch(xT[:, :, :].rearrange("p k n -> p (k n)"), KT * NT)
        ea = take_x(NCH * 2 * GH).rearrange("p (c r g) -> p c r g", c=NCH, r=2)
        Ha = take_x(NCH * 2 * GH).rearrange("p (c r g) -> p c r g", c=NCH, r=2)
        take_ys = scratch(ysT[:, :, :].rearrange("p k n -> p (k n)"), 8 * NT)
        stg_fin = take_ys(2 * 3 * P).rearrange("p (r t n) -> p r t n", r=2, t=3)
        EB = [take_ys(256).rearrange("p (r s c) -> p r s c", r=2, s=L) for _ in range(4)]
        tA, tB = ([Ga_flat[:, (2 * k + u) * 256:(2 * k + u + 1) * 256].rearrange("p (r s c) -> p r s c", r=2, s=L) for u in range(2)]
                  for k in range(2))
        take_o = scratch(oT[:, :, :].rearrange("p k n -> p (k n)"), 8 * NT)
        t1_flat = take_o(PG * 9 * CH)
        t1 = t1_flat.rearrange("p (g k c) -> p g k c", g=PG, k=9)
        FinS = take_o(2 * NB * GH).rearrange("p (r b g) -> p r b g", r=2, b=NB)
        dI = take_o(PG * CH).rearrange("p (g c) -> p g c", g=PG)
        Hst = [take_o(160).rearrange("p (h r n) -> p h r n", h=2, r=2) for _ in range(2)]
        UTst = [take_o(80) for _ in range(2)]
        par = ysT[:, :, :].rearrange("p k n -> p (k n)")
        Cn = par[:, 0:2048].rearrange("p (r t d s) -> p r t d s", r=2, t=8, d=2)
        par = oT[:, :, :].rearrange("p k n -> p (k n)")
        h0n = par[:, 0:512].rearrange("p (r t n) -> p r t n", r=2, t=2)
        lamn = par[:, 512:896].rearrange("p (a n) -> p a n", a=3)
        ldn = par[:, 896:898]
        Bn = par[:, 1024:2048].rearrange("p (r g c) -> p r g c", r=2, g=GH)
        tp = par[:, 2048:2560].rearrange("p (t g) -> p t g", t=16)
        tb = UTa_flat[:, 0:1024].rearrange("p (t g c) -> p t g c", t=2, g=GH)

        with program() as block:
            @block.sync
            def _(sp):
                for r, c in enumerate((c_re, c_im)):
                    for d in range(2):
                        sp.dma_start(Cn[:, r, :, d, :], c[0].rearrange("(t g) c p -> (g c) t p", g=8)).then_inc(S("cn_landed"), 16)
                for r, h in enumerate((h0_re, h0_im)):
                    sp.dma_start(h0n[:, r, :, :], h[0].rearrange("b g p -> (b g p)").rearrange("(t a n) -> a t n", a=P, n=P))\
                        .then_inc(S("h0_landed"), 16)
                for part in range(NPART):
                    if part >= 2:
                        sp.wait_ge(S("u_staged"), PG * (part - 1))
                    sp.dma_start(urows[part % 2][0:NCH, :, :], u_dram.rearrange("(a s) c -> a s c", s=L)[:, :, part * PG * 32:(part + 1) * PG * 32])\
                        .then_inc(S(f"u_landed{part % 2}"), 16)

                def spread_g(part):
                    sp.wait_ge(S("g_diag"), part + 1)
                    if part >= 2:
                        sp.wait_ge(S("y_full"), PG * (part - 1) + 2)
                    for s in range(L):
                        for h in range(2):
                            sp.dma_start(Tt[part % 2][s * CH:(s + 1) * CH, h, :, s * CH:P], Ga[h * CH:(h + 1) * CH, :, 0:P - s * CH])\
                                .then_inc(S("t_landed"), 16)

                sp.wait_ge(S("t_zero"), 2)
                for part in range(NPART):
                    if part % 2 == 0:
                        spread_g(part)
                        spread_g(part + 1)
                    sp.wait_ge(S("y_copied"), PG * (part + 1) + 2)
                    sp.dma_start(y_dram.rearrange("(a s) c -> a s c", s=L)[:, :, part * PG * 32:(part + 1) * PG * 32],
                                 urows[part % 2][0:NCH, :, :]).then_inc(S(f"y_stored{part % 2}"), 16)
                for r, (op, os) in enumerate(((sre_prompt, sre_sample), (sim_prompt, sim_sample))):
                    sp.wait_ge(S("fin_copied"), r + 1)
                    for t in range(2):
                        sp.dma_start(os[0].rearrange("b g p -> (b g p)").rearrange("(t a n) -> t a n", a=P, n=P)[t],
                                     stg_fin[:, r, t, :]).then_inc(S("stored"), 16)
                    sp.dma_start(op[0, 0].rearrange("(g h) p -> g (h p)", h=2), stg_fin[0:GH, r, 2, :]).then_inc(S("stored"), 16)
                sp.wait_ge(S("stored"), 6 * 16)

            @block.gpsimd
            def _(pool):
                for b in range(2):
                    nc.gpsimd.memset(Tt[b], 0.0).then_inc(S("t_zero"), 1)
                for part in range(NPART):
                    pool.wait_ge(S(f"u_landed{part % 2}"), 16 * (part // 2 + 1))
                    with pool.Fori(0, PG // 2) as i:
                        for u in range(2):
                            n = part * PG + u
                            pool.wait_ge(S("turned"), i * 2 + n + 3)
                            nc.gpsimd.tensor_copy(ust[u][0:NCH], urows[part % 2][0:NCH, :, bass.ds(i * 64 + u * 32, 32)]
                                                  .rearrange("p s (h c) -> p h s c", h=2)).then_inc(S("u_staged"), 1)

                def stage_b(part):
                    with pool.Fori(0, PG // 2) as i:
                        for u in range(2):
                            n = part * PG + u
                            pool.wait_ge(S("g_full"), i * 2 + n + 1)
                            nc.gpsimd.tensor_tensor(Bst[u], Bb[:, :, bass.ds(i * 2 + n, 1), :].broadcast_to([P, 2, 2, CH]),
                                                    C("half").unsqueeze(1).unsqueeze(3).broadcast_to([P, 2, 2, CH]), ALU.mult)\
                                .then_inc(S("b_staged"), 1)
                    if part:
                        pool.wait_ge(S("g_diag"), part)
                    nc.gpsimd.tensor_tensor(dI[0:32], C("chandiag", 32).unsqueeze(1).broadcast_to([32, PG, CH]),
                                            dcol[0:32, part * PG:(part + 1) * PG].unsqueeze(2).broadcast_to([32, PG, CH]), ALU.mult).then_inc(S("d_ready"), 1)
                    pool.wait_ge(S("d_ready"), part + 1)
                    pool.wait_ge(S("g_copied"), PG * (part + 1) + 2)
                    nc.gpsimd.tensor_tensor(Ga[0:32, :, 0:CH], Ga[0:32, :, 0:CH], dI[0:32], ALU.add).then_inc(S("g_diag"), 1)

                pool.wait_ge(S("q_ready"), 1)
                pool.wait_ge(S("d_landed"), 16)
                for half in range(NPART // 2):
                    for part in (2 * half, 2 * half + 1):
                        stage_b(part)
                    pool.wait_ge(S("h_done"), 1)
                    for part in (2 * half, 2 * half + 1):
                        with pool.Fori(0, PG // 2) as i:
                            for u in range(2):
                                n = part * PG + u
                                pool.wait_ge(S("y_full"), i * 2 + n + 1)
                                nc.gpsimd.tensor_copy(UTst[u], UTa[:, bass.ds(i * 2 + n, 1), :].rearrange("p a n -> p (a n)"))
                                nc.gpsimd.tensor_tensor(Hst[u], Ha[:, :, :, bass.ds(i * 2 + n, 1)].rearrange("p c r a -> p a r c").broadcast_to([P, 2, 2, NCH]),
                                                        C("half").unsqueeze(2).unsqueeze(3).broadcast_to([P, 2, 2, NCH]), ALU.mult)\
                                    .then_inc(S("h_staged"), 1)

            @block.tensor
            def _(pe):
                for name, k in (("turned", 4), ("e_full", 2), ("g_full", 2), ("y_full", 2)):
                    pe.sem_inc(S(name), k)
                pe.wait_ge(S("ldt_rows"), 1)
                for a in range(3):
                    tr = nc.tensor.transpose(PS[0][:, a * GH:(a + 1) * GH], lamn[0:GH, a, :], ident[0:GH, 0:GH])
                tr.then_inc(S("lam_full"), 1)
                pe.wait_ge(S("cn_landed"), 64)
                for r in range(2):
                    for t in range(8):
                        tr = nc.tensor.transpose(PS[4 + 2 * r + t // 4][:, (t % 4) * P:(t % 4 + 1) * P],
                                                 Cn[:, r, t, :, :].rearrange("p d s -> p (d s)"), ident)
                tr.then_inc(S("ct_full"), 1)
                pe.wait_ge(S("h0_landed"), 32)
                for r in range(2):
                    for t in range(2):
                        tr = nc.tensor.transpose(PS[1][:, (2 * r + t) * P:(2 * r + t + 1) * P], h0n[:, r, t, :], ident)
                tr.then_inc(S("h0_full"), 1)
                pe.wait_ge(S("ct_ready"), 1)

                def turn_pair(m, u):
                    bank = PS[4 + u % 2]
                    pe.wait_ge(S("u_staged"), m + 1)
                    pe.wait_ge(S("eb_ready"), m + 1)
                    pe.wait_ge(S("e_staged"), m + 1)
                    for r in range(2):
                        nc.tensor.transpose(bank[:, r * P:(r + 1) * P], EB[u][:, r].rearrange("p s c -> p (s c)"), ident)
                    for h in range(2):
                        tr = nc.tensor.transpose(bank[:, 256 + h * NCH:256 + (h + 1) * NCH],
                                                 ust[u % 2][0:NCH, h].rearrange("p s c -> p (s c)"), ident[0:NCH, 0:NCH])
                    tr.then_inc(S("turned"), 1)

                def multiply_pair(m, u):
                    pe.wait_ge(S("e_staged"), m + 3)
                    pe.wait_ge(S("e_copied"), m + 1)
                    for h in range(2):
                        for r in range(2):
                            mm = pe.matmul(PS[6 + u % 2][h * 64:(h + 1) * 64, r * NCH:(r + 1) * NCH],
                                           stg[u % 2][:, r * P + h * 64:r * P + (h + 1) * 64],
                                           stg[u % 2][:, 256 + h * NCH:256 + (h + 1) * NCH], start=True, stop=True)
                    mm.then_inc(S("e_full"), 1)

                for m in range(2):
                    turn_pair(m, m)
                with pe.Fori(0, GH // 4 - 1) as i:
                    for u in range(4):
                        turn_pair(i * 4 + (u + 2), (u + 2) % 4)
                        multiply_pair(i * 4 + u, u)
                for m in range(GH - 4, GH):
                    if m + 2 < GH:
                        turn_pair(m + 2, (m + 2) % 4)
                    multiply_pair(m, m % 4)
                pe.wait_ge(S("e_copied"), GH + 2)

                def taps(part):
                    pe.wait_ge(S("q_ready"), part + 1)
                    with pe.Fori(0, PG // 2) as i:
                        for u in range(2):
                            n = part * PG + u
                            pe.wait_ge(S("b_staged"), i * 2 + n + 1)
                            pe.wait_ge(S("g_copied"), i * 2 + n + 1)
                            for r in range(2):
                                mm = pe.matmul(PS[6 + u][0:32, 0:P], Bst[u][:, r].rearrange("p h c -> p (h c)"),
                                               Q[part % 2][:, r, bass.ds(i * 2 + u, 1), 0:L, :].rearrange("p a k c -> p (a k c)"),
                                               start=r == 0, stop=r == 1)
                            mm.then_inc(S("g_full"), 1)

                def outputs_of(part):
                    pe.wait_ge(S("t_landed"), 256 * (part + 1))
                    with pe.Fori(0, PG // 2) as i:
                        for u in range(2):
                            n = part * PG + u
                            pe.wait_ge(S("h_staged"), i * 2 + n + 1)
                            pe.wait_ge(S("y_copied"), i * 2 + n + 1)
                            for h in range(2):
                                out = PS[4 + u][0:NCH, h * P:(h + 1) * P]
                                pe.matmul(out, UTst[u][:, h * NCH:(h + 1) * NCH],
                                          Tt[part % 2][:, h, bass.ds(i * 2 + u, 1), :].rearrange("p a n -> p (a n)"), start=True, stop=False)
                                for r in range(2):
                                    mm = pe.matmul(out, Hst[u][:, h, r, :],
                                                   Q[part % 2][:, r, bass.ds(i * 2 + u, 1), 1:L + 1, :].rearrange("p a k c -> p (a k c)"),
                                                   start=False, stop=r == 1)
                            mm.then_inc(S("y_full"), 1)

                for half in range(NPART // 2):
                    for stage in (taps, outputs_of):
                        for part in (2 * half, 2 * half + 1):
                            stage(part)
                pe.wait_ge(S("fin_ready"), 1)
                for r in range(2):
                    if r:
                        pe.wait_ge(S("fin_copied"), r)
                    for t in range(2):
                        nc.tensor.transpose(PS[6][:, t * P:(t + 1) * P], FinS[:, r, 4 * t:4 * t + 4, :].rearrange("p b g -> p (b g)"), ident)
                    nc.tensor.transpose(PS[6][0:GH, 256:384], FinP[:, r, :], ident).then_inc(S("fin_full"), 1)

            @block.scalar
            def _(act):
                for name in ("e_staged", "g_copied", "y_copied"):
                    act.sem_inc(S(name), 2)
                for a, lam in enumerate((lam_re, lam_im)):
                    act.dma_start(lamn[0:GH, a, :], lam[0].rearrange("(g h) p -> g (h p)", h=2)).then_inc(S("lam_landed"), 16)
                act.dma_start(ldn[0:GH, :], log_dt[0].rearrange("(g h) -> g h", h=2)).then_inc(S("lam_landed"), 16)
                for r, b in enumerate((b_re, b_im)):
                    for h in range(2):
                        act.dma_start(Bn[h * 64:(h + 1) * 64, r, :, :], b[0].rearrange("(g h) p c -> h p g c", h=2)[h])\
                            .then_inc(S("bn_landed"), 16)
                act.dma_start(dcol[0:32, :], ssm_d[0].rearrange("(g a) -> a g", a=32)).then_inc(S("d_landed"), 16)
                act.wait_ge(S("lam_ready"), 1)
                nc.scalar.activation(tp[:, 3, :], tp[:, 2, :], ACT.Exp).then_inc(S("dt_ready"), 1)
                act.wait_ge(S("arg_ready"), 1)
                nc.scalar.activation(tp[:, 6, :], tp[:, 4, :], ACT.Exp).then_inc(S("mag_ready"), 1)
                act.wait_ge(S("arg_ready"), 2)
                nc.scalar.activation(tp[:, 9, :], tp[:, 7, :], ACT.Sin)
                nc.scalar.activation(tp[:, 10, :], tp[:, 8, :], ACT.Sin).then_inc(S("sin_ready"), 1)
                act.wait_ge(S("ct_ready"), 1)
                with act.Fori(0, GH // 2) as i:
                    for u in range(2):
                        act.wait_ge(S("turned"), i * 2 + (u + 5))
                        act.wait_ge(S("e_full"), i * 2 + (u + 1))
                        nc.scalar.copy(UTa[:, bass.ds(i * 2 + u, 1), :].rearrange("p a n -> p (a n)"), PS[4 + u][:, 256:336])
                        nc.scalar.copy(stg[u], PS[4 + u][:, 0:336]).then_inc(S("e_staged"), 1)
                for half in range(NPART // 2):
                    for part in (2 * half, 2 * half + 1):
                        if part:
                            act.wait_ge(S("t_landed"), 256 * part)
                        with act.Fori(0, PG // 2) as i:
                            for u in range(2):
                                act.wait_ge(S("g_full"), i * 2 + (part * PG + u + 3))
                                nc.scalar.copy(Ga[0:32, bass.ds(i * 2 + u, 1), :].rearrange("p a n -> p (a n)"), PS[6 + u][0:32, 0:P])\
                                    .then_inc(S("g_copied"), 1)
                    for part in (2 * half, 2 * half + 1):
                        if part >= 2:
                            act.wait_ge(S(f"y_stored{part % 2}"), 16 * (part // 2))
                        with act.Fori(0, PG // 2) as i:
                            for u in range(2):
                                act.wait_ge(S("y_full"), i * 2 + (part * PG + u + 3))
                                nc.scalar.copy(urows[part % 2][0:NCH, :, bass.ds(i * 64 + u * 32, 32)].rearrange("p s (h c) -> p h s c", h=2),
                                               PS[4 + u][0:NCH, 0:256].rearrange("p (h s c) -> p h s c", h=2, s=L)).then_inc(S("y_copied"), 1)

            @block.vector
            def _(dve):
                V = nc.vector
                order = [0]

                def link(ins):
                    order[0] += 1
                    ins.then_inc(S("s5_order"), 1)
                    dve.wait_ge(S("s5_order"), order[0])

                dve.sem_inc(S("e_copied"), 2)
                dve.wait_ge(S("lam_landed"), 48)
                V.tensor_copy(lamn[0:GH, 2, :].rearrange("p (h s) -> p h s", h=2),
                              ldn[0:GH, :].unsqueeze(2).broadcast_to([GH, 2, 64])).then_inc(S("ldt_rows"), 1)
                dve.wait_ge(S("lam_full"), 1)
                V.tensor_copy(tp[:, 0:3, :], PS[0][:, 0:96].rearrange("p (a g) -> p a g", a=3)).then_inc(S("lam_ready"), 1)
                dve.wait_ge(S("lam_ready"), 1)
                dve.wait_ge(S("dt_ready"), 1)
                V.tensor_tensor(tp[:, 4, :], tp[:, 0, :], tp[:, 3, :], ALU.mult).then_inc(S("arg_ready"), 1)
                link(V.tensor_tensor(tp[:, 5, :], tp[:, 1, :], tp[:, 3, :], ALU.mult))
                link(V.tensor_scalar(tp[:, 7, :], tp[:, 5, :], float(1 / (2 * np.pi)), MAGIC, ALU.mult, ALU.add))
                link(V.tensor_scalar(tp[:, 7, :], tp[:, 7, :], MAGIC, None, ALU.subtract))
                link(V.scalar_tensor_tensor(out=tp[:, 8, :], in0=tp[:, 7, :], scalar=-TWO_PI_HI, in1=tp[:, 5, :], op0=ALU.mult, op1=ALU.add))
                link(V.scalar_tensor_tensor(out=tp[:, 11, :], in0=tp[:, 7, :], scalar=-TWO_PI_LO, in1=tp[:, 8, :], op0=ALU.mult, op1=ALU.add))
                link(V.tensor_scalar(tp[:, 7, :], tp[:, 11, :], 3.1415925, -3.1415925, ALU.min, ALU.max))
                link(V.tensor_scalar(tp[:, 12, :], tp[:, 7, :], -1.0, None, ALU.mult))
                link(V.tensor_tensor(tp[:, 13, :], tp[:, 12, :], tp[:, 7, :], ALU.max))
                V.tensor_scalar(tp[:, 8, :], tp[:, 13, :], -1.0, float(np.pi / 2), ALU.mult, ALU.add).then_inc(S("arg_ready"), 1)
                dve.wait_ge(S("sin_ready"), 1)
                dve.wait_ge(S("mag_ready"), 1)
                V.tensor_tensor(PK[:, 0, 1, :], tp[:, 6, :], tp[:, 10, :], ALU.mult)
                link(V.tensor_tensor(PK[:, 1, 1, :], tp[:, 6, :], tp[:, 9, :], ALU.mult))
                V.memset(PK[:, 0, 0, :], 1.0)
                V.memset(PK[:, 1, 0, :], 0.0)
                V.tensor_scalar(tp[:, 7, :], PK[:, 0, 1, :], -1.0, None, ALU.add)
                V.tensor_tensor(tp[:, 8, :], tp[:, 0, :], tp[:, 0, :], ALU.mult)
                link(V.tensor_tensor(tp[:, 9, :], tp[:, 1, :], tp[:, 1, :], ALU.mult))
                link(V.tensor_tensor(tp[:, 8, :], tp[:, 8, :], tp[:, 9, :], ALU.add))
                V.reciprocal(tp[:, 9, :], tp[:, 8, :])
                V.tensor_tensor(tp[:, 10, :], tp[:, 7, :], tp[:, 0, :], ALU.mult)
                V.tensor_tensor(tp[:, 11, :], PK[:, 1, 1, :], tp[:, 1, :], ALU.mult)
                V.tensor_tensor(tp[:, 12, :], PK[:, 1, 1, :], tp[:, 0, :], ALU.mult)
                link(V.tensor_tensor(tp[:, 13, :], tp[:, 7, :], tp[:, 1, :], ALU.mult))
                V.tensor_tensor(tp[:, 10, :], tp[:, 10, :], tp[:, 11, :], ALU.add)
                link(V.tensor_tensor(tp[:, 12, :], tp[:, 12, :], tp[:, 13, :], ALU.subtract))
                V.tensor_tensor(tp[:, 14, :], tp[:, 10, :], tp[:, 9, :], ALU.mult)
                link(V.tensor_tensor(tp[:, 15, :], tp[:, 12, :], tp[:, 9, :], ALU.mult))
                for k in range(1, L):
                    V.tensor_tensor(tp[:, 7, :], PK[:, 0, k, :], PK[:, 0, 1, :], ALU.mult)
                    V.tensor_tensor(tp[:, 8, :], PK[:, 1, k, :], PK[:, 1, 1, :], ALU.mult)
                    V.tensor_tensor(tp[:, 10, :], PK[:, 0, k, :], PK[:, 1, 1, :], ALU.mult)
                    link(V.tensor_tensor(tp[:, 11, :], PK[:, 1, k, :], PK[:, 0, 1, :], ALU.mult))
                    V.tensor_tensor(PK[:, 0, k + 1, :], tp[:, 7, :], tp[:, 8, :], ALU.subtract)
                    link(V.tensor_tensor(PK[:, 1, k + 1, :], tp[:, 10, :], tp[:, 11, :], ALU.add))
                V.tensor_scalar(NPI, PK[:, 1], -1.0, None, ALU.mult)
                link(V.tensor_scalar(NPR, PK[:, 0], -1.0, None, ALU.mult))
                for s in range(L):
                    V.tensor_copy(RK[:, :, :, s], PK[:, :, L - 1 - s, :])
                dve.wait_ge(S("bn_landed"), 64)
                fr, fi = (tp[:, 14 + r, :].unsqueeze(2).broadcast_to([P, GH, CH]) for r in range(2))
                V.tensor_tensor(Bb[:, 0], Bn[:, 0], fr, ALU.mult)
                V.tensor_tensor(Bb[:, 1], Bn[:, 1], fr, ALU.mult)
                V.tensor_tensor(tb[:, 0], Bn[:, 1], fi, ALU.mult)
                link(V.tensor_tensor(tb[:, 1], Bn[:, 0], fi, ALU.mult))
                V.tensor_tensor(Bb[:, 0], Bb[:, 0], tb[:, 0], ALU.subtract)
                V.tensor_tensor(Bb[:, 1], Bb[:, 1], tb[:, 1], ALU.add).then_inc(S("bbar_ready"), 1)
                dve.wait_ge(S("bbar_ready"), 1)
                dve.wait_ge(S("ct_full"), 1)
                for r in range(2):
                    for b in range(2):
                        for h in range(2):
                            V.tensor_copy(Ct[h * 64:(h + 1) * 64, r, b * 16:(b + 1) * 16, :],
                                          PS[4 + 2 * r + b][h * 64:(h + 1) * 64, :].rearrange("p (g h c) -> p g h c", h=2, c=CH)[:, :, h, :])
                dve.wait_ge(S("h0_full"), 1)
                link(V.tensor_copy(H0.rearrange("p r b g -> p (r b g)"), PS[1][:, :]))
                V.memset(Ha[:, 0, :, :], 0.0).then_inc(S("ct_ready"), 1)

                def spread_pair(m, u):
                    v = u % 2
                    bb = Bb[:, :, bass.ds(m, 1), :].rearrange("p r a c -> p r (a c)").unsqueeze(2).broadcast_to([P, 2, L, CH])
                    rk = [RK[:, r, bass.ds(m, 1), :].rearrange("p a s -> p (a s)").unsqueeze(1).unsqueeze(3)
                          .broadcast_to([P, 2, L, CH]) for r in range(2)]
                    dve.wait_ge(S("turned"), m + 1)
                    V.tensor_tensor(tA[v], bb, rk[0], ALU.mult)
                    V.tensor_tensor(tB[v], bb, rk[1], ALU.mult).then_inc(S("eb_parts"), 1)
                    dve.wait_ge(S("eb_parts"), m + 1)
                    V.tensor_tensor(EB[u][:, 0], tA[v][:, 0], tB[v][:, 1], ALU.subtract)
                    V.tensor_tensor(EB[u][:, 1], tB[v][:, 0], tA[v][:, 1], ALU.add).then_inc(S("eb_ready"), 1)

                def copy_pair(m, u):
                    dve.wait_ge(S("e_full"), m + 3)
                    V.tensor_copy(ea[:, :, :, bass.ds(m, 1)].rearrange("p c r a -> p r (c a)"),
                                  PS[6 + u % 2][:, 0:2 * NCH].rearrange("p (r c) -> p r c", r=2)).then_inc(S("e_copied"), 1)

                for m in range(3):
                    if m == 2:
                        dve.wait_ge(S("eb_ready"), 1)
                    spread_pair(m, m)
                with dve.Fori(0, GH // 4 - 1) as i:
                    for u in range(4):
                        dve.wait_ge(S("eb_ready"), i * 4 + (u + 2))
                        spread_pair(i * 4 + (u + 3), (u + 3) % 4)
                        copy_pair(i * 4 + u, u)
                for m in range(GH - 4, GH):
                    if m + 3 < GH:
                        dve.wait_ge(S("eb_ready"), m + 2)
                        spread_pair(m + 3, (m + 3) % 4)
                    copy_pair(m, m % 4)
                dve.wait_ge(S("e_copied"), GH + 2)

                def make_q(part):
                    gs = slice(part * PG, (part + 1) * PG)

                    def spread(table):
                        return table[:, :, gs].rearrange("p k g -> p g k").unsqueeze(3).broadcast_to([P, PG, 9, CH])

                    def rows(r):
                        return Ct[:, r, gs, :].unsqueeze(2).broadcast_to([P, PG, 9, CH])

                    q = Q[part % 2]
                    if part:
                        dve.wait_ge(S("q_ready"), part)
                    if part >= 2:
                        dve.wait_ge(S("y_full"), PG * (part - 1) + 2)
                    V.tensor_tensor(q[:, 0], rows(0), spread(PK[:, 0]), ALU.mult)
                    link(V.tensor_tensor(t1, rows(1), spread(NPI), ALU.mult))
                    link(V.tensor_tensor(q[:, 0], q[:, 0], t1, ALU.add))
                    V.tensor_tensor(q[:, 1], rows(0), spread(NPI), ALU.mult)
                    link(V.tensor_tensor(t1, rows(1), spread(NPR), ALU.mult))
                    V.tensor_tensor(q[:, 1], q[:, 1], t1, ALU.add).then_inc(S("q_ready"), 1)

                make_q(0)
                make_q(1)
                a8r = PK[:, 0, L, :].unsqueeze(1).broadcast_to([P, 2, GH])
                link(V.tensor_copy(Ha[:, NPC:NCH, :, :].rearrange("p b r g -> p r b g"), H0))

                def state_step(state, extra, out, mark):
                    V.tensor_tensor(sc[:, 0], a8r, state, ALU.mult)
                    V.tensor_tensor(sc[:, 1, 0, :], NPI[:, L, :], state[:, 1, :], ALU.mult)
                    mark(V.tensor_tensor(sc[:, 1, 1, :], PK[:, 1, L, :], state[:, 0, :], ALU.mult), 1)
                    mark(V.tensor_tensor(sc[:, 2], sc[:, 0], extra, ALU.add), 2)
                    mark(V.tensor_tensor(out, sc[:, 2], sc[:, 1], ALU.add), 3)

                steps, unroll = NPC - 1, 3

                def scan_step(i, u):
                    def at(buf, k):
                        return buf[:, bass.ds(i * unroll + (u + k), 1), :, :].rearrange("p a r g -> p (a r) g")

                    def mark(ins, k):
                        ins.then_inc(S("scan_order"), 1)
                        dve.wait_ge(S("scan_order"), i * (3 * unroll) + (3 * u + k))

                    state_step(at(Ha, 0), at(ea, 0), at(Ha, 1), mark)

                with dve.Fori(0, steps // unroll) as i:
                    for u in range(unroll):
                        scan_step(i, u)
                for u in range(steps % unroll):
                    scan_step(steps // unroll, u)
                dve.sem_inc(S("h_done"), 1)
                last = NPC - 1
                state_step(Ha[:, last], ea[:, last], FinP, lambda ins, k: link(ins))
                ser, sei = (ea[:, NPC:NCH, r, :] for r in range(2))
                pr, npi, pi = (x[:, L, :].unsqueeze(1).broadcast_to([P, NB, GH]) for x in (PK[:, 0], NPI, PK[:, 1]))
                s1, s2 = (t1_flat[:, k * 256:(k + 1) * 256].rearrange("p (b g) -> p b g", b=NB) for k in range(2))
                for r, (x, y) in enumerate(((npi, 1), (pi, 0))):
                    V.tensor_tensor(s1, pr, H0[:, r, :, :], ALU.mult)
                    link(V.tensor_tensor(s2, x, H0[:, y, :, :], ALU.mult))
                    link(V.tensor_tensor(s1, s1, s2, ALU.add))
                    link(V.tensor_tensor(FinS[:, r, :, :], s1, (ser, sei)[r], ALU.add))
                for part in range(2, NPART):
                    make_q(part)
                dve.sem_inc(S("fin_ready"), 1)
                for r in range(2):
                    dve.wait_ge(S("fin_full"), r + 1)
                    V.tensor_copy(stg_fin[:, r, 0:2, :], PS[6][:, 0:256].rearrange("p (t n) -> p t n", t=2))
                    V.tensor_copy(stg_fin[0:GH, r, 2, :], PS[6][0:GH, 256:384]).then_inc(S("fin_copied"), 1)

        take = scratch()
        kvp = take(2 * 1536).rearrange("p (t n) -> p t n", t=2)
        Sb = [take(4 * SEQ).rearrange("p (h k) -> p h k", h=4) for _ in range(2)]
        PTs = [take(4 * SEQ).rearrange("p (b h q) -> p b h q", b=2, h=4) for _ in range(2)]
        oacc = take(2 * 1024).rearrange("p (t h d) -> p t h d", t=2, h=NH)
        ot = [take(256).rearrange("p (h d) -> p h d", h=4) for _ in range(2)]
        nmx, rs, wgt = (take(64).rearrange("p (n h) -> p n h", h=4) for _ in range(3))
        pcol = take(4).rearrange("p (v m) -> p v m", v=2)
        pe32 = take(2 * P).rearrange("p (v d s) -> p v d s", v=2, d=2)
        pl32 = take(2)
        pl = take(2 * 2 * 16).rearrange("p (a c) -> p a c", a=4)
        Gp = take(4 * 32).rearrange("p (a c) -> p a c", a=4)
        Gr = take(2 * P).rearrange("p (g n c) -> p g n c", g=2, n=4)
        kcT = take(32).rearrange("p (g c) -> p g c", g=2)
        Vbd = take(4 * 256).rearrange("p (g n d) -> p g n d", g=4, n=4)
        Pc = take(512).rearrange("p (h c) -> p h c", h=NH)
        PcT = take(512)
        cm, cs_, cw = (take(NH) for _ in range(3))
        Sc = take(NH * NC_P).rearrange("p (h c) -> p h c", h=NH)
        work = [(qt, br, g) for qt in range(2) for br in range(2) for g in range(NKV)]
        NW = len(work)

        with program() as block:
            @block.sync
            def _(sp):
                for t in range(2):
                    sp.dma_start(kvp[:, t, 0:1024], kvr_prompt[0, 0, t * P:(t + 1) * P].rearrange("t a g d -> t (a g d)")).then_inc(S("kvp_landed"), 16)
                    sp.dma_start(kvp[:, t, 1024:1536], win_prompt[0, 0, t * P:(t + 1) * P].rearrange("t a g d -> t (a g d)")).then_inc(S("kvp_landed"), 16)
                for b in range(NB):
                    sp.dma_start(win_sample[0, b, 0:WIN - NQ].rearrange("t a g d -> t (a g d)"),
                                 state_win[0, b, NQ:WIN].rearrange("t a g d -> t (a g d)")).then_inc(S("stored"), 16)
                sp.wait_ge(S("stored"), (NB + 6) * 16)

            @block.gpsimd
            def _(pool):
                nc.gpsimd.memset(phi[:, :, :], 0.0).then_inc(S("phi_zero"), 1)
                nc.gpsimd.memset(Gp, 0.0).then_inc(S("pads_zero"), 1)
                nc.gpsimd.memset(Vbd, 0.0).then_inc(S("pads_zero"), 1)
                nc.gpsimd.memset(Pc, 0.0).then_inc(S("pads_zero"), 1)
                nc.gpsimd.tensor_copy(qs[:, :, :], qT[:, :, SEQ:NT]).then_inc(S("qs_ready"), 1)
                nc.gpsimd.tensor_copy(ks[:, 0:2, :], kvT[:, 4:6, SEQ:NT]).then_inc(S("qs_ready"), 1)
                nc.gpsimd.tensor_copy(ks[:, 2:4, :], kvT[:, 8:10, SEQ:NT]).then_inc(S("qs_ready"), 1)

            @block.scalar
            def _(act):
                for n in range(8):
                    act.dma_start(pcol[n * 16:(n + 1) * 16, :, :], w_pool[0].rearrange("v (m s) -> s v m", s=16)).then_inc(S("pool_landed"), 16)
                act.dma_start(pl32[0:32, :], w_pool[0].rearrange("v l -> l v")).then_inc(S("pool_landed"), 16)
                for d in range(2):
                    act.dma_start(pe32[0:32, :, d, :], w_pe[0].rearrange("v l d -> l v d")).then_inc(S("pool_landed"), 16)
                act.wait_ge(S("phi_zero"), 1)
                for h in range(2):
                    act.dma_start(phi[h * 64:(h + 1) * 64, :, h * 64:(h + 1) * 64], w_phi[0].rearrange("v a b -> a v b")).then_inc(S("phi_landed"), 16)
                act.wait_ge(S("pads_zero"), 3)
                act.wait_ge(S("ppool_ready"), 1)
                nc.scalar.activation(Gp[:, :, 0:NC_P], pl[:, :, 0:NC_P], ACT.Gelu_apprx_tanh).then_inc(S("pgelu_ready"), 1)
                for qt in range(2):
                    act.wait_ge(S("pc_shifted"), qt + 1)
                    nc.scalar.activation(Sc, Sc, ACT.Exp).then_inc(S("pc_exp"), 1)
                    act.wait_ge(S("pct_full"), qt + 1)
                    nc.scalar.copy(PcT, PS[7][:, :]).then_inc(S("pct_copied"), 1)
                for n in range(NW + 1):
                    if n < NW:
                        KE = P * (work[n][0] + 1)
                        act.wait_ge(S("pmax_ready"), n + 1)
                        for h in range(4):
                            ins = nc.scalar.activation(Sb[n % 2][:, h, 0:KE], Sb[n % 2][:, h, 0:KE], ACT.Exp,
                                                       bias=nmx[:, n, h:h + 1], accum_out=rs[:, n, h:h + 1])
                        ins.then_inc(S("p_ready"), 1)
                    if n >= 1:
                        m = n - 1
                        act.wait_ge(S("pt_full"), m + 1)
                        if m >= 2:
                            act.wait_ge(S("o_full"), m - 1)
                        for kb in range(work[m][0] + 1):
                            ins = nc.scalar.copy(PTs[m % 2][:, kb].rearrange("p h q -> p (h q)"), PS[4 + kb][:, :])
                        ins.then_inc(S("pt_copied"), 1)

            @block.tensor
            def _(pe):
                pe.wait_ge(S("pool_landed"), 176)
                for v in range(2):
                    mm = pe.matmul(PS[5][:, v:v + 1], pe32[0:32, v].rearrange("p d s -> p (d s)"), pl32[0:32, v:v + 1], start=True, stop=True)
                mm.then_inc(S("pec_full"), 1)
                pe.wait_ge(S("poolw_ready"), 1)
                pe.wait_ge(S("kvp_landed"), 64)
                for t in range(2):
                    for a in range(4):
                        mm = pe.matmul(PS[6][:, a * 32:(a + 1) * 32].rearrange("p (m t n) -> p m t n", m=2, t=2)[:, :, t, :],
                                       kvp[:, t, a * P:(a + 1) * P], poolw[:, a // 2].rearrange("p m n -> p (m n)"), start=True, stop=True)
                mm.then_inc(S("ppool_full"), 1)
                pe.wait_ge(S("pgr_ready"), 1)
                pe.wait_ge(S("phi_landed"), 32)
                for g in range(2):
                    pe.matmul(PS[7][:, g * 16:g * 16 + NC_P], phi[:, 0, :], Gp[:, g, 0:NC_P], start=True, stop=True)
                for g in range(2):
                    mm = pe.matmul(PS[7][:, 64 + g * P:64 + (g + 1) * P], Gr[:, g].rearrange("p n c -> p (n c)"), phi[:, 1, :], start=True, stop=True)
                mm.then_inc(S("pcv_full"), 1)
                pe.wait_ge(S("pcv_copied"), 1)
                for qt in range(2):
                    for h in range(NH):
                        g, n = h // 4, h % 4
                        a = (g % 2) * 64
                        mm = pe.matmul(PS[(6, 0)[g % 2]][:, h * 32:h * 32 + NC_P], qT[a:a + 64, (g // 2) * 4 + n, qt * P:(qt + 1) * P],
                                       kcT[a:a + 64, g // 2, 0:NC_P], start=True, stop=True)
                    mm.then_inc(S("pcs_full"), 1)
                    pe.wait_ge(S("pc_ready"), qt + 1)
                    for g in range(4):
                        tr = nc.tensor.transpose(PS[7][:, g * P:(g + 1) * P], Pc[:, 4 * g:4 * g + 4, :].rearrange("p h c -> p (h c)"), ident)
                    tr.then_inc(S("pct_full"), 1)
                    pe.wait_ge(S("pct_copied"), qt + 1)
                    if qt:
                        pe.wait_ge(S("pco_done"), qt)
                    for g in range(4):
                        mm = pe.matmul(PS[4 + g // 2][:, (g % 2) * 256:(g % 2 + 1) * 256], PcT[:, g * P:(g + 1) * P],
                                       Vbd[:, g].rearrange("p n d -> p (n d)"), start=True, stop=True)
                    mm.then_inc(S("pco_full"), 1)
                pe.wait_ge(S("pco_done"), 2)
                for n in range(NW + 2):
                    if n < NW:
                        qt, br, g = work[n]
                        KE = P * (qt + 1)
                        if n >= 2:
                            pe.wait_ge(S("s_read"), n - 1)
                        a = (g % 2) * 64
                        for h in range(4):
                            mm = pe.matmul(PS[2 * (n % 2) + h // 2][:, (h % 2) * 256:(h % 2) * 256 + KE],
                                           qT[a:a + 64, (g // 2) * 4 + h, qt * P:(qt + 1) * P],
                                           kvT[a:a + 64, 4 + 4 * br + g // 2, 0:KE], start=True, stop=True)
                        mm.then_inc(S("s_full"), 1)
                    if 1 <= n <= NW:
                        m = n - 1
                        qt = work[m][0]
                        pe.wait_ge(S("p_ready"), m + 1)
                        if m:
                            pe.wait_ge(S("pt_copied"), m)
                        for kb in range(qt + 1):
                            for h in range(4):
                                tr = nc.tensor.transpose(PS[4 + kb][:, h * P:(h + 1) * P], Sb[m % 2][:, h, kb * P:(kb + 1) * P], ident)
                        tr.then_inc(S("pt_full"), 1)
                    if n >= 2:
                        m = n - 2
                        qt, br, g = work[m]
                        pe.wait_ge(S("pt_copied"), m + 1)
                        if m >= 2:
                            pe.wait_ge(S("o_done"), m - 1)
                        for h in range(4):
                            for kb in range(qt + 1):
                                mm = pe.matmul(PS[6 + m % 2][:, h * 64:(h + 1) * 64], PTs[m % 2][:, kb, h, :],
                                               kvp[:, kb, (768 if br == 0 else 1280) + g * 64:(768 if br == 0 else 1280) + (g + 1) * 64],
                                               start=kb == 0, stop=kb == qt)
                        mm.then_inc(S("o_full"), 1)
                pe.wait_ge(S("o_done"), NW)
                for n in range(4):
                    t, c = n // 2, n % 2
                    for j in range(4):
                        tr = nc.tensor.transpose(PS[n][:, j * P:(j + 1) * P],
                                                 oacc[:, t, 2 * (4 * c + j):2 * (4 * c + j) + 2, :].rearrange("p h d -> p (h d)"), ident)
                    tr.then_inc(S("ot_full"), 1)

            @block.vector
            def _(dve):
                V = nc.vector
                order = [0]

                def link(ins):
                    order[0] += 1
                    ins.then_inc(S("p_order"), 1)
                    dve.wait_ge(S("p_order"), order[0])

                dve.wait_ge(S("pool_landed"), 176)
                V.tensor_tensor(poolw[:, :, :, :], pcol.unsqueeze(3).broadcast_to([P, 2, 2, 8]),
                                C("submask").unsqueeze(1).unsqueeze(1).broadcast_to([P, 2, 2, 8]), ALU.mult).then_inc(S("poolw_ready"), 1)
                dve.wait_ge(S("pec_full"), 1)
                link(V.tensor_copy(pec[:, :], PS[5][:, 0:2]))
                dve.wait_ge(S("ppool_full"), 1)
                parts = PS[6][:, 0:P].rearrange("p (a m c) -> p a m c", a=4, m=2)
                for v in range(2):
                    V.tensor_scalar(pl[:, 2 * v:2 * v + 2, 0:NC_P], parts[:, 2 * v:2 * v + 2, 0, 0:NC_P], pec[:, v:v + 1], None, ALU.add).then_inc(S("p_order"), 1)
                order[0] += 2
                dve.wait_ge(S("p_order"), order[0])
                V.tensor_tensor(pl[:, :, 0:NC_P], pl[:, :, 0:NC_P], parts[:, :, 1, 1:NC_P + 1], ALU.add).then_inc(S("ppool_ready"), 1)
                dve.wait_ge(S("pgelu_ready"), 1)
                V.tensor_copy(Gr, Gp[:, 2:4, :].unsqueeze(2).broadcast_to([P, 2, 4, 32])).then_inc(S("pgr_ready"), 1)
                dve.wait_ge(S("pcv_full"), 1)
                V.tensor_copy(kcT[:, :, 0:NC_P], PS[7][:, 0:32].rearrange("p (g c) -> p g c", g=2)[:, :, 0:NC_P])
                for n in range(4):
                    ins = V.tensor_copy(Vbd[n * 32:(n + 1) * 32, :, n, :], PS[7][n * 32:(n + 1) * 32, 64:320].rearrange("p (g d) -> p g d", g=4))
                ins.then_inc(S("pcv_copied"), 1)
                for qt in range(2):
                    dve.wait_ge(S("pcs_full"), qt + 1)
                    bias = C("biascp")[:, qt * 240:(qt + 1) * 240].rearrange("p (h c) -> p h c", h=NH)
                    valid = C("validcp")[:, qt * NC_P:(qt + 1) * NC_P].unsqueeze(1).broadcast_to([P, NH, NC_P])
                    for par in range(2):
                        for g in (par, par + 2):
                            hs = slice(4 * g, 4 * g + 4)
                            ins = V.tensor_tensor(Sc[:, hs, :], PS[(6, 0)[par]][:, :].rearrange("p (h c) -> p h c", h=NH)[:, hs, 0:NC_P],
                                                  bias[:, hs, :], ALU.add)
                    link(ins)
                    link(V.tensor_reduce(cm, Sc, AX_X, ALU.max))
                    V.tensor_tensor(Sc, Sc, cm.unsqueeze(2).broadcast_to([P, NH, NC_P]), ALU.subtract).then_inc(S("pc_shifted"), 1)
                    dve.wait_ge(S("pc_exp"), qt + 1)
                    link(V.tensor_reduce(cs_, Sc, AX_X, ALU.add))
                    V.tensor_tensor(Pc[:, :, 0:NC_P], Sc, valid, ALU.mult).then_inc(S("pc_ready"), 1)
                    link(V.reciprocal(cs_, cs_))
                    if qt:
                        dve.wait_ge(S("pco_done"), qt)
                    link(V.tensor_tensor(cw, cs_, gN[:, qt, 0:NH], ALU.mult))
                    dve.wait_ge(S("pco_full"), qt + 1)
                    for b in range(2):
                        ins = V.tensor_tensor(oacc[:, qt, 8 * b:8 * b + 8, :], PS[4 + b][:, :].rearrange("p (h d) -> p h d", h=8),
                                              cw[:, 8 * b:8 * b + 8].unsqueeze(2).broadcast_to([P, 8, 64]), ALU.mult)
                    ins.then_inc(S("pco_done"), 1)
                dve.wait_ge(S("pco_done"), 2)
                for n in range(NW + 2):
                    if n < NW:
                        qt, br, g = work[n]
                        KE = P * (qt + 1)
                        dve.wait_ge(S("s_full"), n + 1)
                        if n >= 2:
                            dve.wait_ge(S("pt_full"), n - 1)
                        for h in range(4):
                            ins = V.scalar_tensor_tensor(out=Sb[n % 2][:, h, 0:KE], in0=C("distp")[:, SEQ - KE:SEQ], scalar=-slope(4 * g + h),
                                                         in1=PS[2 * (n % 2) + h // 2][:, (h % 2) * 256:(h % 2) * 256 + KE], op0=ALU.mult, op1=ALU.add)
                        ins.then_inc(S("s_read"), 1)
                        dve.wait_ge(S("s_read"), n + 1)
                        V.tensor_reduce(nmx[:, n, :], Sb[n % 2][:, :, 0:KE], AX_X, ALU.max, negate=True).then_inc(S("pmax_ready"), 1)
                    if n >= 2:
                        m = n - 2
                        qt, br, g = work[m]
                        dve.wait_ge(S("o_full"), m + 1)
                        dve.wait_ge(S("p_ready"), m + 1)
                        link(V.reciprocal(rs[:, m, :], rs[:, m, :]))
                        link(V.tensor_tensor(wgt[:, m, :], rs[:, m, :], gN[:, qt, (br + 1) * NH + 4 * g:(br + 1) * NH + 4 * g + 4], ALU.mult))
                        link(V.tensor_tensor(ot[m % 2], PS[6 + m % 2][:, 0:256].rearrange("p (h d) -> p h d", h=4),
                                             wgt[:, m, :].unsqueeze(2).broadcast_to([P, 4, 64]), ALU.mult))
                        V.tensor_tensor(oacc[:, qt, 4 * g:4 * g + 4, :], oacc[:, qt, 4 * g:4 * g + 4, :], ot[m % 2], ALU.add).then_inc(S("o_done"), 1)
                for n in range(4):
                    t, c = n // 2, n % 2
                    dve.wait_ge(S("ot_full"), n + 1)
                    V.tensor_copy(oT[:, 4 * c:4 * c + 4, t * P:(t + 1) * P], PS[n][:, :].rearrange("p (j q) -> p j q", j=4)).then_inc(S("ot_ready"), 1)
                dve.wait_ge(S("ot_ready"), 4)

        phase.close()
        kept.close()
        open_weights(phase, "w2")
        last = phase.enter_context(ExitStack())
        open_arena(last, "arena3")
        take = scratch()
        take_x = scratch(xT[:, :, :].rearrange("p k n -> p (k n)"), KT * NT)
        take_ys = scratch(ysT[:, :, :].rearrange("p k n -> p (k n)"), 8 * NT)
        RP = 4
        pageA = [take_x(768) for _ in range(RP)]
        Vs = take(NPG * 256).rearrange("p (g n) -> p g n", g=NPG)
        KTs = take(2 * PAST).rearrange("p (g k) -> p g k", g=2)
        Ss = take(PAST + NQ)
        Sw = take(WIN + NQ)
        PT2 = [take(512) for _ in range(2)]
        sgb = [take(NT) for _ in range(2)]
        wn = take_x(4 * 512).rearrange("p (t n) -> p t n", t=4)
        KwT = take_ys(2 * WIN).rearrange("p (g k) -> p g k", g=2)
        kb = take(PAST + WIN + 2 * NQ)
        vnew = take_ys(2 * 256).rearrange("p (a n) -> p a n", a=2)
        plS = take_ys(4 * NC_S).rearrange("p (a c) -> p a c", a=4)
        kcs = take(2 * P).rearrange("p (g c) -> p g c", g=2)
        vcs = take_ys(256)
        Pcs = take(NC_S)
        pcT = take(P)
        qst = take(2 * 64).rearrange("p (g r) -> p g r", g=2)
        kst = take(4 * NQ).rearrange("p (a q) -> p a q", a=4)
        gw = take(3)
        mx3, rs3, rw3 = (take(3) for _ in range(3))
        imp0, imp1, msk = (take(NBLK) for _ in range(3))
        top = take(16)
        waits = take(1)
        od = take(P).rearrange("p (u d) -> p u d", u=2)
        ptab = take(NB * NPG).bitcast(I32)

        with program() as block:
            @block.sync
            def _(sp):
                sp.dma_start(ptab[0:1, :], page_table.rearrange("b g -> (b g)").rearrange("(o n) -> o n", o=1)).then_inc(S("ptab_landed"), 16)
                sp.dma_start(kb, kbias).then_inc(S("kb_landed"), 16)
                sp.wait_ge(S("ptab_landed"), 16)
                n_pool = cache_kv.shape[1]
                rows = cache_kv[0].rearrange("n t a g d -> n t (a g d)")
                with sp.Fori(0, NB) as b:
                    def page(p):
                        return sp.value_load(ptab[0:1, bass.ds(b * NPG + p, 1)], min_val=0, max_val=n_pool - 1)

                    for step in range(2):
                        load_tile(sp, job_mg, b * 2, step)
                    for p in range(NPG):
                        if p in (5, 7):
                            load_tile(sp, job_mg, b * 2 + 1, p // 7)
                        sp.wait_ge(S("page_used"), b * NPG + p + 1)
                        sp.dma_start(pageA[p % RP], rows[bass.ds(page(p), 1), :, 0:768].rearrange("o t n -> (o t) n")).then_inc(S(f"page_landed{p % RP}"), 16)
                    sp.wait_ge(S("so_full"), b + 1)
                    sp.dma_start(wn, state_win[0, bass.ds(b, 1)].rearrange("o (t p) a g d -> p (o t) (a g d)", p=P)).then_inc(S("wn_landed"), 16)
                    sp.dma_start(vnew[0:NQ, 0, :], kvr_sample[0, bass.ds(b, 1), :, 3].rearrange("o t g d -> (o t) (g d)")).then_inc(S("wn_landed"), 16)
                    sp.dma_start(vnew[0:NQ, 1, :], win_sample[0, bass.ds(b, 1), WIN - NQ:WIN, 1].rearrange("o t g d -> (o t) (g d)")).then_inc(S("wn_landed"), 16)
                    for p in range(NPG):
                        sp.dma_start(Vs[:, p, :], rows[bass.ds(page(p), 1), :, 768:1024].rearrange("o t n -> (o t) n")).then_inc(S("v_landed"), 16)

            @block.gpsimd
            def _(pool):
                with pool.Fori(0, NB) as b:
                    pool.wait_ge(S("so_done"), b + 1)
                    for g in range(2):
                        nc.gpsimd.tensor_tensor(qst[:, g, :].rearrange("p (h n q) -> p h n q", h=2, n=4),
                                                qs[:, 4 * g:4 * g + 4, bass.ds(b * NQ, NQ)].unsqueeze(1).broadcast_to([P, 2, 4, NQ]),
                                                C("half").unsqueeze(2).unsqueeze(3).broadcast_to([P, 2, 4, NQ]), ALU.mult)
                    nc.gpsimd.tensor_copy(kst, ks[:, :, bass.ds(b * NQ, NQ)])
                    nc.gpsimd.tensor_copy(gw, gS[:, :, bass.ds(b, 1)].rearrange("p r a -> p (r a)")).then_inc(S("q_staged"), 1)

            @block.tensor
            def _(pe):
                pe.sem_inc(S("page_used"), RP)
                pe.sem_inc(S("so_full"), 1)
                with pe.Fori(0, NB) as b:
                    pe.wait_ge(S("so_done"), b + 1)
                    for p in range(NPG):
                        pe.wait_ge(S(f"page_landed{p % RP}"), b * (16 * NPG // RP) + 16 * (p // RP + 1))
                        if p % 2 == 0:
                            pe.wait_ge(S("kt_copied"), b * 8 + (p // 2 + 1))
                        for g in range(2):
                            tr = nc.tensor.transpose(PS[6 + p // 2 % 2][:, (p % 2 * 2 + g) * P:(p % 2 * 2 + g + 1) * P],
                                                     pageA[p % RP][:, 512 + g * P:512 + (g + 1) * P], ident)
                        if p % 2:
                            tr.then_inc(S("kt_full"), 1)
                        for a in range(4):
                            mm = pe.matmul(PS[4 + a // 2][:, a % 2 * 256:a % 2 * 256 + 256].rearrange("p (m c) -> p m c", m=2)[:, :, p * 8:p * 8 + 8],
                                           pageA[p % RP][:, a * P:(a + 1) * P], poolw[:, a // 2].rearrange("p m n -> p (m n)"), start=True, stop=True)
                        mm.then_inc(S("page_used"), 1)
                        if p in (3, 9):
                            multiply(pe, job_mg, b * 2, p // 9, actr[:, 0], actr[:, 1])
                    pe.wait_ge(S("sgelu_ready"), b + 1)
                    pe.wait_ge(S("kt_copied"), b * 8 + 10)
                    for g in range(2):
                        pe.matmul(PS[6][:, g * P:g * P + NC_S], phi[:, 0, :], plS[:, g, :], start=True, stop=True)
                    for g in range(2):
                        mm = pe.matmul(PS[6][0:NC_S, 256 + g * P:256 + (g + 1) * P], plS[:, 2 + g, :], phi[:, 1, :], start=True, stop=True)
                    mm.then_inc(S("cv_full"), 1)
                    pe.wait_ge(S("q_staged"), b + 1)
                    pe.wait_ge(S("cv_copied"), b + 1)
                    for g in range(2):
                        mm = pe.matmul(PS[7][g * 64:(g + 1) * 64, 0:NC_S], qst[:, g, :], kcs[:, g, 0:NC_S], start=True, stop=True)
                    mm.then_inc(S("cs_full"), 1)
                    for c in range(5):
                        if c >= 2:
                            pe.wait_ge(S("sel_read"), b * 5 + (c - 1))
                        for g in range(2):
                            if c < 4:
                                mm = pe.matmul(PS[4 + c % 2][g * 64:(g + 1) * 64, :], qst[:, g, :], KTs[:, g, c * 512:(c + 1) * 512], start=True, stop=True)
                            else:
                                mm = pe.matmul(PS[4][g * 64:(g + 1) * 64, 0:NQ], qst[:, g, :],
                                               kst[:, g, :], start=True, stop=True)
                        mm.then_inc(S("sel_full"), 1)
                    pe.wait_ge(S("cp_ready"), b + 1)
                    nc.tensor.transpose(PS[6][0:NC_S, 0:P], Pcs, ident).then_inc(S("pcT_full"), 1)
                    pe.wait_ge(S("pcT_copied"), b + 1)
                    pe.wait_ge(S("sel_read"), b * 5 + 4)
                    mm = pe.matmul(PS[5][:, 0:256], pcT[0:NC_S, :], vcs[0:NC_S, :], start=True, stop=True)
                    mm.then_inc(S("oc_full"), 1)
                    pe.matmul(PS[7][:, 0:NBLK], pcT[0:NC_S, :], C("overlap", NC_S), start=True, stop=True).then_inc(S("imp_full"), 1)
                    pe.wait_ge(S("imp_copied"), b + 1)
                    pe.matmul(PS[7][:, 64:64 + NBLK], C("same"), imp0, start=True, stop=True).then_inc(S("impsum_full"), 1)
                    multiply(pe, job_mg, b * 2 + 1, 0, actr[:, 0], actr[:, 1])
                    pe.wait_ge(S("wn_landed"), b * 48 + 48)
                    pe.wait_ge(S("imp_read"), b + 1)
                    for t in range(4):
                        for g in range(2):
                            tr = nc.tensor.transpose(PS[6 + t // 2][:, (t % 2 * 2 + g) * P:(t % 2 * 2 + g + 1) * P],
                                                     wn[:, t, g * P:(g + 1) * P], ident)
                        if t % 2:
                            tr.then_inc(S("kw_full"), 1)
                    pe.wait_ge(S("oc_done"), b + 1)
                    pe.wait_ge(S("kw_copied"), b * 2 + 2)
                    for g in range(2):
                        mm = pe.matmul(PS[5][g * 64:(g + 1) * 64, :], qst[:, g, :], KwT[:, g, :], start=True, stop=True)
                    pe.wait_ge(S("sel_read"), b * 5 + 5)
                    for g in range(2):
                        mm = pe.matmul(PS[4][g * 64:(g + 1) * 64, 0:NQ], qst[:, g, :], kst[:, 2 + g, :], start=True, stop=True)
                    mm.then_inc(S("w_full"), 1)
                    multiply(pe, job_mg, b * 2 + 1, 1, actr[:, 0], actr[:, 1])
                    pe.wait_ge(S("w_read"), b + 1)
                    pe.wait_ge(S("v_landed"), b * (16 * NPG) + 16 * NPG)
                    for n in range(7):
                        if n < 6:
                            pe.wait_ge(S("sp_ready"), b * 2 + (1 if n < 4 else 2))
                            pe.wait_ge(S("spt_copied"), b * 6 + (n + 1))
                            bank = PS[6 + n % 2]
                            if n < 5:
                                for j in range(4):
                                    src = Ss[:, (4 * n + j) * P:(4 * n + j + 1) * P] if n < 4 else Sw[:, j * P:(j + 1) * P]
                                    tr = nc.tensor.transpose(bank[:, j * P:(j + 1) * P], src, ident)
                            else:
                                nc.tensor.transpose(bank[0:NQ, 0:P], Ss[:, PAST:PAST + NQ], ident)
                                tr = nc.tensor.transpose(bank[0:NQ, P:2 * P], Sw[:, WIN:WIN + NQ], ident)
                            tr.then_inc(S("spt_full"), 1)
                        if n >= 1:
                            m = n - 1
                            pe.wait_ge(S("spt_copied"), b * 6 + (m + 3))
                            if m < 5:
                                for j in range(4):
                                    mm = pe.matmul(PS[5 if m < 4 else 4][:, 0:256], PT2[m % 2][:, j * P:(j + 1) * P],
                                                   Vs[:, 4 * m + j, :] if m < 4 else wn[:, j, 256:512],
                                                   start=j == 0 and m in (0, 4), stop=False)
                                mm.then_inc(S("pv_used"), 1)
                            else:
                                pe.matmul(PS[5][:, 0:256], PT2[m % 2][0:NQ, 0:P], vnew[0:NQ, 0, :], start=False, stop=True)
                                mm = pe.matmul(PS[4][:, 0:256], PT2[m % 2][0:NQ, P:2 * P], vnew[0:NQ, 1, :], start=False, stop=True)
                                mm.then_inc(S("so_full"), 1)
                    pe.wait_ge(S("od_ready"), b + 1)
                    nc.tensor.transpose(PS[6][:, 0:P], od.rearrange("p u d -> p (u d)"), ident).then_inc(S("odT_full"), 1)

            @block.scalar
            def _(act):
                act.sem_inc(S("kt_copied"), 2)
                act.sem_inc(S("spt_copied"), 2)
                act.sem_inc(S("so_done"), 1)

                def gate(b, j, s):
                    i = b * 2 + j
                    full(act, job_mg, i, s)
                    act.wait_ge(S(f"sg_stored{s}"), i * 16 + 16)
                    nc.scalar.activation(sgb[s], PS[s][:, 0:NT], ACT.Sigmoid).then_inc(S(f"bank_free{s}"), 1)
                    act.wait_ge(S(f"bank_free{s}"), i + (job_mg.base + 2))
                    act.dma_start(sg_dram[:, bass.ds(i * 2 + s, 1), :].rearrange("p a n -> p (a n)"), sgb[s]).then_inc(S(f"sg_stored{s}"), 16)

                for s in range(2):
                    act.sem_inc(S(f"sg_stored{s}"), 16)
                with act.Fori(0, NB) as b:
                    for s in range(2):
                        round_tile(act, job_mg, b * 2, s)
                    for n in range(8):
                        act.wait_ge(S("kt_full"), b * 8 + (n + 1))
                        nc.scalar.copy(KTs[:, :, n * 256:(n + 1) * 256].rearrange("p g (t k) -> p t g k", t=2),
                                       PS[6 + n % 2][:, :].rearrange("p (t g k) -> p t g k", t=2, g=2)).then_inc(S("kt_copied"), 1)
                        if n in (1, 4):
                            round_tile(act, job_mg, b * 2 + 1, n // 4)
                            gate(b, 0, n // 4)
                    act.wait_ge(S("pooled_ready"), b + 1)
                    nc.scalar.activation(plS, plS, ACT.Gelu_apprx_tanh).then_inc(S("sgelu_ready"), 1)
                    act.wait_ge(S("cv_full"), b + 1)
                    nc.scalar.copy(kcs[:, :, 0:NC_S], PS[6][:, 0:256].rearrange("p (g c) -> p g c", g=2)[:, :, 0:NC_S])
                    nc.scalar.copy(vcs[0:NC_S, :], PS[6][0:NC_S, 256:512]).then_inc(S("cv_copied"), 1)
                    act.wait_ge(S("cmax_ready"), b + 1)
                    nc.scalar.activation(Pcs, Pcs, ACT.Exp, bias=mx3[:, 0:1], accum_out=rs3[:, 0:1]).then_inc(S("cexp_ready"), 1)
                    act.wait_ge(S("pcT_full"), b + 1)
                    nc.scalar.copy(pcT[0:NC_S, :], PS[6][0:NC_S, 0:P]).then_inc(S("pcT_copied"), 1)
                    for n in range(2):
                        act.wait_ge(S("kw_full"), b * 2 + (n + 1))
                        nc.scalar.copy(KwT[:, :, n * 256:(n + 1) * 256].rearrange("p g (t k) -> p t g k", t=2),
                                       PS[6 + n][:, :].rearrange("p (t g k) -> p t g k", t=2, g=2)).then_inc(S("kw_copied"), 1)
                    gate(b, 1, 0)
                    act.wait_ge(S("smax_ready"), b * 2 + 1)
                    nc.scalar.activation(Ss, Ss, ACT.Exp, bias=mx3[:, 1:2], accum_out=rs3[:, 1:2]).then_inc(S("sp_ready"), 1)
                    act.wait_ge(S("smax_ready"), b * 2 + 2)
                    nc.scalar.activation(Sw, Sw, ACT.Exp, bias=mx3[:, 2:3], accum_out=rs3[:, 2:3]).then_inc(S("sp_ready"), 1)
                    gate(b, 1, 1)
                    for n in range(6):
                        act.wait_ge(S("spt_full"), b * 6 + (n + 1))
                        if n >= 2:
                            act.wait_ge(S("pv_used"), b * 5 + (n - 1))
                        if n < 5:
                            nc.scalar.copy(PT2[n % 2], PS[6 + n % 2][:, :]).then_inc(S("spt_copied"), 1)
                        else:
                            nc.scalar.copy(PT2[n % 2][0:NQ, 0:256], PS[6 + n % 2][0:NQ, 0:256]).then_inc(S("spt_copied"), 1)
                    act.wait_ge(S("odT_full"), b + 1)
                    for h in range(2):
                        ins = nc.scalar.copy(oT[h * 64:(h + 1) * 64, :, bass.ds(b * NQ + SEQ, NQ)],
                                             PS[6][h * 64:(h + 1) * 64, 0:P].rearrange("p (t h q) -> p t h q", h=2, q=NQ)[:, :, h, :])
                    ins.then_inc(S("so_done"), 1)
                for s in range(2):
                    act.wait_ge(S(f"sg_stored{s}"), 16 * (job_mg.n + 1))

            @block.vector
            def _(dve):
                V = nc.vector
                dve.wait_ge(S("kb_landed"), 16)
                NL = 15
                with dve.Fori(0, NB) as b:
                    order = [0]

                    def link(ins):
                        order[0] += 1
                        ins.then_inc(S("s_order"), 1)
                        dve.wait_ge(S("s_order"), b * NL + order[0])

                    for j in range(2):
                        for s in range(2):
                            rest_tile(dve, job_mg, b * 2 + j, s)
                    dve.wait_ge(S("page_used"), b * NPG + NPG + RP)
                    for v in range(2):
                        parts = PS[4 + v][:, :].rearrange("p (g m c) -> p g m c", g=2, m=2)
                        link(V.tensor_scalar(plS[:, 2 * v:2 * v + 2, :], parts[:, :, 0, 0:NC_S], pec[:, v:v + 1], None, ALU.add))
                        ins = V.tensor_tensor(plS[:, 2 * v:2 * v + 2, :], plS[:, 2 * v:2 * v + 2, :], parts[:, :, 1, 1:NC_S + 1], ALU.add)
                    ins.then_inc(S("pooled_ready"), 1)
                    dve.wait_ge(S("cs_full"), b + 1)
                    link(V.tensor_tensor(Pcs, PS[7][:, 0:NC_S], C("biascs"), ALU.add))
                    V.tensor_reduce(mx3[:, 0:1], Pcs, AX_X, ALU.max, negate=True).then_inc(S("cmax_ready"), 1)
                    for c in range(5):
                        w = 512 if c < 4 else NQ
                        dve.wait_ge(S("sel_full"), b * 5 + (c + 1))
                        V.tensor_tensor(Ss[:, c * 512:c * 512 + w], PS[4 + c % 2][:, 0:w], kb[:, c * 512:c * 512 + w], ALU.add).then_inc(S("sel_read"), 1)
                        if c == 0:
                            dve.wait_ge(S("cexp_ready"), b + 1)
                            link(V.reciprocal(rs3[:, 0:1], rs3[:, 0:1]))
                            V.tensor_scalar(Pcs, Pcs, rs3[:, 0:1], None, ALU.mult).then_inc(S("cp_ready"), 1)
                    dve.wait_ge(S("imp_full"), b + 1)
                    V.tensor_copy(imp0, PS[7][:, 0:NBLK]).then_inc(S("imp_copied"), 1)
                    dve.wait_ge(S("oc_full"), b + 1)
                    for g in range(4):
                        r = slice(g * 32, (g + 1) * 32)
                        ins = V.tensor_scalar(od[r, 0, :], PS[5][r, g * 64:(g + 1) * 64], gw[r, 0:1], None, ALU.mult)
                    ins.then_inc(S("oc_done"), 1)
                    dve.wait_ge(S("impsum_full"), b + 1)
                    V.tensor_copy(imp1, PS[7][:, 64:64 + NBLK]).then_inc(S("imp_read"), 1)
                    dve.wait_ge(S("imp_read"), b + 1)
                    V.memset(imp1[:, 0:1], FORCED)
                    link(V.memset(imp1[:, NBLK - 2:NBLK], FORCED))
                    V.memset(waits, 0.0)
                    link(V.max(top[:, 0:8], imp1))
                    V.memset(waits, 0.0)
                    link(V.match_replace(imp0, top[:, 0:8], imp1, -BIG))
                    V.memset(waits, 0.0)
                    link(V.max(top[:, 8:16], imp0))
                    V.memset(waits, 0.0)
                    link(V.match_replace(imp1, top[:, 8:16], imp0, -BIG))
                    link(V.tensor_scalar(msk, imp1, -1.0, -BIG, ALU.is_gt, ALU.mult))
                    blocks = Ss[:, 0:PAST].rearrange("p (s k) -> p s k", k=64)
                    link(V.tensor_tensor(blocks, blocks, msk[:, 0:32].unsqueeze(2).broadcast_to([P, 32, 64]), ALU.add))
                    V.tensor_reduce(mx3[:, 1:2], Ss, AX_X, ALU.max, negate=True).then_inc(S("smax_ready"), 1)
                    dve.wait_ge(S("w_full"), b + 1)
                    V.tensor_tensor(Sw[:, 0:WIN], PS[5][:, :], kb[:, PAST + NQ:PAST + NQ + WIN], ALU.add)
                    V.tensor_tensor(Sw[:, WIN:WIN + NQ], PS[4][:, 0:NQ], kb[:, PAST + NQ + WIN:], ALU.add).then_inc(S("w_read"), 1)
                    dve.wait_ge(S("w_read"), b + 1)
                    V.tensor_reduce(mx3[:, 2:3], Sw, AX_X, ALU.max, negate=True).then_inc(S("smax_ready"), 1)
                    dve.wait_ge(S("sp_ready"), b * 2 + 2)
                    link(V.reciprocal(rs3[:, 1:3], rs3[:, 1:3]))
                    link(V.tensor_tensor(rw3[:, 1:3], rs3[:, 1:3], gw[:, 1:3], ALU.mult))
                    dve.wait_ge(S("so_full"), b + 2)
                    for br in range(2):
                        for g in range(4):
                            r = slice(g * 32, (g + 1) * 32)
                            ins = V.scalar_tensor_tensor(out=od[r, 0, :], in0=PS[5 - br][r, g * 64:(g + 1) * 64], scalar=rw3[r, 1 + br:2 + br],
                                                         in1=od[r, 0, :], op0=ALU.mult, op1=ALU.add)
                        link(ins)
                    V.tensor_copy(od[:, 1, :], od[:, 0, :]).then_inc(S("od_ready"), 1)
                    assert order[0] == NL, order[0]

        take = scratch()
        yn = take(3 * SSMW).rearrange("p (t n) -> p t n", t=3)
        with program() as block:
            @block.sync
            def _(sp):
                for b in range(2):
                    sp.wait_ge(S(f"y_stored{b}"), 16 * (NPART // 2))
                for t in range(3):
                    sp.dma_start(yn[0:TOK[t], t, :], y_dram[t * P:t * P + TOK[t]]).then_inc(S("yn_landed"), 16)

            @block.tensor
            def _(pe):
                pe.wait_ge(S("yn_landed"), 48)
                for n in range(6):
                    t, c = n // 2, n % 2
                    if n >= 4:
                        pe.wait_ge(S("ys_ready"), n - 3)
                    for j in range(4):
                        tr = nc.tensor.transpose(PS[4 + n % 4][:, j * P:j * P + TOK[t]],
                                                 yn[0:TOK[t], t, (4 * c + j) * P:(4 * c + j + 1) * P], ident[0:TOK[t], 0:TOK[t]])
                    tr.then_inc(S("ys_full"), 1)

            @block.scalar
            def _(act):
                for n in range(6):
                    t, c = n // 2, n % 2
                    act.wait_ge(S("ys_full"), n + 1)
                    nc.scalar.activation(ysT[:, 4 * c:4 * c + 4, t * P:t * P + TOK[t]],
                                         PS[4 + n % 4][:, :].rearrange("p (j n) -> p j n", j=4)[:, :, 0:TOK[t]],
                                         ACT.Gelu_apprx_tanh).then_inc(S("ys_ready"), 1)

        take = scratch()
        sgm = take(32 * NT).rearrange("p (t n) -> p t n", t=32)
        mT = take(KT * NT).rearrange("p (t n) -> p t n", t=KT)
        sB = [take(NT) for _ in range(2)]
        tmp = take(NT)
        hi, lo = actr[:, 0], actr[:, 1]

        def tile_of(buf, t):
            return buf[:, bass.ds(t, 1), :].rearrange("p a n -> p (a n)")

        def add_to_x(dve, job):
            def read(i, s):
                full(dve, job, i, s)
                nc.vector.tensor_tensor(tile_of(xT, i * 2 + s), tile_of(xT, i * 2 + s), PS[s][:, 0:NT], ALU.add).then_inc(S(f"bank_free{s}"), 1)
            return read

        splits = [(oT[:, 0:4, :], 0), (oT[:, 4:8, :], 4), (ysT[:, 0:4, :], 8), (ysT[:, 4:8, :], 12)]
        m_splits = [(mT[:, t:t + 4, :], t) for t in range(0, KT, 4)]
        with program() as block:
            @block.sync
            def _(sp):
                for job in (job_ao, job_glu, job_out):
                    stream(sp, job)

            @block.gpsimd
            def _(pool):
                pool.wait_ge(S("m_ready"), 9)
                pool.dma_start(xT[:, :, :], x_dram).then_inc(S("x_back"), 16)

            @block.tensor
            def _(pe):
                pe.wait_ge(S("oy_split"), 4)
                products(pe, job_ao, hi, lo)
                products(pe, job_glu, hi, lo, 8)
                pe.wait_ge(S("m_split"), 4)
                products(pe, job_out, hi, lo)

            @block.scalar
            def _(act):
                def glu_gate(i, s):
                    full(act, job_glu, i, s)
                    nc.scalar.activation(sB[s], PS[2 + s][:, 0:NT], ACT.Sigmoid).then_inc(S("sigmoid_ready"), 1)

                def round_all(pieces, done):
                    for src, t in pieces:
                        nc.scalar.copy(actr[:, 0, t:t + 4, :], src).then_inc(S(done), 1)

                for n in range(2):
                    act.dma_start(sgm[:, 8 * n:8 * n + 8, :], sg_dram[:, 8 * n:8 * n + 8, :]).then_inc(S("sg_back0"), 16)
                round_all(splits, "oy_rounded")
                act.wait_ge(S("sg_back0"), 32)
                act.dma_start(sgm[:, 16:32, :], sg_dram[:, 16:32, :]).then_inc(S("sg_back1"), 16)
                follow(act, [job_ao, job_glu], round_tile, [None, glu_gate])
                act.wait_ge(S("m_ready"), 17)
                round_all(m_splits, "m_rounded")
                follow(act, [job_out], round_tile, [None])

            @block.vector
            def _(dve):
                V = nc.vector

                def rest_all(pieces, rounded, done):
                    for n, (src, t) in enumerate(pieces):
                        dve.wait_ge(S(rounded), n + 1)
                        V.tensor_tensor(actr[:, 1, t:t + 4, :], src, actr[:, 0, t:t + 4, :].bitcast(F32), ALU.subtract).then_inc(S(done), 1)

                def branch_a(i, s):
                    full(dve, job_ao, i, s)
                    dve.wait_ge(S("sg_back0"), 32)
                    for side in range(2):
                        t = i * 4 + (2 * s + side)
                        ins = V.tensor_tensor(tile_of(mT, t), PS[s + 2 * side][:, 0:NT], tile_of(sgm, t), ALU.mult)
                    ins.then_inc(S(f"bank_free{s}"), 1)

                def branch_b(i, s):
                    full(dve, job_glu, i, s)
                    dve.wait_ge(S("sg_back1"), 16)
                    dve.wait_ge(S("m_ready"), i * 2 + (s + 1))
                    V.tensor_tensor(tmp, PS[s][:, 0:NT], tile_of(sgm, i * 2 + (16 + s)), ALU.mult).then_inc(S("glu_read"), 1)
                    dve.wait_ge(S("glu_read"), i * 2 + (s + 1))
                    dve.wait_ge(S("sigmoid_ready"), i * 2 + (s + 1))
                    V.tensor_tensor(tmp, tmp, sB[s], ALU.mult).then_inc(S(f"bank_free{s}"), 1)
                    dve.wait_ge(S(f"bank_free{s}"), i + (job_glu.base + 2))
                    V.tensor_tensor(tile_of(mT, i * 2 + s), tile_of(mT, i * 2 + s), tmp, ALU.add).then_inc(S("m_ready"), 1)

                rest_all(splits, "oy_rounded", "oy_split")
                dve.sem_inc(S("m_ready"), 1)
                follow(dve, [job_ao, job_glu], rest_tile, [branch_a, branch_b])
                rest_all(m_splits, "m_rounded", "m_split")
                dve.wait_ge(S("x_back"), 16)
                follow(dve, [job_out], rest_tile, [add_to_x(dve, job_out)])

        last.close()
        hid = phase.enter_context(nc.sbuf_tensor("hid", [P, 2, FK, NT], F32R))
        open_arena(phase, "arena4")
        take = scratch()
        yT = take(KT * NT).rearrange("p (t n) -> p t n", t=KT)
        sB = take(NT)
        tmp = take(NT)
        yrow = [take(1024) for _ in range(2)]
        outputs = [(y_prompt[0, 0:P], P), (y_prompt[0, P:SEQ], P), (y_sample.rearrange("b t d -> (b t) d"), TOK[2])]
        with program() as block:
            @block.sync
            def _(sp):
                for c in range(FC):
                    stream(sp, job_ffn[c])
                    stream(sp, job_down[c])
                for t, (dst, rows) in enumerate(outputs):
                    for c in range(2):
                        sp.wait_ge(S("y_copied_out"), 4 * t + 2 * c + 2)
                        sp.dma_start(dst[:, c * 1024:(c + 1) * 1024], yrow[c][0:rows, :]).then_inc(S(f"yrow_stored{c}"), 16)
                for c in range(2):
                    sp.wait_ge(S(f"yrow_stored{c}"), 48)

            @block.gpsimd
            def _(pool):
                norm_split_rest(pool)

            @block.tensor
            def _(pe):
                norm_sum(pe, norm2)
                pe.wait_ge(S("h_ready"), KT)
                for c in range(FC):
                    products(pe, job_ffn[c], hi, lo)
                    pe.wait_ge(S("hid_ready"), FK * (c + 1) + 1)
                    products(pe, job_down[c], hid[:, 0], hid[:, 1])
                pe.wait_ge(S("x3_ready"), 1)
                norm_sum(pe, norm3)
                pe.wait_ge(S("y_ready"), KT)
                for n in range(12):
                    t, c = n // 4, n % 4
                    if n >= 2:
                        pe.wait_ge(S("y_copied_out"), n - 1)
                    for j in range(4):
                        tr = nc.tensor.transpose(PS[4 + n % 2][0:TOK[t], j * P:(j + 1) * P], yT[:, 4 * c + j, t * P:t * P + TOK[t]], ident)
                    tr.then_inc(S("y_turned"), 1)

            @block.scalar
            def _(act):
                norm_squares(act, norm2, xT)
                norm_root(act, norm2)
                norm_split_round(act)

                def silu(c):
                    def read(i, s):
                        if s == 0:
                            full(act, job_ffn[c], i, 0)
                            act.wait_ge(S("silu_used"), i + (FK * c + 1))
                            nc.scalar.activation(sB, PS[0][:, 0:NT], ACT.Silu).then_inc(S("bank_free0"), 1)
                    return read

                jobs, reads = [], []
                for c in range(FC):
                    jobs += [job_ffn[c], job_down[c]]
                    reads += [silu(c), None]
                follow(act, jobs, round_tile, reads)
                act.wait_ge(S("x3_ready"), 1)
                norm_squares(act, norm3, xT)
                norm_root(act, norm3)

            @block.vector
            def _(dve):
                V = nc.vector
                norm_rstd(dve, norm2)
                norm_split_scale(dve, xT, 1)
                dve.sem_inc(S("silu_used"), 1)
                dve.sem_inc(S("hid_ready"), 1)

                def gated(c):
                    def read(i, s):
                        if s:
                            n = FK * c
                            full(dve, job_ffn[c], i, 1)
                            dve.wait_ge(S("bank_free0"), i + (job_ffn[c].base + 2))
                            dve.wait_ge(S("hid_ready"), i + (n + 1))
                            V.tensor_tensor(tmp, PS[1][:, 0:NT], sB, ALU.mult).then_inc(S("silu_used"), 1)
                            dve.wait_ge(S("silu_used"), i + (n + 2))
                            V.tensor_copy(hid[:, 0, bass.ds(i, 1), :].rearrange("p a n -> p (a n)"), tmp).then_inc(S("bank_free1"), 1)
                            dve.wait_ge(S("bank_free1"), i + (job_ffn[c].base + 2))
                            V.tensor_tensor(hid[:, 1, bass.ds(i, 1), :].rearrange("p a n -> p (a n)"), tmp,
                                            hid[:, 0, bass.ds(i, 1), :].rearrange("p a n -> p (a n)").bitcast(F32), ALU.subtract).then_inc(S("hid_ready"), 1)
                    return read

                jobs, reads = [], []
                for c in range(FC):
                    jobs += [job_ffn[c], job_down[c]]
                    reads += [gated(c), add_to_x(dve, job_down[c])]
                follow(dve, jobs, rest_tile, reads)
                for s in range(2):
                    dve.wait_ge(S(f"bank_free{s}"), steps_before[0] + 1)
                dve.sem_inc(S("x3_ready"), 1)
                norm_rstd(dve, norm3)
                for k in range(KT):
                    norm_scale(dve, xT, yT[:, k, :], 2, k, "y_ready")
                for n in range(12):
                    t, c = n // 4, n % 4
                    dve.wait_ge(S("y_turned"), n + 1)
                    if t:
                        dve.wait_ge(S(f"yrow_stored{c // 2}"), 16 * t)
                    V.tensor_copy(yrow[c // 2][0:TOK[t], (c % 2) * 512:(c % 2 + 1) * 512], PS[4 + n % 2][0:TOK[t], :]).then_inc(S("y_copied_out"), 1)
        phase.close()


_INS = ["x_prompt", "x_sample", "cache_kv", "state_win", "state_ssm_re", "state_ssm_im", "page_table", "g_mix", "w_in",
        "w_cmp_pe", "w_cmp_pool", "w_cmp_phi", "w_attn_out", "ssm_lam_re", "ssm_lam_im", "ssm_log_dt", "ssm_b_re",
        "ssm_b_im", "ssm_c_re", "ssm_c_im", "ssm_d", "w_glu", "w_out", "g_ffn", "w_gate", "w_up", "w_down", "g_final"]
_MATRICES = {"w_in", "w_attn_out", "w_glu", "w_out", "w_gate", "w_up", "w_down"}
_OUTS = [(1, SEQ, DM), (NB, NQ, DM), (1, 1, SEQ, 4, NKV, HD), (1, 1, SEQ, 2, NKV, HD), (1, 1, NG, NS), (1, 1, NG, NS),
         (1, NB, NQ, 4, NKV, HD), (1, NB, WIN, 2, NKV, HD), (1, NB, NG, NS), (1, NB, NG, NS)]


def kernel(**inputs):
    import concourse.bacc as _bacc
    from concourse.bass_utils import run_bass_kernel_spmd as _run

    nc = _bacc.Bacc("TRN2", target_bir_lowering=False, num_devices=1)
    arrays, ins, outs = {}, [], []
    given = {name: np.ascontiguousarray(inputs[name]) for name in _INS}
    given["small_constants"] = small_constants()[0]
    given["key_biases"] = key_biases()
    for name, a in given.items():
        arrays[f"in_{name}_dram"] = a
        ap = nc.dram_tensor(f"in_{name}_dram", a.shape, mybir.dt.from_np(a.dtype), kind="ExternalInput").ap()
        ins.append(ap[0] if name in _MATRICES else ap)
    for i, shape in enumerate(_OUTS):
        outs.append(nc.dram_tensor(f"out_{i}_dram", shape, F32, kind="ExternalOutput").ap())
    build(nc, ins, outs)
    r = _run(nc, [arrays], core_ids=[0])
    return tuple(r.results[0][f"out_{i}_dram"] for i in range(len(_OUTS)))
```
